# Optimizing a Trainium2 kernel written in Bass

```python
import jax, jax.numpy as jnp
from jax import lax
import numpy as np

D_MODEL = 1024
BATCH = 1
SEQ = 256
DEPTH = 2

N_A_LAYERS = DEPTH // 2
N_B_LAYERS = DEPTH - N_A_LAYERS

EPS = 1e-6
PLE_DIM = 256
D_FF = ((8 * D_MODEL // 3 + 255) // 256) * 256

A_KEY_DIM = 128
A_HEADS = D_MODEL // A_KEY_DIM
A_VAL_DIM = D_MODEL // A_HEADS
A_WIDTH = A_HEADS * A_KEY_DIM
A_CHUNK = 64

B_HEADS = 16
B_NOPE = 128
B_ROPE = 64
B_VDIM = 128
B_Q_LORA = 512
B_KV_LORA = 256
Q_BLOCK = 128
ROPE_THETA = 10000.0


def _rmsnorm(x, g):
    x32 = x.astype(jnp.float32)
    y = x32 * lax.rsqrt(jnp.mean(x32 * x32, axis=-1, keepdims=True) + EPS)
    return (y * g.astype(jnp.float32)).astype(x.dtype)

def _swiglu(h, w_in, w_out):
    gate, up = jnp.split(h @ w_in, 2, axis=-1)
    return (jax.nn.silu(gate) * up) @ w_out

def _rope(x, positions):
    d = x.shape[-1]
    inv_freq = 1.0 / (ROPE_THETA ** (jnp.arange(0, d, 2, dtype=jnp.float32) / d))
    ang = positions.astype(jnp.float32)[..., None] * inv_freq
    ang = ang.reshape(ang.shape[:2] + (1,) * (x.ndim - 3) + (d // 2,))
    cos, sin = jnp.cos(ang), jnp.sin(ang)
    x32 = x.astype(jnp.float32)
    x1, x2 = x32[..., : d // 2], x32[..., d // 2:]
    return jnp.concatenate([x1 * cos - x2 * sin, x2 * cos + x1 * sin], axis=-1).astype(x.dtype)

def _hgrn2_chunk(state, inp):
    q, k, v, g = inp
    b = jnp.cumsum(g, axis=2)
    o_inter = jnp.einsum('bhtk,bhkv->bhtv', q * jnp.exp(b), state)
    causal = jnp.tril(jnp.ones((A_CHUNK, A_CHUNK), dtype=bool))[:, :, None]
    diff = b[:, :, :, None, :] - b[:, :, None, :, :]
    decay = jnp.where(causal, jnp.exp(jnp.where(causal, diff, 0.0)), 0.0)
    scores = jnp.einsum('bhtk,bhsk,bhtsk->bhts', q, k, decay)
    o_intra = jnp.einsum('bhts,bhsv->bhtv', scores, v)
    b_last = b[:, :, -1:, :]
    new_state = jnp.exp(b_last[:, :, 0, :])[..., None] * state + jnp.einsum(
        'bhsk,bhsv->bhkv', k * jnp.exp(b_last - b), v)
    return new_state, o_inter + o_intra

def _hgrn2_mixer(h, w_in, lb, out_gain, w_out):
    bsz, seq, _ = h.shape
    q, f_logit, i, g = jnp.split(h @ w_in, 4, axis=-1)
    f_logit = f_logit.astype(jnp.float32)
    lb = lb.astype(jnp.float32)
    log_f = jnp.log(lb + (1.0 - lb) * jax.nn.sigmoid(f_logit))
    k = (1.0 - lb) * jax.nn.sigmoid(-f_logit)
    n_chunks = seq // A_CHUNK

    def to_chunks(t, d):
        t = t.astype(jnp.float32).reshape(bsz, n_chunks, A_CHUNK, A_HEADS, d)
        return t.transpose(1, 0, 3, 2, 4)

    qc = to_chunks(q, A_KEY_DIM) * (A_KEY_DIM ** -0.5)
    kc = to_chunks(k, A_KEY_DIM)
    vc = to_chunks(i, A_VAL_DIM)
    gc = to_chunks(log_f, A_KEY_DIM)
    s0 = jnp.zeros((bsz, A_HEADS, A_KEY_DIM, A_VAL_DIM), jnp.float32)
    _, o = lax.scan(_hgrn2_chunk, s0, (qc, kc, vc, gc))
    o = o.transpose(1, 0, 3, 2, 4).reshape(bsz, seq, A_HEADS, A_VAL_DIM)
    o = _rmsnorm(o, out_gain).reshape(bsz, seq, A_HEADS * A_VAL_DIM)
    o = o * jax.nn.sigmoid(g.astype(jnp.float32))
    return o.astype(h.dtype) @ w_out

def _mla_shared_kv(x, positions, norm_in, w_down, latent_norm, w_up):
    bsz, seq, _ = x.shape
    h = _rmsnorm(x, norm_in)
    c_kv, k_r = jnp.split(h @ w_down, [B_KV_LORA], axis=-1)
    c_kv = _rmsnorm(c_kv, latent_norm)
    kv = (c_kv @ w_up).reshape(bsz, seq, B_HEADS, B_NOPE + B_VDIM)
    k_nope, v = jnp.split(kv, [B_NOPE], axis=-1)
    k_rope = _rope(k_r, positions)
    return k_nope, k_rope, v

def _mla_mixer(h, positions, k_nope, k_rope, v, w_dq, q_norm, w_uq, w_out):
    bsz, seq, _ = h.shape
    c_q = _rmsnorm(h @ w_dq, q_norm)
    q = (c_q @ w_uq).reshape(bsz, seq, B_HEADS, B_NOPE + B_ROPE)
    q_nope, q_rope = jnp.split(q, [B_NOPE], axis=-1)
    q_rope = _rope(q_rope, positions)
    n_blocks = seq // Q_BLOCK
    scale = (B_NOPE + B_ROPE) ** -0.5

    def blocks(t):
        return t.reshape((bsz, n_blocks, Q_BLOCK) + t.shape[2:]).swapaxes(0, 1)

    key_idx = jnp.arange(seq)

    def attend(args):
        qn, qr, blk = args
        s = (jnp.einsum('bqhd,bkhd->bhqk', qn, k_nope)
             + jnp.einsum('bqhd,bkd->bhqk', qr, k_rope)).astype(jnp.float32) * scale
        q_idx = blk * Q_BLOCK + jnp.arange(Q_BLOCK)
        mask = q_idx[:, None] >= key_idx[None, :]
        s = jnp.where(mask[None, None], s, -jnp.inf)
        pr = jax.nn.softmax(s, axis=-1).astype(v.dtype)
        return jnp.einsum('bhqk,bkhd->bqhd', pr, v)

    o = lax.map(attend, (blocks(q_nope), blocks(q_rope), jnp.arange(n_blocks, dtype=jnp.int32)))
    o = o.swapaxes(0, 1).reshape(bsz, seq, B_HEADS * B_VDIM)
    return o @ w_out

def first_inputs(seed: int = 0) -> dict:
    key = jax.random.key(seed)
    ks = jax.random.split(key, 24)
    f32 = jnp.float32

    def w(k, shape, fan_in):
        return jax.random.normal(k, shape, f32) * (fan_in ** -0.5)

    def gain(k, shape):
        return 1.0 + 0.02 * jax.random.normal(k, shape, f32)

    offset = jax.random.randint(ks[2], (BATCH, 1), 0, 1024, dtype=jnp.int32)
    positions = offset + jnp.arange(SEQ, dtype=jnp.int32)[None, :]
    return {
        'x': jax.random.normal(ks[0], (BATCH, SEQ, D_MODEL), f32),
        'p': jax.random.normal(ks[1], (DEPTH, BATCH, SEQ, PLE_DIM), f32),
        'positions': positions,
        'norm_gains': gain(ks[3], (DEPTH, 4, D_MODEL)),
        'ffn_w_in': w(ks[4], (DEPTH, 2, D_MODEL, 2 * D_FF), D_MODEL),
        'ffn_w_out': w(ks[5], (DEPTH, 2, D_FF, D_MODEL), D_FF),
        'ple_w_gate': w(ks[6], (DEPTH, D_MODEL, D_MODEL), D_MODEL),
        'ple_w_in': w(ks[7], (DEPTH, PLE_DIM, D_MODEL), PLE_DIM),
        'a_w_in': w(ks[8], (N_A_LAYERS, D_MODEL, 4 * A_WIDTH), D_MODEL),
        'a_lb_logits': 0.1 * jax.random.normal(ks[9], (N_A_LAYERS + 1, A_WIDTH), f32),
        'a_out_gain': gain(ks[10], (N_A_LAYERS, A_VAL_DIM)),
        'a_w_out': w(ks[11], (N_A_LAYERS, A_WIDTH, D_MODEL), A_WIDTH),
        'kv_norm_in': gain(ks[12], (D_MODEL,)),
        'kv_w_down': w(ks[13], (D_MODEL, B_KV_LORA + B_ROPE), D_MODEL),
        'kv_latent_norm': gain(ks[14], (B_KV_LORA,)),
        'kv_w_up': w(ks[15], (B_KV_LORA, B_HEADS * (B_NOPE + B_VDIM)), B_KV_LORA),
        'b_w_dq': w(ks[16], (N_B_LAYERS, D_MODEL, B_Q_LORA), D_MODEL),
        'b_q_norm': gain(ks[17], (N_B_LAYERS, B_Q_LORA)),
        'b_w_uq': w(ks[18], (N_B_LAYERS, B_Q_LORA, B_HEADS * (B_NOPE + B_ROPE)), B_Q_LORA),
        'b_w_out': w(ks[19], (N_B_LAYERS, B_HEADS * B_VDIM, D_MODEL), B_HEADS * B_VDIM),
        'final_norm': gain(ks[20], (D_MODEL,)),
    }

def first_block(x, p, positions, norm_gains, ffn_w_in, ffn_w_out, ple_w_gate, ple_w_in,
              a_w_in, a_lb_logits, a_out_gain, a_w_out,
              kv_norm_in, kv_w_down, kv_latent_norm, kv_w_up,
              b_w_dq, b_q_norm, b_w_uq, b_w_out, final_norm):
    lower_bounds = jnp.cumsum(jax.nn.softmax(a_lb_logits.astype(jnp.float32), axis=0), axis=0)
    shared = None
    if N_A_LAYERS == 0:
        shared = _mla_shared_kv(x, positions, kv_norm_in, kv_w_down, kv_latent_norm, kv_w_up)
    for li in range(DEPTH):
        g = norm_gains[li]
        x = x + 0.5 * _swiglu(_rmsnorm(x, g[0]), ffn_w_in[li, 0], ffn_w_out[li, 0])
        h = _rmsnorm(x, g[1])
        if li < N_A_LAYERS:
            x = x + _hgrn2_mixer(h, a_w_in[li], lower_bounds[li], a_out_gain[li], a_w_out[li])
        else:
            bi = li - N_A_LAYERS
            k_nope, k_rope, v = shared
            x = x + _mla_mixer(h, positions, k_nope, k_rope, v,
                               b_w_dq[bi], b_q_norm[bi], b_w_uq[bi], b_w_out[bi])
        x = x + 0.5 * _swiglu(_rmsnorm(x, g[2]), ffn_w_in[li, 1], ffn_w_out[li, 1])
        gate = jax.nn.sigmoid((_rmsnorm(x, g[3]) @ ple_w_gate[li]).astype(jnp.float32))
        x = x + (gate * (p[li] @ ple_w_in[li]).astype(jnp.float32)).astype(x.dtype)
        if li == N_A_LAYERS - 1:
            shared = _mla_shared_kv(x, positions, kv_norm_in, kv_w_down, kv_latent_norm, kv_w_up)
    return _rmsnorm(x, final_norm)


HEAD_DIM = 64
MOBA_HEADS = D_MODEL // (2 * HEAD_DIM)
NSA_HEADS = D_MODEL // (2 * HEAD_DIM)
NSA_KV_GROUPS = 2
NSA_HPG = NSA_HEADS // NSA_KV_GROUPS
MOBA_BLOCK = 256
MOBA_TOPK = 3
CMP_LEN = 32
CMP_STRIDE = 16
SLC_BLOCK = 64
SLC_TOPN = 16
WINDOW = 512
Q_CHUNK = 128
RMS_EPS = 1e-6
NEG = -1e9
FORCE_BONUS = 1e4

MOBA_W = MOBA_HEADS * HEAD_DIM
NSA_W = NSA_HEADS * HEAD_DIM
KV_W = NSA_KV_GROUPS * HEAD_DIM
SPLITS = [MOBA_W] * 4 + [NSA_W] + [KV_W] * 6 + [3 * NSA_HEADS] + [NSA_W]
D_IN = sum(SPLITS)


def rmsnorm(x, g):
    xf = x.astype(jnp.float32)
    y = xf * lax.rsqrt(jnp.mean(xf * xf, axis=-1, keepdims=True) + RMS_EPS)
    return (y * g.astype(jnp.float32)).astype(x.dtype)

def alibi_slopes(n):
    return jnp.asarray(2.0 ** (-8.0 * np.arange(1, n + 1) / n), dtype=jnp.float32)

def cmp_to_slc_matrix(n_cmp, n_slc):
    i = np.arange(n_cmp)[:, None]
    j = np.arange(n_slc)[None, :]
    start = i * CMP_STRIDE
    end = start + CMP_LEN
    ov = (start < (j + 1) * SLC_BLOCK) & (end > j * SLC_BLOCK)
    return jnp.asarray(ov.astype(np.float32))

def compress_blocks(k, pe, w1, w2):
    B, S, G, dh = k.shape
    T = (S - CMP_LEN) // CMP_STRIDE + 1
    idx = np.arange(T)[:, None] * CMP_STRIDE + np.arange(CMP_LEN)[None, :]
    win = k[:, idx] + pe[:, None, :]
    win = win.transpose(0, 3, 1, 2, 4).reshape(B, G, T, CMP_LEN * dh)
    return jax.nn.gelu(win @ w1) @ w2

def hybrid_mixer(h, w_in, w_out, pe_k, pe_v, w_ck1, w_ck2, w_cv1, w_cv2):
    B, S, _ = h.shape
    dh = HEAD_DIM
    NC = S // Q_CHUNK
    NB = -(-S // MOBA_BLOCK)
    KM = min(MOBA_TOPK, NB)
    NBS = S // SLC_BLOCK
    NS = min(SLC_TOPN, NBS)
    T = (S - CMP_LEN) // CMP_STRIDE + 1
    scale = dh ** -0.5

    u = h @ w_in
    offs = np.cumsum(SPLITS)[:-1].tolist()
    (qm, km, vm, zm, qn, kc, vc, ks, vs, kw, vw, gl, zn) = jnp.split(u, offs, axis=-1)

    def heads(a, n):
        return a.reshape(B, S, n, dh).transpose(0, 2, 1, 3)

    pad = NB * MOBA_BLOCK - S
    qm = heads(qm, MOBA_HEADS) * scale
    km = jnp.pad(heads(km, MOBA_HEADS), ((0, 0), (0, 0), (0, pad), (0, 0))).reshape(B, MOBA_HEADS, NB, MOBA_BLOCK, dh)
    vm = jnp.pad(heads(vm, MOBA_HEADS), ((0, 0), (0, 0), (0, pad), (0, 0))).reshape(B, MOBA_HEADS, NB, MOBA_BLOCK, dh)
    kmean = jnp.mean(km, axis=3)

    G = NSA_KV_GROUPS
    qn = qn.reshape(B, S, G, NSA_HPG, dh).transpose(0, 2, 3, 1, 4) * scale
    kc = compress_blocks(kc.reshape(B, S, G, dh), pe_k, w_ck1, w_ck2)
    vc = compress_blocks(vc.reshape(B, S, G, dh), pe_v, w_cv1, w_cv2)
    ks = heads(ks, G).reshape(B, G, NBS, SLC_BLOCK, dh)
    vs = heads(vs, G).reshape(B, G, NBS, SLC_BLOCK, dh)
    kw = jnp.pad(heads(kw, G), ((0, 0), (0, 0), (WINDOW, 0), (0, 0)))
    vw = jnp.pad(heads(vw, G), ((0, 0), (0, 0), (WINDOW, 0), (0, 0)))
    gates = jax.nn.sigmoid(gl.astype(jnp.float32)).reshape(B, S, G, NSA_HPG, 3)

    slope_m = alibi_slopes(MOBA_HEADS)
    slope_n = alibi_slopes(NSA_HEADS).reshape(G, NSA_HPG)
    M = cmp_to_slc_matrix(T, NBS)
    hidx = jnp.arange(MOBA_HEADS)[:, None, None]
    gidx = jnp.arange(G)[:, None, None]

    def chunk(i):
        b = i // NC
        s0 = (i % NC) * Q_CHUNK
        t = s0 + jnp.arange(Q_CHUNK)
        take = lambda a: lax.dynamic_index_in_dim(a, b, 0, keepdims=False)

        q = lax.dynamic_slice_in_dim(take(qm), s0, Q_CHUNK, axis=1)
        Kb, Vb, Kmean = take(km), take(vm), take(kmean)
        cur = s0 // MOBA_BLOCK
        gsc = jnp.einsum('hqd,hnd->hqn', q, Kmean).astype(jnp.float32)
        gsc = jnp.where(jnp.arange(NB) < cur, gsc, NEG)
        _, sel = lax.top_k(gsc, KM)
        sel_ok = jnp.arange(KM) < cur
        k_sel = Kb[hidx, sel]
        v_sel = Vb[hidx, sel]
        s_sel = jnp.einsum('hqd,hqkbd->hqkb', q, k_sel).astype(jnp.float32)
        pos_sel = sel[..., None] * MOBA_BLOCK + jnp.arange(MOBA_BLOCK)
        d_sel = (t[None, :, None, None] - pos_sel).astype(jnp.float32)
        s_sel = jnp.where(sel_ok[None, None, :, None], s_sel - slope_m[:, None, None, None] * d_sel, NEG)
        k_own = lax.dynamic_index_in_dim(Kb, cur, 1, keepdims=False)
        v_own = lax.dynamic_index_in_dim(Vb, cur, 1, keepdims=False)
        s_own = jnp.einsum('hqd,hkd->hqk', q, k_own).astype(jnp.float32)
        d_own = t[:, None] - (cur * MOBA_BLOCK + jnp.arange(MOBA_BLOCK))[None, :]
        s_own = jnp.where(d_own >= 0, s_own - slope_m[:, None, None] * d_own.astype(jnp.float32), NEG)
        logits = jnp.concatenate([s_sel.reshape(MOBA_HEADS, Q_CHUNK, KM * MOBA_BLOCK), s_own], axis=-1)
        p = jax.nn.softmax(logits, axis=-1).astype(v_own.dtype)
        p_sel = p[..., :KM * MOBA_BLOCK].reshape(MOBA_HEADS, Q_CHUNK, KM, MOBA_BLOCK)
        o_m = (jnp.einsum('hqkb,hqkbd->hqd', p_sel, v_sel)
               + jnp.einsum('hqb,hbd->hqd', p[..., KM * MOBA_BLOCK:], v_own))
        o_m = o_m.transpose(1, 0, 2).reshape(Q_CHUNK, MOBA_W)

        qg = lax.dynamic_slice_in_dim(take(qn), s0, Q_CHUNK, axis=2)
        kcb, vcb = take(kc), take(vc)
        s_c = jnp.einsum('gjqd,gtd->gjqt', qg, kcb).astype(jnp.float32)
        d_c = t[:, None] - (jnp.arange(T) * CMP_STRIDE + CMP_LEN - 1)[None, :]
        ok_c = d_c >= 0
        s_c = jnp.where(ok_c, s_c - slope_n[:, :, None, None] * d_c.astype(jnp.float32), NEG)
        p_c = jax.nn.softmax(s_c, axis=-1) * ok_c
        o_c = jnp.einsum('gjqt,gtd->gjqd', p_c.astype(vcb.dtype), vcb)
        imp = jnp.einsum('gjqt,tn->gqn', p_c, M)
        blk = t // SLC_BLOCK
        jn = jnp.arange(NBS)[None, :]
        forced = (jn == 0) | (jn == blk[:, None]) | (jn == blk[:, None] - 1)
        imp = jnp.where(forced, FORCE_BONUS, imp)
        imp = jnp.where(jn <= blk[:, None], imp, NEG)
        _, sidx = lax.top_k(imp, NS)
        s_valid = sidx <= blk[None, :, None]
        ksb = take(ks)[gidx, sidx]
        vsb = take(vs)[gidx, sidx]
        s_s = jnp.einsum('gjqd,gqnbd->gjqnb', qg, ksb).astype(jnp.float32)
        d_s = t[None, :, None, None] - (sidx[..., None] * SLC_BLOCK + jnp.arange(SLC_BLOCK))
        ok_s = (d_s >= 0) & s_valid[..., None]
        s_s = jnp.where(ok_s[:, None], s_s - slope_n[:, :, None, None, None] * d_s[:, None].astype(jnp.float32), NEG)
        p_s = jax.nn.softmax(s_s.reshape(G, NSA_HPG, Q_CHUNK, NS * SLC_BLOCK), axis=-1)
        p_s = p_s.reshape(G, NSA_HPG, Q_CHUNK, NS, SLC_BLOCK).astype(vsb.dtype)
        o_s = jnp.einsum('gjqnb,gqnbd->gjqd', p_s, vsb)
        kwb = lax.dynamic_slice_in_dim(take(kw), s0, WINDOW + Q_CHUNK, axis=1)
        vwb = lax.dynamic_slice_in_dim(take(vw), s0, WINDOW + Q_CHUNK, axis=1)
        s_w = jnp.einsum('gjqd,gkd->gjqk', qg, kwb).astype(jnp.float32)
        pos_w = s0 - WINDOW + jnp.arange(WINDOW + Q_CHUNK)
        d_w = t[:, None] - pos_w[None, :]
        ok_w = (d_w >= 0) & (d_w < WINDOW) & (pos_w >= 0)[None, :]
        s_w = jnp.where(ok_w, s_w - slope_n[:, :, None, None] * d_w.astype(jnp.float32), NEG)
        p_w = jax.nn.softmax(s_w, axis=-1).astype(vwb.dtype)
        o_w = jnp.einsum('gjqk,gkd->gjqd', p_w, vwb)
        g = lax.dynamic_slice_in_dim(take(gates), s0, Q_CHUNK, axis=0).transpose(1, 2, 0, 3)
        g = g.astype(o_c.dtype)
        o_n = g[..., 0:1] * o_c + g[..., 1:2] * o_s + g[..., 2:3] * o_w
        o_n = o_n.transpose(2, 0, 1, 3).reshape(Q_CHUNK, NSA_W)
        return o_m, o_n

    o_m, o_n = lax.map(chunk, jnp.arange(B * NC))
    o_m = o_m.reshape(B, S, MOBA_W)
    o_n = o_n.reshape(B, S, NSA_W)
    y = jnp.concatenate([o_m * jax.nn.silu(zm), o_n * jax.nn.silu(zn)], axis=-1)
    return y @ w_out

def second_inputs(seed: int = 0) -> dict:
    key = jax.random.key(seed)
    ks = jax.random.split(key, 16)
    L, D, dh = DEPTH, D_MODEL, HEAD_DIM
    nrm = lambda k, shape, s: jax.random.normal(k, shape, jnp.float32) * s
    return {
        "x": nrm(ks[0], (BATCH, SEQ, D), 1.0),
        "c": nrm(ks[1], (BATCH, D), 1.0),
        "w_ada": nrm(ks[2], (L, D, 3 * D), D ** -0.5),
        "b_ada": nrm(ks[3], (L, 3 * D), 0.01),
        "g_pre": 1.0 + nrm(ks[4], (L, D), 0.1),
        "g_post": 1.0 + nrm(ks[5], (L, D), 0.1),
        "w_in": nrm(ks[6], (L, D, D_IN), D ** -0.5),
        "w_out": nrm(ks[7], (L, D, D), D ** -0.5),
        "pe_k": nrm(ks[8], (L, CMP_LEN, dh), 0.1),
        "pe_v": nrm(ks[9], (L, CMP_LEN, dh), 0.1),
        "w_ck1": nrm(ks[10], (L, CMP_LEN * dh, dh), (CMP_LEN * dh) ** -0.5),
        "w_ck2": nrm(ks[11], (L, dh, dh), dh ** -0.5),
        "w_cv1": nrm(ks[12], (L, CMP_LEN * dh, dh), (CMP_LEN * dh) ** -0.5),
        "w_cv2": nrm(ks[13], (L, dh, dh), dh ** -0.5),
    }

def second_block(x, c, w_ada, b_ada, g_pre, g_post, w_in, w_out, pe_k, pe_v, w_ck1, w_ck2, w_cv1, w_cv2):
    D = x.shape[-1]
    cs = jax.nn.silu(c)
    for l in range(DEPTH):
        mod = cs @ w_ada[l] + b_ada[l]
        shift, scale, gate = mod[:, None, :D], mod[:, None, D:2 * D], mod[:, None, 2 * D:]
        h = rmsnorm(x, g_pre[l]) * (1.0 + scale) + shift
        y = hybrid_mixer(h, w_in[l], w_out[l], pe_k[l], pe_v[l], w_ck1[l], w_ck2[l], w_cv1[l], w_cv2[l])
        x = x + gate * rmsnorm(y, g_post[l])
    return x


def setup_inputs(seed=0):
    out = dict(first_inputs(seed))
    for name, value in second_inputs(seed + 1).items():
        if name != "x":
            out[name + "_2"] = value
    return out


def reference(
    x, p, positions, norm_gains, ffn_w_in, ffn_w_out, ple_w_gate, ple_w_in, a_w_in, a_lb_logits,
    a_out_gain, a_w_out, kv_norm_in, kv_w_down, kv_latent_norm, kv_w_up, b_w_dq, b_q_norm,
    b_w_uq, b_w_out, final_norm, c_2, w_ada_2, b_ada_2, g_pre_2, g_post_2, w_in_2, w_out_2,
    pe_k_2, pe_v_2, w_ck1_2, w_ck2_2, w_cv1_2, w_cv2_2,
):
    x = first_block(
        x, p, positions, norm_gains, ffn_w_in, ffn_w_out, ple_w_gate, ple_w_in, a_w_in,
        a_lb_logits, a_out_gain, a_w_out, kv_norm_in, kv_w_down, kv_latent_norm, kv_w_up,
        b_w_dq, b_q_norm, b_w_uq, b_w_out, final_norm,
    )
    return second_block(
        x, c_2, w_ada_2, b_ada_2, g_pre_2, g_post_2, w_in_2, w_out_2, pe_k_2, pe_v_2, w_ck1_2,
        w_ck2_2, w_cv1_2, w_cv2_2,
    )


_drawn_inputs = setup_inputs


def setup_inputs(seed=0):
    import zlib

    import numpy as np

    out = dict(_drawn_inputs(seed))
    spreads = {}
    factors = {'a_out_gain': 4.461,
     'kv_norm_in': 8.0,
     'kv_latent_norm': 8.0,
     'b_q_norm': 8.0,
     'b_ada_2': 2.849,
     'pe_k_2': 8.0}
    for name, (base, spread) in spreads.items():
        noise = np.random.default_rng([zlib.crc32(name.encode()), seed]).standard_normal(out[name].shape)
        drawn = base * np.exp(spread * noise) if base else spread * noise
        out[name] = __import__('jax').numpy.asarray(drawn.astype(out[name].dtype))
    for name, factor in factors.items():
        out[name] = (out[name] * factor).astype(out[name].dtype)
    return out
```

```python
import numpy as np

import concourse.bass as bass
from concourse import mybir

F32 = mybir.dt.float32
F32R = mybir.dt.float32r
I32 = mybir.dt.int32
U32 = mybir.dt.uint32
ACT = mybir.ActivationFunctionType
ALU = mybir.AluOpType
AX = mybir.AxisListType

P = 128
T = 256
TB = T // P
D = 1024
KD = D // P
FF = 2816
KF = FF // P
PAIRS = KF // 2
EPS = 1e-6
NEG = -1e30

CH = 2048
NRAW = 2
NSLOT = 4
AHEAD = NSLOT - 1
MOD_STEPS = 7
MOD = 2 * 3 * D // 4 // 256

HEADS_A = 8
CHUNK_A = 64
HEADS_B = 16
NOPE, ROPE, VDIM = 128, 64, 128
SCALE_B = float((NOPE + ROPE) ** -0.5)
HEADS_C = 8
DH = 64
GROUPS = 2
CMP_T = 15
OFF = dict(qm=0, km=512, vm=1024, zm=1536, qn=2048, kcvc=2560, ksvs=2816, kwvw=3072, gl=3328, zn=3352)
LEVELS = [64, 32, 16, 8, 4, 2, 1]

C_IDENT, C_PERM, C_CAUS, C_DIST, C_DMASK, C_RESET = 0, 128, 256, 384, 640, 896
C_CMPD, C_CMPM, C_ROWV, C_FREQ, C_SIGN, C_SWAP, C_LVL = 1152, 1182, 1212, 1214, 1215, 1216, 1344
C_N = C_LVL + 128 * len(LEVELS)


def shape_constants():
    c = np.zeros((P, C_N), np.float32)
    p = np.arange(P)
    c[:, C_IDENT:C_IDENT + P] = np.eye(P)
    swap = (p // 64) * 64 + (p % 64 + 32) % 64
    c[swap, C_PERM + p] = 1.0
    c[(p + 64) % P, C_SWAP + p] = 1.0
    c[:, C_CAUS:C_CAUS + P] = np.where(p[:, None] >= p[None, :], 0.0, NEG)
    dist = p[:, None] + P - np.arange(T)[None, :]
    c[:, C_DIST:C_DIST + T] = np.maximum(dist, 0)
    c[:, C_DMASK:C_DMASK + T] = np.where(dist >= 0, 0.0, NEG)
    c[:, C_RESET:C_RESET + T] = (np.arange(T) % CHUNK_A != 0)[None, :]
    for b in range(TB):
        d = (b * P + p)[:, None] - (np.arange(CMP_T) * 16 + 31)[None, :]
        c[:, C_CMPD + b * CMP_T:C_CMPD + (b + 1) * CMP_T] = np.maximum(d, 0)
        c[:, C_CMPM + b * CMP_T:C_CMPM + (b + 1) * CMP_T] = np.where(d >= 0, 0.0, NEG)
        c[:, C_ROWV + b] = (b * P + p) >= 31
    half = ROPE // 2
    freq = np.float32(1.0) / (np.float32(10000.0) ** (np.arange(0, ROPE, 2, dtype=np.float32) / np.float32(ROPE)))
    c[:, C_FREQ] = freq[p % half]
    c[:, C_SIGN] = np.where(p % ROPE < half, -1.0, 1.0)
    for n, L in enumerate(LEVELS):
        s, t = p[:, None], p[None, :]
        c[:, C_LVL + n * P:C_LVL + (n + 1) * P] = (s // (2 * L) == t // (2 * L)) & (s % (2 * L) < L) & (t % (2 * L) >= L)
    return c


class Steps:

    def __init__(self, at):
        self.at, self.count, self.last = at, {}, None

    def __call__(self, sem, name=None, by=1):
        n = self.count.get(sem.name, 0) + by
        self.count[sem.name] = n
        self.last = (sem, n)
        if name is not None:
            self.at[name] = (sem.name, n)
        return sem, by

    def skip(self, sem, by):
        self.count[sem.name] = self.count.get(sem.name, 0) + by
        self.last = (sem, self.count[sem.name])


def chunk_table():
    first, n = {}, 0
    sizes = []
    for f, after in ((0, [("hgrn", 16), ("aout", 4)]), (1, [("ple0", 5), ("kvd", 2)]),
                     (2, [("dq", 2), ("kvup", 4), ("uq", 8), ("bout", 8)]), (3, [("ple1", 5)])):
        sizes += [(f"in{f}", 2 * PAIRS), (f"out{f}", PAIRS)] + after
    for l in range(2):
        sizes += [(f"win{l}", 16), (f"wout{l}", 4)]
    for name, size in sizes:
        first[name] = n
        n += size
    return first, n


def build(nc, io, known):
    at = {}
    first, n_chunks = chunk_table()

    parts = {first["kvd"] + 1: 2}
    parts.update({first["uq"] + u: 4 for u in range(8)})
    landings = []
    for c in range(n_chunks):
        landings.append((landings[c - NRAW] if c >= NRAW else 0) + parts.get(c, 1))

    names = ["x_landed", "setup_landed", "ple_landed", "cmp_landed", "out_landed", "landed0", "landed1",
             "hi_ready", "lo_ready", "pe_groups", "act_steps", "dve_steps", "pool_steps",
             "gate_scaled", "up_scaled", "silu_ready", "hidden_ready", "hidden_hi", "hidden_lo", "mod_landed", "mod_steps"]
    sem = {n: nc.alloc_semaphore(n) for n in names}
    landed = [sem["landed0"], sem["landed1"]]
    hi_ready, lo_ready, pe_groups = sem["hi_ready"], sem["lo_ready"], sem["pe_groups"]
    act_steps, dve_steps, pool_steps = sem["act_steps"], sem["dve_steps"], sem["pool_steps"]
    gate_scaled, up_scaled, silu_ready = sem["gate_scaled"], sem["up_scaled"], sem["silu_ready"]
    hidden_ready, hidden_hi, hidden_lo = sem["hidden_ready"], sem["hidden_hi"], sem["hidden_lo"]

    def when(name):
        s, n = known[name] if known else ("pe_groups", 1)
        return sem[s], n

    base = [(nc.sbuf_base + 63) // 64 * 64]

    def fixed(name, shape, dt=F32):
        size = int(np.prod(shape[1:])) * 4
        t = nc.alloc_sbuf_tensor_at(name, shape, dt, offset=base[0])
        base[0] += (size + 63) // 64 * 64
        return t

    w_raw = fixed("w_raw", [P, NRAW, CH])
    w_hi = fixed("w_hi", [P, NSLOT, CH], F32R)
    w_lo = fixed("w_lo", [P, NSLOT, CH], F32R)
    X = fixed("X", [P, KD, T])
    xh = fixed("xh", [P, KD, T], F32R)
    xl = fixed("xl", [P, KD, T], F32R)
    sq_at = base[0]
    sq = fixed("sq", [P, KD, T])
    rs = fixed("rs", [P, T])
    std = fixed("std", [P, T])
    ones = fixed("ones", [P, P])
    const = fixed("const", [P, C_N])
    cos = fixed("cos", [P, T])
    sin = fixed("sin", [P, T])
    col0 = fixed("col0", [P, 104])
    col1 = fixed("col1", [P, 88])
    col2 = fixed("col2", [P, 64])
    latent_at = base[0]
    ckh = fixed("ckh", [P, 2, T], F32R)
    ckl = fixed("ckl", [P, 2, T], F32R)
    krz = fixed("krz", [P, 2, T])
    eps = fixed("eps", [P, 1])
    lb = fixed("lb", [P, KD])
    oml = fixed("oml", [P, KD])
    small = fixed("small", [P, 64])
    rst = fixed("rst", [P, TB])
    csf = fixed("csf", [P, KD])
    mods = fixed("mods", [P, 2, 24])
    gpre = fixed("gpre", [P, KD])
    gpost = fixed("gpost", [P, KD])
    ptok = fixed("ptok", [P, 2, TB, T])
    region = base[0]

    def at_offset(start):
        pos = [start]

        def place(name, shape, dt=F32):
            size = int(np.prod(shape[1:])) * 4
            t = nc.alloc_sbuf_tensor_at(name, shape, dt, offset=pos[0])
            pos[0] += (size + 63) // 64 * 64
            assert pos[0] <= nc.sbuf_usable_end, (name, pos[0])
            return t
        return place, pos

    place, _ = at_offset(region)
    xtok = place("xtok", [P, TB, D])
    vrow0 = place("vrow0", [P, P])
    vrow1 = place("vrow1", [P, P])
    vrow2 = place("vrow2", [P, P])
    pos_i = place("pos_i", [P, T], I32)
    ang = place("ang", [P, T])
    turns = place("turns", [P, T])
    red = place("red", [P, T])
    mag = place("mag", [P, T])
    place, _ = at_offset(region)
    hh = place("hh", [P, KF, T], F32R)
    hl = place("hl", [P, KF, T], F32R)
    gate_t = place("gate_t", [P, 2, 2, T])
    up_t = place("up_t", [P, 2, 2, T])
    silu_t = place("silu_t", [P, 2, 2, T])
    hid_t = place("hid_t", [P, 2, 2, T])
    mod_raw = place("mod_raw", [P, KD // 2, 256])
    mod_acc = place("mod_acc", [P, MOD, 256])
    place, _ = at_offset(region)
    hg_a = place("hg_a", [P, KD, T])
    hg_k = place("hg_k", [P, KD, T])
    hg_b = place("hg_b", [P, KD, T])
    hg_q = place("hg_q", [P, KD, T])
    hg_v = place("hg_v", [P, TB, D])
    hg_g = place("hg_g", [P, KD, T])
    hg_f0 = place("hg_f0", [P, KD, T])
    hg_f = [hg_f0, sq]
    hg_s = place("hg_s", [P, KD, 3, P])
    hg_t = place("hg_t", [P, KD])
    place, _ = at_offset(region)
    pt = place("pt", [P, 2, T])
    pth = place("pth", [P, 2, T], F32R)
    ptl = place("ptl", [P, 2, T], F32R)
    pp = place("pp", [P, KD, T])
    pg = place("pg", [P, KD, T])
    place, _ = at_offset(region)
    ck = place("ck", [P, 2, T])
    kr = place("kr", [P, T])
    kr_t = place("kr_t", [P, 2, T])
    rs2_kv = place("rs2_kv", [P, T])
    std2_kv = place("std2_kv", [P, T])
    place, posn = at_offset(region)
    oh_at = posn[0]
    qn = place("qn", [P, HEADS_B, T])
    ol_at = posn[0]
    kn = place("kn", [P, HEADS_B, T])
    qr = place("qr", [P, HEADS_B // 2, T])
    vb = place("vb", [P, TB, HEADS_B * VDIM])
    temp_at = posn[0]
    cq = place("cq", [P, 4, T])
    cqh = place("cqh", [P, 4, T], F32R)
    cql = place("cql", [P, 4, T], F32R)
    place, _ = at_offset(sq_at)
    qr_t = place("qr_t", [P, 2, T])
    qraw = place("qraw", [P, 2, T])
    rs2 = place("rs2", [P, T])
    std2 = place("std2", [P, T])
    place, _ = at_offset(oh_at)
    oh = place("oh", [P, HEADS_B, T], F32R)
    place, _ = at_offset(ol_at)
    ol = place("ol", [P, HEADS_B, T], F32R)
    place, _ = at_offset(temp_at)
    sB = place("sB", [P, 3, 2, 3 * P])
    nmB = place("nmB", [P, 3, 4])
    denB = place("denB", [P, 3, 4])
    rdB = place("rdB", [P, 3, 4])
    place, _ = at_offset(sq_at)
    ptB = place("ptB", [P, 2, 2, 3 * P])
    place, posn = at_offset(region)
    qm = place("qm", [P, 4, T])
    qs = place("qs", [P, 4, T])
    kmz = place("kmz", [P, 4, 2, T])
    ksz = place("ksz", [P, GROUPS, 2, T])
    kwz = place("kwz", [P, GROUPS, 2, T])
    y_at = posn[0]
    vmz = place("vmz", [P, TB, HEADS_C, P])
    vsz = place("vsz", [P, TB, GROUPS, 2, P])
    vwz = place("vwz", [P, TB, GROUPS, 2, P])
    zm = place("zm", [P, 4, T])
    zn = place("zn", [P, 4, T])
    kcz = place("kcz", [P, GROUPS, 2, 16])
    vcz = place("vcz", [16, GROUPS, 2, P])
    gates = place("gates", [P, TB, 24])
    cbias = place("cbias", [P, HEADS_C, TB, CMP_T])
    gh = place("gh", [DH, 64])
    gx = place("gx", [DH, 64])
    wc2 = place("wc2", [DH, 3, DH])
    temp_at = posn[0]
    kA = place("kA", [P, 4, T])
    win = place("win", [P, 2, 16, 2 * CMP_T])
    wc1 = place("wc1", [P, 2, 16, DH])
    place, _ = at_offset(temp_at)
    sC = place("sC", [P, 3, 2, 3 * P])
    ptC = place("ptC", [P, 2, 2, 3 * P])
    nmC = place("nmC", [P, 3, 4])
    denC = place("denC", [P, 3, 4])
    rdC = place("rdC", [P, 3, 4])
    yC = place("yC", [P, 2, T])
    place, _ = at_offset(latent_at)
    kc2 = place("kc2", [P, 2, GROUPS, T])
    place, _ = at_offset(y_at)
    y2 = place("y2", [P, KD, T])
    bias = sq
    place, _ = at_offset(region)
    otok = place("otok", [P, TB, D])

    bank = [nc.alloc_psum_tensor(f"bank{i}", [P, 512], F32) for i in range(8)]
    ident = const[:, C_IDENT:C_IDENT + P]

    def g_norm(l, g):
        return lambda k: col0[:, (l * 4 + g) * KD + k:(l * 4 + g) * KD + k + 1]

    def g_kv(k):
        return col0[:, 81 + k:82 + k]

    def g_latent(k):
        return col0[:, 89 + k:90 + k]

    def g_q(k):
        return col0[:, 91 + k:92 + k]

    def g_final(k):
        return col0[:, 95 + k:96 + k]

    out_gain = col0[:, 80:81]

    def rep(ap, n):
        shape = list(ap.shape)
        return ap.unsqueeze(1).to_broadcast([shape[0], n] + shape[1:])

    def two(ap):
        return ap.rearrange("p (a n) -> p a n", a=2)

    def f32(ap):
        return ap.bitcast(F32)

    def slot(w, c, k):
        rows, cols = k
        return w[:, c % NSLOT, 0:rows * cols].rearrange("p (k n) -> p k n", k=rows)

    WIN = ([("qm", j) for j in range(2)] + [("km", j) for j in range(2)] + [("vm", j) for j in range(2)]
           + [("zm", j) for j in range(2)] + [("qn", j) for j in range(2)]
           + [("kcvc", 0), ("ksvs", 0), ("kwvw", 0), ("gl", 0)] + [("zn", j) for j in range(2)])

    ITEMS = [("moba", m, True, True) for m in range(4)]
    for m in range(4):
        ITEMS += [("win", m, True, False), ("slc", m, False, False), ("cmp", m, False, True)]

    block_ctx = nc.Block()
    block = block_ctx.__enter__()

    @block.sync
    def _(sp):
        def slot_free(c):
            if c >= NRAW:
                sp.wait_ge(lo_ready, c - NRAW + 1)

        def load(c, k, src):
            slot_free(c)
            dst = w_raw[:, c % NRAW, 0:k[0] * k[1]].rearrange("p (k n) -> p k n", k=k[0])
            sp.dma_start(dst, src.rearrange("(k p) n -> p k n", p=P)).then_inc(landed[c % NRAW], 16)

        def load_ffn(f):
            l, w = f // 2, f % 2
            c = first[f"in{f}"]
            w_in, w_out = io["ffn_w_in"][l, w], io["ffn_w_out"][l, w]

            def pair(c, p, it):
                for half in range(2):
                    if it is None and c + half < NRAW:
                        pass
                    else:
                        sp.wait_ge(lo_ready, c + half - NRAW + 1 + (0 if it is None else 2 * it))
                    cols = bass.ds(half * FF + 256 * p + (0 if it is None else 256 * it), 256)
                    sp.dma_start(w_raw[:, (c + half) % NRAW, :].rearrange("p (k n) -> p k n", k=KD),
                                 w_in[:, cols].rearrange("(k p) n -> p k n", p=P)).then_inc(landed[(c + half) % NRAW], 16)

            pair(c, 0, None)
            with sp.Fori(0, PAIRS - 1) as it:
                pair(c + 2, 1, it)
            c = first[f"out{f}"]
            load(c, (2, D), w_out[0:256, :])
            with sp.Fori(0, (PAIRS - 1) // 2) as it:
                for j in range(2):
                    cc = c + 1 + j
                    sp.wait_ge(lo_ready, cc - NRAW + 1 + 2 * it)
                    rows = bass.ds(256 * (1 + j) + 512 * it, 256)
                    sp.dma_start(w_raw[:, cc % NRAW, :].rearrange("p (k n) -> p k n", k=2),
                                 w_out[rows, :].rearrange("(k p) n -> p k n", p=P)).then_inc(landed[cc % NRAW], 16)

        def load_cols(name, w, width, cols, count=None):
            c = first[name]
            for j in range(count if count is not None else cols // width):
                load(c + j, (w.shape[0] // P, width), w[:, j * width:(j + 1) * width])

        def load_rows(name, w):
            c = first[name]
            for j in range(w.shape[0] // 256):
                load(c + j, (2, w.shape[1]), w[256 * j:256 * j + 256, :])

        load_ffn(0)
        a_in = io["a_w_in"][0]
        for n, seg in enumerate((1, 0, 2, 3)):
            for j in range(4):
                load(first["hgrn"] + 4 * n + j, (KD, 256), a_in[:, seg * D + 256 * j:seg * D + 256 * j + 256])
        load_cols("aout", io["a_w_out"][0], 256, D)
        load_ffn(1)

        def load_ple(l):
            c = first[f"ple{l}"]
            load(c, (2, D), io["ple_w_in"][l])
            for j in range(4):
                load(c + 1 + j, (KD, 256), io["ple_w_gate"][l][:, 256 * j:256 * j + 256])

        load_ple(0)
        load(first["kvd"], (KD, 256), io["kv_w_down"][:, 0:256])
        c = first["kvd"] + 1
        slot_free(c)
        for h in range(2):
            sp.dma_start(w_raw[:, c % NRAW, 0:KD * P].rearrange("p (k h n) -> p k h n", k=KD, h=2)[:, :, h, :],
                         io["kv_w_down"][:, 256:320].rearrange("(k p) n -> p k n", p=P)).then_inc(landed[c % NRAW], 16)
        load_ffn(2)
        load_cols("dq", io["b_w_dq"][0], 256, 512)
        for j in range(4):
            load(first["kvup"] + j, (2, D), io["kv_w_up"][:, D * j:D * j + D])
        for u in range(8):
            c = first["uq"] + u
            slot_free(c)
            for at_, width in ((0, NOPE), (NOPE, ROPE)):
                for h in range(2):
                    src = io["b_w_uq"][0][:, (2 * u + h) * (NOPE + ROPE) + at_:(2 * u + h) * (NOPE + ROPE) + at_ + width]
                    col = 2 * at_ + h * width
                    sp.dma_start(w_raw[:, c % NRAW, 0:4 * 384].rearrange("p (k n) -> p k n", k=4)[:, :, col:col + width],
                                 src.rearrange("(k p) n -> p k n", p=P)).then_inc(landed[c % NRAW], 16)
        load_rows("bout", io["b_w_out"][0])
        load_ffn(3)
        load_ple(1)
        for l in range(2):
            w = io["w_in_2"][l]
            for n, (name, j) in enumerate(WIN):
                width = 24 if name == "gl" else 256
                load(first[f"win{l}"] + n, (KD, width), w[:, OFF[name] + 256 * j:OFF[name] + 256 * j + width])
            load_cols(f"wout{l}", io["w_out_2"][l], 256, D)
        for b in range(TB):
            sp.wait_ge(*when(("otok", b)))
            sp.dma_start(io["out"][0, b * P:(b + 1) * P, :], otok[:, b, :]).then_inc(sem["out_landed"], 16)
        sp.wait_ge(sem["out_landed"], 16 * TB)

    @block.gpsimd
    def _(pool):
        did = Steps(at)
        nc.gpsimd.memset(ones[:, :], 1.0).then_inc(*did(pool_steps))
        nc.gpsimd.memset(eps[:, :], EPS).then_inc(*did(pool_steps))
        nc.gpsimd.memset(krz[:, :, :], 0.0).then_inc(*did(pool_steps, "memsets"))
        G = nc.gpsimd

        def modulation(f):
            l = f // 2
            steps, landed_ = sem["mod_steps"], sem["mod_landed"]
            pool.wait_ge(*when({0: "csf", 1: ("x", 2, 3), 2: "ckl", 3: ("x", 6, 3)}[f]))
            if f:
                pool.wait_ge(*when(("modsum", f - 1)))
            for j in range(MOD):
                acc = mod_acc[:, j, :]
                n = MOD_STEPS * (MOD * f + j)
                for half in range(2):
                    if n:
                        pool.wait_ge(steps, n)
                    cols = slice(256 * (MOD * (f % 2) + j), 256 * (MOD * (f % 2) + j + 1))
                    pool.dma_start(mod_raw[:, :, :], io["w_ada_2"][l][512 * half:512 * half + 512, cols].rearrange("(k p) n -> p k n", p=P)).then_inc(landed_, 16)
                    pool.wait_ge(landed_, 16 * (2 * (MOD * f + j) + half + 1))
                    c = csf[:, KD // 2 * half:KD // 2 * (half + 1)].unsqueeze(2).to_broadcast([P, KD // 2, 256])
                    G.tensor_tensor(mod_raw[:, :, :], mod_raw[:, :, :], c, ALU.mult).then_inc(steps, 1)
                    pool.wait_ge(steps, n + 1)
                    G.tensor_tensor(mod_raw[:, 0:2, :], mod_raw[:, 0:2, :], mod_raw[:, 2:4, :], ALU.add).then_inc(steps, 1)
                    pool.wait_ge(steps, n + 2)
                    if half == 0:
                        G.tensor_tensor(acc, mod_raw[:, 0, :], mod_raw[:, 1, :], ALU.add).then_inc(steps, 1)
                    else:
                        G.tensor_tensor(mod_raw[:, 0, :], mod_raw[:, 0, :], mod_raw[:, 1, :], ALU.add).then_inc(steps, 1)
                        pool.wait_ge(steps, n + 3)
                        G.tensor_tensor(acc, acc, mod_raw[:, 0, :], ALU.add).then_inc(steps, 1)
                    n += 3

        def levels():
            pool.wait_ge(*when("scans"))

            def halves(t, L):
                r = t[:, :, :].rearrange("p h n -> p (h n)").rearrange("p (b two n) -> p b two n", two=2, n=L)
                return r[:, :, 0, :], r[:, :, 1, :]

            for n, L in enumerate(LEVELS):
                bl, br = halves(hg_b, L)
                al, ar = halves(hg_a, L)
                end = bl[:, :, L - 1:L].to_broadcast([P, HEADS_A * T // (2 * L), L])
                if n == 0:
                    G.tensor_copy(ar, br).then_inc(*did(pool_steps))
                else:
                    pool.wait_ge(*when(("exp", n - 1)))
                    G.tensor_tensor(ar, br, end, ALU.subtract).then_inc(*did(pool_steps))
                G.tensor_tensor(al, end, bl, ALU.subtract).then_inc(*did(pool_steps, ("diff", n)))
            b = hg_b[:, :, :].rearrange("p h (c n) -> p h c n", n=CHUNK_A)
            a = hg_a[:, :, :].rearrange("p h (c n) -> p h c n", n=CHUNK_A)
            def end(c):
                return b[:, :, c, CHUNK_A - 1:CHUNK_A].to_broadcast([P, HEADS_A, CHUNK_A])
            G.tensor_tensor(hg_t[:, :].unsqueeze(2), b[:, :, 0, CHUNK_A - 1:CHUNK_A], b[:, :, 1, CHUNK_A - 1:CHUNK_A], ALU.add).then_inc(*did(pool_steps))
            pool.wait_ge(*did.last)
            pool.wait_ge(*when(("exp", 6)))
            G.tensor_tensor(a[:, :, 0, :], hg_t[:, :].unsqueeze(2).to_broadcast([P, HEADS_A, CHUNK_A]), b[:, :, 0, :], ALU.subtract).then_inc(*did(pool_steps))
            G.tensor_tensor(a[:, :, 1, :], end(1), b[:, :, 1, :], ALU.subtract).then_inc(*did(pool_steps))
            G.tensor_copy(a[:, :, 2, :], b[:, :, 2, :]).then_inc(*did(pool_steps))
            G.tensor_tensor(a[:, :, 3, :], b[:, :, 3, :], end(2), ALU.add).then_inc(*did(pool_steps, ("diff", 7)))

        modulation(0)
        levels()
        for f in range(1, 4):
            modulation(f)
        for l in range(2):
            pool.wait_ge(*when(("x", 9 + l, 3)))
            for z in (kmz, vmz, ksz, kwz, vsz, vwz, kcz, vcz):
                last = nc.gpsimd.memset(z[tuple(slice(None) for _ in z.shape)], 0.0).then_inc(*did(pool_steps))
            nc.gpsimd.memset(small[:, 32:33], 0.0).then_inc(*did(pool_steps, ("zeros", l)))

    @block.scalar
    def _(act):
        did = Steps(at)
        A = nc.scalar.activation

        setup = [(const[:, :], io["consts"]),
                 (vrow0[0:64, :], io["norm_gains"].rearrange("l g (k p) -> (l g k) p", p=P)),
                 (vrow0[64:80, :], io["a_lb_logits"].rearrange("r (k p) -> (r k) p", p=P)),
                 (vrow0[80:81, :], io["a_out_gain"]),
                 (vrow0[81:89, :], io["kv_norm_in"].rearrange("(k p) -> k p", p=P)),
                 (vrow0[89:91, :], io["kv_latent_norm"].rearrange("(k p) -> k p", p=P)),
                 (vrow0[91:95, :], io["b_q_norm"].rearrange("l (k p) -> (l k) p", p=P)),
                 (vrow0[95:103, :], io["final_norm"].rearrange("(k p) -> k p", p=P)),
                 (vrow1[0:48, :], io["b_ada_2"].rearrange("l (k p) -> (l k) p", p=P)),
                 (vrow1[48:64, :], io["g_pre_2"].rearrange("l (k p) -> (l k) p", p=P)),
                 (vrow1[64:80, :], io["g_post_2"].rearrange("l (k p) -> (l k) p", p=P)),
                 (vrow1[80:88, :], io["c_2"].rearrange("l (k p) -> (l k) p", p=P)),
                 (vrow2[0:32, :], io["pe_k_2"].rearrange("l (r a) d -> (l r) (a d)", a=2)),
                 (vrow2[32:64, :], io["pe_v_2"].rearrange("l (r a) d -> (l r) (a d)", a=2)),
                 (pos_i[0:1, :], io["positions"])]
        act.dma_start(xtok[:, :, :], io["x"][0].rearrange("(b p) n -> p b n", p=P)).then_inc(sem["x_landed"], 16)
        for dst, src in setup:
            act.dma_start(dst, src).then_inc(sem["setup_landed"], 16)
        for l in range(2):
            act.dma_start(ptok[:, l, :, :], io["p"][l, 0].rearrange("(b p) n -> p b n", p=P)).then_inc(sem["ple_landed"], 16)

        def hi(c, it=None):
            if c >= n_chunks:
                return
            i2 = 0 if it is None else 32 * it
            i4 = 0 if it is None else 4 * it
            act.wait_ge(landed[c % NRAW], 16 * landings[c] + i2)
            if c >= NSLOT:
                act.wait_ge(pe_groups, when(("chunk", c - NSLOT))[1] + i4)
            A(w_hi[:, c % NSLOT, :], w_raw[:, c % NRAW, :], ACT.Copy).then_inc(*did(hi_ready))

        def norm(nu, v, gain, s, free):
            for m in range(4):
                act.wait_ge(*when(("x", v, m)))
                if s is not None:
                    if m == 0 and s > 0:
                        act.wait_ge(*when(("sums", s - 1)))
                    A(sq[:, 2 * m:2 * m + 2, :], X[:, 2 * m:2 * m + 2, :], ACT.Square).then_inc(*did(act_steps, ("sq", s, m)))
                if m == 0 and free is not None:
                    act.wait_ge(*when(free))
                for k in (2 * m, 2 * m + 1):
                    A(xh[:, k, :], X[:, k, :], ACT.Copy, scale=gain(k)).then_inc(*did(act_steps, ("xh", nu, k)))

        def root(s):
            act.wait_ge(*when(("sums", s)))
            if s > 0:
                act.wait_ge(*when(("rs", s - 1)))
            A(std[:, :], bank[3][:, 0:T], ACT.Sqrt, bias=eps[:, :], scale=1.0 / D).then_inc(*did(act_steps, ("std", s)))

        def ffn(f, nu, v, gain, s, free):
            norm(nu, v, gain, s, free)
            c = first[f"in{f}"]
            n0 = PAIRS * f

            def pair(c, p, it=None):
                o = 0 if it is None else 2 * it
                hi(c + AHEAD, it)
                act.wait_ge(gate_scaled, n0 + p + 1 + o)
                if it is not None or p >= 2:
                    act.wait_ge(hidden_ready, n0 + max(p - 1, 1) + o)
                A(silu_t[:, p % 2, :, :], gate_t[:, p % 2, :, :], ACT.Silu).then_inc(*did(silu_ready))
                hi(c + 1 + AHEAD, it)
                act.wait_ge(hidden_ready, n0 + p + 1 + o)
                k = bass.ds(2 * p + (0 if it is None else 4 * it), 2)
                A(hh[:, k, :], hid_t[:, p % 2, :, :], ACT.Copy).then_inc(*did(hidden_hi))

            def first_pair():
                hi(c + AHEAD)
                if s is not None:
                    root(s)
                act.wait_ge(gate_scaled, n0 + 1)
                A(silu_t[:, 0, :, :], gate_t[:, 0, :, :], ACT.Silu).then_inc(*did(silu_ready))
                hi(c + 1 + AHEAD)
                act.wait_ge(hidden_ready, n0 + 1)
                A(hh[:, 0:2, :], hid_t[:, 0, :, :], ACT.Copy).then_inc(*did(hidden_hi))

            first_pair()
            with act.Fori(0, (PAIRS - 1) // 2) as it:
                for j in range(2):
                    pair(c + 2 + 2 * j, 1 + j, it)
            turns_left = (PAIRS - 1) // 2 - 1
            did.skip(hi_ready, 4 * turns_left)
            did.skip(silu_ready, 2 * turns_left)
            did.skip(hidden_hi, 2 * turns_left)
            c = first[f"out{f}"]
            for q in range(2):
                hi(c + q + AHEAD)
            with act.Fori(0, 2) as it:
                for q in range(4):
                    hi(c + 2 + q + AHEAD, it)
            did.skip(hi_ready, 4)
            hi(c + 10 + AHEAD)

        def rope_tables():
            act.wait_ge(*when("angles"))
            A(sin[:, :], red[:, :], ACT.Sin).then_inc(*did(act_steps))
            act.wait_ge(*when("quarter"))
            A(cos[:, :], mag[:, :], ACT.Sin).then_inc(*did(act_steps, "sin"))

        for c in range(AHEAD):
            hi(c)
        act.wait_ge(*when(("col", 1)))
        A(csf[:, :], col1[:, 80:88], ACT.Silu).then_inc(*did(act_steps, "csf"))
        act.wait_ge(*when("lb_shift"))
        A(small[:, 16:32], small[:, 0:16], ACT.Exp).then_inc(*did(act_steps, "lb_exp"))
        rope_tables()
        act.wait_ge(*when("memsets"))
        ffn(0, 0, 0, g_norm(0, 0), 0, None)

        c0 = first["hgrn"]
        norm(1, 1, g_norm(0, 1), 1, ("chunk", first["out0"] - 1))
        for j in range(4):
            hi(c0 + j + AHEAD)
            if j == 0:
                root(1)
            act.wait_ge(*when(("f", j)))
            A(hg_k[:, 2 * j:2 * j + 2, :], hg_a[:, 2 * j:2 * j + 2, :], ACT.Sigmoid, scale=-1.0).then_inc(*did(act_steps))
            act.wait_ge(*did.last)
            A(hg_a[:, 2 * j:2 * j + 2, :], hg_a[:, 2 * j:2 * j + 2, :], ACT.Sigmoid).then_inc(*did(act_steps, ("sg", j)))
        act.wait_ge(*did.last)
        act.wait_ge(*when("lb"))
        for h in range(HEADS_A):
            A(hg_a[:, h, :], hg_a[:, h, :], ACT.Ln, bias=lb[:, h:h + 1], scale=oml[:, h:h + 1]).then_inc(*did(act_steps, ("ln", h)))
        for j in range(4):
            hi(c0 + 4 + j + AHEAD)

        def level_exp(n):
            act.wait_ge(*when(("diff", n)))
            if n >= 2:
                act.wait_ge(*when((("lev", n - 2), 3)))
            elif n == 1:
                act.wait_ge(*when(("sums", 1)))
            A(hg_f[n % 2][:, :, :], hg_a[:, :, :], ACT.Exp).then_inc(*did(act_steps, ("exp", n)))

        level_exp(0)
        for n in range(8):
            hi(c0 + 8 + n + AHEAD)
            if n < 7:
                level_exp(n + 1)
        act.wait_ge(*when(("g", 3)))
        A(hg_g[:, :, :], hg_g[:, :, :], ACT.Sigmoid).then_inc(*did(act_steps, "gate_sg"))
        for m in range(4):
            act.wait_ge(*when(("o", m)))
            A(sq[:, 2 * m:2 * m + 2, :], two(bank[4 + m][:, :]), ACT.Square).then_inc(*did(act_steps, ("osq", m)))
        for m in range(4):
            act.wait_ge(*when(("osum", m)))
            A(hg_a[:, 2 * m:2 * m + 2, :], two(bank[m][:, :]), ACT.Ln, bias=eps[:, :], scale=1.0 / P).then_inc(*did(act_steps, ("oln", m)))
        for m in range(4):
            act.wait_ge(*when(("oln", m)))
            A(hg_a[:, 2 * m:2 * m + 2, :], hg_a[:, 2 * m:2 * m + 2, :], ACT.Exp, scale=-0.5).then_inc(*did(act_steps, ("ors", m)))
        for m in range(4):
            act.wait_ge(*when(("og", m)))
            A(xh[:, 2 * m:2 * m + 2, :], hg_b[:, 2 * m:2 * m + 2, :], ACT.Copy).then_inc(*did(act_steps, ("oh", m)))
        for j in range(4):
            hi(first["aout"] + j + AHEAD)

        ffn(1, 3, 2, g_norm(0, 2), 2, ("chunk", first["in1"] - 1))

        def ple(l, nu, v, s):
            c = first[f"ple{l}"]
            hi(c + AHEAD)
            act.wait_ge(*when(("pt", l)))
            A(pth[:, :, :], pt[:, :, :], ACT.Copy).then_inc(*did(act_steps, ("pth", l)))
            norm(nu, v, g_norm(l, 3), s, ("chunk", c - 1))
            for j in range(4):
                hi(c + 1 + j + AHEAD)
                if j == 0:
                    root(s)
                act.wait_ge(*when(("pg", l, j)))
                A(pg[:, 2 * j:2 * j + 2, :], pg[:, 2 * j:2 * j + 2, :], ACT.Sigmoid).then_inc(*did(act_steps, ("pgs", l, j)))

        ple(0, 4, 3, 3)

        norm(5, 4, g_kv, 4, ("chunk", first["kvd"] - 1))
        hi(first["kvd"] + AHEAD)
        root(4)
        act.wait_ge(*when("ck"))
        A(sq[:, 0:2, :], ck[:, :, :], ACT.Square).then_inc(*did(act_steps, "cksq"))
        hi(first["kvd"] + 1 + AHEAD)
        act.wait_ge(*when("cksum"))
        A(std2_kv[:, :], bank[6][:, 0:T], ACT.Sqrt, bias=eps[:, :], scale=1.0 / 256).then_inc(*did(act_steps, "ckstd"))
        act.wait_ge(*when("ckn"))
        A(ckh[:, :, :], ck[:, :, :], ACT.Copy).then_inc(*did(act_steps, "ckh"))

        ffn(2, 6, 4, g_norm(1, 0), None, ("chunk", first["in2"] - 1))

        norm(7, 5, g_norm(1, 1), 5, ("chunk", first["out2"] - 1))
        c0 = first["dq"]
        for j in range(2):
            hi(c0 + j + AHEAD)
            if j == 0:
                root(5)
            act.wait_ge(*when(("cq", j)))
            A(sq[:, 2 * j:2 * j + 2, :], cq[:, 2 * j:2 * j + 2, :], ACT.Square).then_inc(*did(act_steps, ("cqsq", j)))
        for u in range(4):
            hi(first["kvup"] + u + AHEAD)
            for b in range(TB):
                act.wait_ge(*when(("v", u, b)))
                A(vb[:, b, 512 * u:512 * u + 512], bank[4 * (u % 2) + 2 + b][:, :], ACT.Copy).then_inc(*did(act_steps, ("vb", u, b)))
            if u == 0:
                act.wait_ge(*when("cqsum"))
                A(std2[:, :], bank[4][:, 0:T], ACT.Sqrt, bias=eps[:, :], scale=1.0 / 512).then_inc(*did(act_steps, "cqstd"))
            if u == 1:
                for j in range(4):
                    act.wait_ge(*when(("cqn", j)))
                    A(cqh[:, j, :], cq[:, j, :], ACT.Copy).then_inc(*did(act_steps, ("cqh", j)))
        for u in range(8 - AHEAD):
            hi(first["uq"] + u + AHEAD)

        def exps(item, s, nm, den):
            act.wait_ge(*when(("max", item)))
            for h in range(2):
                for b in range(TB):
                    cols = slice(0, P) if b == 0 else slice(P, 3 * P)
                    A(s[:, h, cols], s[:, h, cols], ACT.Exp, bias=nm[:, 2 * b + h:2 * b + h + 1],
                      accum_out=den[:, 2 * b + h:2 * b + h + 1]).then_inc(*did(act_steps, ("exps", item)))

        def probs_t(item, buf, width):
            act.wait_ge(*when(("pt", item)))
            for h in range(2):
                A(buf[:, h, 0:width], bank[4 + h][:, 0:width], ACT.Copy).then_inc(*did(act_steps, ("ptcopy", item)))

        for i in range(8):
            exps(("b", i), sB[:, i % 3], nmB[:, i % 3], denB[:, i % 3])
            if i >= 6:
                hi(first["bout"] + i - 6)
            if i >= 1:
                probs_t(("b", i - 1), ptB[:, (i - 1) % 2], 3 * P)
            if i >= 2:
                act.wait_ge(*when(("ob", i - 2)))
                A(oh[:, 2 * (i - 2):2 * (i - 2) + 2, :], two(bank[6 + i % 2][:, :]), ACT.Copy).then_inc(*did(act_steps, ("oh", "b", i - 2)))
        probs_t(("b", 7), ptB[:, 1], 3 * P)
        hi(first["bout"] + 2)
        for i in (6, 7):
            act.wait_ge(*when(("ob", i)))
            A(oh[:, 2 * i:2 * i + 2, :], two(bank[6 + i % 2][:, :]), ACT.Copy).then_inc(*did(act_steps, ("oh", "b", i)))
        for j in range(8):
            hi(first["bout"] + j + AHEAD)

        ffn(3, 8, 6, g_norm(1, 2), 6, ("chunk", first["in3"] - 1))
        ple(1, 9, 7, 7)

        def squares(v, s):
            for m in range(4):
                act.wait_ge(*when(("x", v, m)))
                if m == 0:
                    act.wait_ge(*when(("sums", s - 1)))
                A(sq[:, 2 * m:2 * m + 2, :], X[:, 2 * m:2 * m + 2, :], ACT.Square).then_inc(*did(act_steps, ("sq", s, m)))
            root(s)

        squares(8, 8)

        for l in range(2):
            nu, v, s = 10 + 2 * l, 9 + l, 9 + 2 * l
            act.wait_ge(*when(("x", v, 3)))
            for kv, name in enumerate(("ck", "cv")):
                act.dma_start(wc1[:, kv, :, :], io[f"w_{name}1_2"][l].rearrange("(r p) e -> p r e", p=P)).then_inc(sem["cmp_landed"], 16)
                for n in ((0, 1), (2,))[kv]:
                    act.dma_start(wc2[:, n, :], io[f"w_{name}2_2"][l]).then_inc(sem["cmp_landed"], 16)
            squares(v, s)
            for k in range(KD):
                act.wait_ge(*when(("xn", l, k)))
                A(xh[:, k, :], sq[:, k, :], ACT.Identity, bias=mods[:, l, k:k + 1]).then_inc(*did(act_steps, ("xh", nu, k)))
            c0 = first[f"win{l}"]
            for n, (name, j) in enumerate(WIN):
                if n + AHEAD < 16:
                    hi(c0 + n + AHEAD)
                if name in ("zm", "zn"):
                    act.wait_ge(*when(("win", l, n)))
                    z = zm if name == "zm" else zn
                    A(z[:, 2 * j:2 * j + 2, :], two(bank[n % 8][:, :]), ACT.Silu).then_inc(*did(act_steps, ("z", l, n)))
                if name == "gl":
                    act.wait_ge(*when(("win", l, n)))
                    A(gates[:, :, :], two(bank[n % 8][:, 0:64])[:, :, 0:24], ACT.Sigmoid).then_inc(*did(act_steps, ("gates", l)))
            act.wait_ge(*when(("hid", l)))
            A(gh[:, 0:60], bank[0][0:DH, 0:60], ACT.Gelu_apprx_tanh).then_inc(*did(act_steps, ("gelu", l)))

            def tail(i):
                kind, m, start, stop = ITEMS[i]
                probs_t(("c", l, i), ptC[:, i % 2], 2 * P if kind == "cmp" else 3 * P)

            def y_hi(i):
                kind, m, start, stop = ITEMS[i]
                if stop:
                    k = m if kind == "moba" else 4 + m
                    act.wait_ge(*when(("y", l, k)))
                    A(xh[:, k, :], yC[:, k % 2, :], ACT.Copy).then_inc(*did(act_steps, ("yh", l, k)))

            for i, (kind, m, start, stop) in enumerate(ITEMS):
                if kind == "cmp":
                    act.wait_ge(*when(("max", ("c", l, i))))
                    for h in range(2):
                        for b in range(TB):
                            cols = slice(16 * b, 16 * b + CMP_T)
                            A(sC[:, i % 3, h, cols], sC[:, i % 3, h, cols], ACT.Exp, bias=nmC[:, i % 3, 2 * b + h:2 * b + h + 1],
                              accum_out=denC[:, i % 3, 2 * b + h:2 * b + h + 1]).then_inc(*did(act_steps, ("exps", ("c", l, i))))
                else:
                    exps(("c", l, i), sC[:, i % 3], nmC[:, i % 3], denC[:, i % 3])
                if i >= 16 - AHEAD:
                    hi(first[f"wout{l}"] + i - 16 + AHEAD)
                if i >= 1:
                    tail(i - 1)
                if i >= 2:
                    y_hi(i - 2)
            tail(len(ITEMS) - 1)
            y_hi(len(ITEMS) - 2)
            y_hi(len(ITEMS) - 1)
            s += 1
            for j in range(4):
                hi(first[f"wout{l}"] + j + AHEAD)
                act.wait_ge(*when(("y2", l, j)))
                A(sq[:, 2 * j:2 * j + 2, :], y2[:, 2 * j:2 * j + 2, :], ACT.Square).then_inc(*did(act_steps, ("sq", s, j)))
            root(s)

    @block.tensor
    def _(pe):
        did = Steps(at)
        mm = nc.tensor.matmul
        release = {}

        def take(b):
            if b in release:
                pe.wait_ge(*when(release[b]))

        def three(out, lhs, rhs, start, stop, skip=False):
            mm(out, lhs[1], rhs[0], start=start, stop=False, skip_group_check=skip)
            mm(out, lhs[0], rhs[1], start=False, stop=False, skip_group_check=skip)
            return mm(out, lhs[0], rhs[0], start=False, stop=stop, skip_group_check=skip)

        def split(c, k, cols=None):
            pair = [slot(w, c, k) for w in (w_hi, w_lo)]
            return pair

        def sums(s):
            take(3)
            for k in range(KD):
                pe.wait_ge(*when(("sq", s, k // 2)))
                last = mm(bank[3][:, 0:T], ones[:, :], sq[:, k, :], start=(k == 0), stop=(k == KD - 1))
            last.then_inc(*did(pe_groups, ("sums", s)))
            release[3] = ("std", s)

        def columns(c, b, xs, waits, name, tiles=2, kd=KD, width=256):
            take(b)
            pe.wait_ge(lo_ready, c + 1)
            w = split(c, (kd, width))
            for n in range(tiles):
                for k in range(kd):
                    if waits is not None and n == 0:
                        pe.wait_ge(*when(waits(k)))
                    last = three(bank[b][:, n * T:(n + 1) * T], [a[:, k, n * P:(n + 1) * P] for a in w],
                                 [a[:, k, :] for a in xs], k == 0, k == kd - 1)
            last.then_inc(*did(pe_groups, name))
            at[("chunk", c)] = at[name]

        def tokens(c, b, xs, name, cols, kd=KD, width=256):
            take(b)
            pe.wait_ge(lo_ready, c + 1)
            w = split(c, (kd, width))
            n = cols.stop - cols.start
            for t in range(TB):
                for k in range(kd):
                    last = three(bank[b][:, t * (512 // TB if n > 32 else 32):t * (512 // TB if n > 32 else 32) + n],
                                 [a[:, k, t * P:(t + 1) * P] for a in xs], [a[:, k, cols] for a in w], k == 0, k == kd - 1)
            last.then_inc(*did(pe_groups, name))
            at[("chunk", c)] = at[name]

        def mod_sums(f):
            take(2)
            pe.wait_ge(sem["mod_steps"], MOD_STEPS * MOD * (f + 1))
            for n in range(2 * MOD):
                last = mm(bank[2][:, n:n + 1], mod_acc[:, n // 2, n % 2 * P:n % 2 * P + P], ones[:, 0:1], start=True, stop=True)
            last.then_inc(*did(pe_groups, ("modsum", f)))
            release[2] = ("mod", f)

        xs = (xh, xl)

        def xwait(nu):
            return lambda k: ("xl", nu, k)

        def ffn(f, nu, s):
            c = first[f"in{f}"]
            n0 = PAIRS * f
            for b in range(4):
                take(b)

            def half(c, b, waits, it=None):
                pe.wait_ge(lo_ready, c + 1 + (0 if it is None else 4 * it))
                w = split(c, (KD, 256))
                for n in range(2):
                    for k in range(KD):
                        if waits and n == 0:
                            pe.wait_ge(*when(("xl", nu, k)))
                        last = three(bank[b][:, n * T:(n + 1) * T], [a[:, k, n * P:(n + 1) * P] for a in w],
                                     [a[:, k, :] for a in xs], k == 0, k == KD - 1)
                return last

            half(c, 0, True).then_inc(*did(pe_groups, ("gate", f)))
            at[("chunk", c)] = at[("gate", f)]
            if s is not None:
                sums(s)
                take(3)
            half(c + 1, 1, False).then_inc(*did(pe_groups, ("up", f)))
            at[("chunk", c + 1)] = at[("up", f)]
            with pe.Fori(0, (PAIRS - 1) // 2) as it:
                for j in range(2):
                    p = 1 + j
                    b = 2 * (p % 2)
                    pe.wait_ge(gate_scaled, n0 + max(p - 1, 1) + 2 * it)
                    half(c + 2 + 2 * j, b, False, it).then_inc(*did(pe_groups))
                    pe.wait_ge(up_scaled, n0 + max(p - 1, 1) + 2 * it)
                    half(c + 3 + 2 * j, b + 1, False, it).then_inc(*did(pe_groups))
            start = at[("up", f)][1]
            for n in range(2 * (PAIRS - 1)):
                at[("chunk", c + 2 + n)] = ("pe_groups", start + 1 + n)
            did.skip(pe_groups, 2 * (PAIRS - 1) - 4)
            for b in range(2):
                release[b], release[2 + b] = ("ffn_" + "gu"[b], f, PAIRS - 1), ("ffn_" + "gu"[b], f, PAIRS - 2)
            c = first[f"out{f}"]
            for b in range(4, 8):
                take(b)

            def rows(c, q, it=None, only=None):
                pe.wait_ge(lo_ready, c + 1 + (0 if it is None else 4 * it))
                pe.wait_ge(hidden_lo, n0 + q + 1 + (0 if it is None else 4 * it))
                w = split(c, (2, D))
                for n in range(KD):
                    for k in range(2):
                        kk = 2 * q + k if it is None else bass.ds(2 * q + k + 8 * it, 1)
                        xk = [a[:, kk, :] if it is None else a[:, kk, :].rearrange("p a n -> p (a n)") for a in (hh, hl)]
                        last = three(bank[4 + n // 2][:, (n % 2) * T:(n % 2 + 1) * T], [a[:, k, n * P:(n + 1) * P] for a in w],
                                     xk, it is None and q == 0 and n % 2 == 0 and k == 0, q == PAIRS - 1 and k == 1, True)
                    if q == PAIRS - 1 and n % 2:
                        last.then_inc(*did(pe_groups, ("ffn_out", f, n // 2)))
                return last

            for q in range(2):
                rows(c + q, q).then_inc(*did(pe_groups, ("chunk", c + q)))
            with pe.Fori(0, 2) as it:
                for q in range(4):
                    rows(c + 2 + q, 2 + q, it).then_inc(*did(pe_groups))
            start = at[("chunk", c + 1)][1]
            for n in range(8):
                at[("chunk", c + 2 + n)] = ("pe_groups", start + 1 + n)
            did.skip(pe_groups, 4)
            rows(c + PAIRS - 1, PAIRS - 1)
            at[("chunk", c + PAIRS - 1)] = at[("ffn_out", f, 3)]
            for m in range(4):
                release[4 + m] = ("x", {0: 1, 1: 3, 2: 5, 3: 7}[f], m)

        pe.wait_ge(sem["setup_landed"], 16 * 15)
        pe.wait_ge(sem["x_landed"], 16)
        for m in range(4):
            for n in range(2):
                for t in range(TB):
                    k = 2 * m + n
                    last = nc.tensor.transpose(bank[m][:, n * T + t * P:n * T + t * P + P], xtok[:, t, k * P:(k + 1) * P], ident)
            last.then_inc(*did(pe_groups, ("xin", m)))
            release[m] = ("x", 0, m)
        for n, (rows_, cnt) in enumerate(((vrow0, 103), (vrow1, 88), (vrow2, 64))):
            nc.tensor.transpose(bank[4 + n][:, 0:cnt], rows_[0:cnt, :], ident[0:cnt, 0:cnt]).then_inc(*did(pe_groups, ("cols", n)))
            release[4 + n] = ("col", n)
        pe.wait_ge(*when("memsets"))
        pe.wait_ge(*when("pos_f"))
        mm(bank[7][:, 0:T], ones[0:1, :], turns[0:1, :], start=True, stop=True).then_inc(*did(pe_groups, "pos"))
        release[7] = "ang0"

        ffn(0, 0, 0)

        c0 = first["hgrn"]
        for j in range(4):
            columns(c0 + j, 4 + j, xs, xwait(1) if j == 0 else None, ("pf", j))
            release[4 + j] = ("f", j)
            if j == 0:
                sums(1)
                mod_sums(0)
        for j in range(4):
            columns(c0 + 4 + j, 4 + j, xs, None, ("pq", j))
            release[4 + j] = ("q", j)
        pe.wait_ge(*when(("rs", 1)))
        take(3)
        for t in range(TB):
            last = nc.tensor.transpose(bank[3][:, t * P:(t + 1) * P], rs[:, t * P:(t + 1) * P], ident)
        last.then_inc(*did(pe_groups, "rst"))
        release[3] = "rst_copy"

        def scores(name, lhs, rhs, done):
            for m in range(4):
                take(m)
                for n in range(4):
                    h, t = 2 * m + n // 2, n % 2
                    last = mm(bank[m][:, n * P:(n + 1) * P], lhs[:, h, t * P:(t + 1) * P], rhs[:, h, t * P:(t + 1) * P], start=True, stop=True)
                last.then_inc(*did(pe_groups, (name, m)))
                release[m] = (done, m)

        pe.wait_ge(*when("k"))
        scores("diag", hg_k, hg_q, "diag_in")

        def level(n):
            pe.wait_ge(*when(("factors", n)))
            scores(("lev", n), hg_f[n % 2], hg_f[n % 2], ("merge", n))

        for n in range(8):
            c, j = c0 + 8 + n, n % 4
            if n < 4:
                tokens(c, 4 + j, xs, ("pi", j), slice(0, 256))
                release[4 + j] = ("vi", j)
            else:
                columns(c, 4 + j, xs, None, ("pg", j))
                release[4 + j] = ("g", j)
            if n < 7:
                level(n)
        pe.wait_ge(*when(("factors", 7)))
        for m in range(2):
            take(m)
            for n in range(4):
                h = 4 * m + n
                last = mm(bank[m][:, n * P:(n + 1) * P], hg_f[1][:, h, 0:P], hg_f[1][:, h, P:T], start=True, stop=True)
            last.then_inc(*did(pe_groups, ("cross", m)))
            release[m] = ("cross_in", m)
        pe.wait_ge(*when(("cross_in", 1)))
        for m in range(4):
            take(4 + m)
            for n in range(2):
                h = 2 * m + n
                o = bank[4 + m][:, n * T:(n + 1) * T]
                v = [hg_v[:, t, h * P:(h + 1) * P] for t in range(TB)]
                mm(o[:, 0:P], v[0], hg_s[:, h, 0, :], start=True, stop=True)
                mm(o[:, P:T], v[0], hg_s[:, h, 1, :], start=True, stop=False)
                last = mm(o[:, P:T], v[1], hg_s[:, h, 2, :], start=False, stop=True)
            last.then_inc(*did(pe_groups, ("o", m)))
            release[4 + m] = ("og1", m)
        for m in range(4):
            take(m)
            pe.wait_ge(*when(("osq", m)))
            mm(bank[m][:, :], ones[:, :], sq[:, 2 * m:2 * m + 2, :].rearrange("p a n -> p (a n)"), start=True, stop=True).then_inc(*did(pe_groups, ("osum", m)))
            release[m] = ("oln", m)
        for j in range(4):
            columns(first["aout"] + j, 4 + j, xs, (lambda k: ("ol", k // 2)) if j == 0 else None, ("aout", j))
            release[4 + j] = ("x", 2, j)

        ffn(1, 3, 2)

        def ple(l, nu, v, s):
            c = first[f"ple{l}"]
            pe.wait_ge(sem["ple_landed"], 32)
            take(4)
            for k in range(2):
                for t in range(TB):
                    last = nc.tensor.transpose(bank[4][:, k * T + t * P:k * T + t * P + P], ptok[:, l, t, k * P:(k + 1) * P], ident)
            last.then_inc(*did(pe_groups, ("ptin", l)))
            release[4] = ("pt", l)
            pe.wait_ge(lo_ready, c + 1)
            pe.wait_ge(*when(("ptl", l)))
            w = split(c, (2, D))
            for m in range(4):
                take(m)
                for n in (2 * m, 2 * m + 1):
                    for k in range(2):
                        last = three(bank[m][:, (n % 2) * T:(n % 2 + 1) * T], [a[:, k, n * P:(n + 1) * P] for a in w],
                                     [pth[:, k, :], ptl[:, k, :]], k == 0, k == 1)
                last.then_inc(*did(pe_groups, ("pp", l, m)))
                release[m] = ("ppc", l, m)
            at[("chunk", c)] = at[("pp", l, 3)]
            for j in range(4):
                columns(c + 1 + j, 4 + j, xs, xwait(nu) if j == 0 else None, ("pgate", l, j))
                release[4 + j] = ("pg", l, j)
                if j == 0:
                    sums(s)
                    mod_sums(2 * l + 1)

        ple(0, 4, 3, 3)

        c = first["kvd"]
        columns(c, 4, xs, xwait(5), "kd0")
        release[4] = "ck"
        sums(4)
        take(5)
        pe.wait_ge(lo_ready, c + 2)
        w = split(c + 1, (KD, P))
        for k in range(KD):
            last = three(bank[5][:, 0:T], [a[:, k, :] for a in w], [a[:, k, :] for a in xs], k == 0, k == KD - 1)
        last.then_inc(*did(pe_groups, ("chunk", c + 1)))
        release[5] = "kr"
        take(6)
        pe.wait_ge(*when("cksq"))
        for k in range(2):
            last = mm(bank[6][:, 0:T], ones[:, :], sq[:, k, :], start=(k == 0), stop=(k == 1))
        last.then_inc(*did(pe_groups, "cksum"))
        release[6] = "ckstd"
        take(7)
        pe.wait_ge(*when("kr"))
        mm(bank[7][:, 0:T], const[:, C_PERM:C_PERM + P], kr[:, :], start=True, stop=True).then_inc(*did(pe_groups, "krswap"))
        release[7] = "kr_sin"

        ffn(2, 6, None)

        for j in range(2):
            columns(first["dq"] + j, 4 + j, xs, xwait(7) if j == 0 else None, ("dq", j))
            release[4 + j] = ("cq", j)
            if j == 0:
                sums(5)
                mod_sums(2)
        pe.wait_ge(*when("ckl"))
        for u in range(4):
            c = first["kvup"] + u
            pe.wait_ge(lo_ready, c + 1)
            w = split(c, (2, D))
            b0 = 4 * (u % 2)
            for n in range(2):
                take(b0 + n)
                for h in (2 * n, 2 * n + 1):
                    for k in range(2):
                        last = three(bank[b0 + n][:, (h % 2) * T:(h % 2 + 1) * T], [a[:, k, h * 256:h * 256 + P] for a in w],
                                     [ckh[:, k, :], ckl[:, k, :]], k == 0, k == 1)
                last.then_inc(*did(pe_groups, ("k", u, n)))
                release[b0 + n] = ("kn", u, n)
            for t in range(TB):
                take(b0 + 2 + t)
                for k in range(2):
                    vw = [a[:, k, :].rearrange("p (h e) -> p h e", h=4)[:, :, NOPE:NOPE + VDIM] for a in w]
                    last = three(bank[b0 + 2 + t][:, :], [a[:, k, t * P:(t + 1) * P] for a in (ckh, ckl)], vw, k == 0, k == 1)
                last.then_inc(*did(pe_groups, ("v", u, t)))
                release[b0 + 2 + t] = ("vb", u, t)
            at[("chunk", c)] = at[("v", u, 1)]
            if u == 0:
                take(4)
                for k in range(4):
                    pe.wait_ge(*when(("cqsq", k // 2)))
                    last = mm(bank[4][:, 0:T], ones[:, :], sq[:, k, :], start=(k == 0), stop=(k == 3))
                last.then_inc(*did(pe_groups, "cqsum"))
                release[4] = "cqstd"

        def swap(u):
            b = 4 + u % 2
            take(b)
            pe.wait_ge(*when(("qraw", u)))
            mm(bank[b][:, 0:T], const[:, C_PERM:C_PERM + P], qraw[:, u % 2, :], start=True, stop=True).then_inc(*did(pe_groups, ("qswap", u)))
            release[b] = ("q_sin", u)

        for u in range(8):
            c = first["uq"] + u
            pe.wait_ge(lo_ready, c + 1)
            w = split(c, (4, 384))
            b0 = 2 * (u % 2)
            take(b0)
            for h in range(2):
                for k in range(4):
                    if u == 0 and h == 0:
                        pe.wait_ge(*when(("cql", k)))
                    last = three(bank[b0][:, h * T:(h + 1) * T], [a[:, k, h * NOPE:(h + 1) * NOPE] for a in w],
                                 [cqh[:, k, :], cql[:, k, :]], k == 0, k == 3)
            last.then_inc(*did(pe_groups, ("qnope", u)))
            release[b0] = ("qn", u)
            take(b0 + 1)
            for k in range(4):
                last = three(bank[b0 + 1][:, 0:T], [a[:, k, 2 * NOPE:] for a in w], [cqh[:, k, :], cql[:, k, :]], k == 0, k == 3)
            last.then_inc(*did(pe_groups, ("chunk", c)))
            release[b0 + 1] = ("qraw", u)
            if u >= 1:
                swap(u - 1)
        swap(7)

        def transposes(item, p):
            for h in range(2):
                take(4 + h)
            pe.wait_ge(*when(("probs", item)))
            for h in range(2):
                for n, (src, dst) in enumerate(((0, 0), (1, 1), (2, 2))):
                    last = nc.tensor.transpose(bank[4 + h][:, dst * P:(dst + 1) * P], p[:, h, src * P:(src + 1) * P], ident)
                release[4 + h] = ("ptcopy", item)
            last.then_inc(*did(pe_groups, ("pt", item)))

        def scores_b(i):
            pe.wait_ge(*when(("qr", i)))
            b0 = 2 * (i % 2)
            for t in range(TB):
                b = b0 + t
                take(b)
                n = (t + 1) * P
                o = bank[b][:, 0:2 * n]
                mm(o, qr[:, i, t * P:(t + 1) * P], krz[:, :, 0:n], start=True, stop=False, skip_group_check=True)
                for h in range(2):
                    last = mm(o[:, h * n:(h + 1) * n], qn[:, 2 * i + h, t * P:(t + 1) * P], kn[:, 2 * i + h, 0:n],
                              start=False, stop=True, skip_group_check=True)
                last.then_inc(*did(pe_groups, ("s", ("b", i), t)))
                release[b] = ("s", "b", i, t)

        def values_b(i):
            pe.wait_ge(*when(("ptcopy", ("b", i))))
            b = 6 + i % 2
            take(b)
            for h in range(2):
                o = bank[b][:, h * T:(h + 1) * T]
                v = [vb[:, t, (2 * i + h) * VDIM:(2 * i + h + 1) * VDIM] for t in range(TB)]
                mm(o[:, 0:P], v[0], ptB[:, i % 2, h, 0:P], start=True, stop=True)
                mm(o[:, P:T], v[0], ptB[:, i % 2, h, P:T], start=True, stop=False)
                last = mm(o[:, P:T], v[1], ptB[:, i % 2, h, T:T + P], start=False, stop=True)
            last.then_inc(*did(pe_groups, ("ob", i)))
            release[b] = ("ol", "b", i)

        scores_b(0)
        scores_b(1)
        for i in range(8):
            if i < 6:
                scores_b(i + 2)
            if i >= 1:
                values_b(i - 1)
            transposes(("b", i), sB[:, i % 3])
        values_b(7)
        c0 = first["bout"]
        for b in range(4):
            take(b)
        for q in range(8):
            pe.wait_ge(lo_ready, c0 + q + 1)
            pe.wait_ge(*when(("ol", "b", q)))
            w = split(c0 + q, (2, D))
            for n in range(KD):
                for k in range(2):
                    last = three(bank[n // 2][:, (n % 2) * T:(n % 2 + 1) * T], [a[:, k, n * P:(n + 1) * P] for a in w],
                                 [oh[:, 2 * q + k, :], ol[:, 2 * q + k, :]], q == 0 and n % 2 == 0 and k == 0, q == 7 and k == 1, True)
                if q == 7 and n % 2:
                    last.then_inc(*did(pe_groups, ("bout", n // 2)))
            if q < 7:
                last.then_inc(*did(pe_groups, ("chunk", c0 + q)))
        at[("chunk", c0 + 7)] = at[("bout", 3)]
        for m in range(4):
            release[m] = ("x", 6, m)

        ffn(3, 8, 6)
        ple(1, 9, 7, 7)
        sums(8)

        for l in range(2):
            nu, v, s = 10 + 2 * l, 9 + l, 9 + 2 * l
            sums(s)
            c0 = first[f"win{l}"]
            for n, (name, j) in enumerate(WIN):
                c, b = c0 + n, n % 8
                key = ("win", l, n)
                if name in ("qm", "km", "qn", "zm", "zn"):
                    columns(c, b, xs, xwait(nu) if n == 0 else None, key)
                    release[b] = ("z", l, n) if name[0] == "z" else ("proj", l, n)
                elif name == "vm":
                    tokens(c, b, xs, key, slice(0, 256))
                    release[b] = ("proj", l, n)
                elif name == "gl":
                    tokens(c, b, xs, key, slice(0, 24), width=24)
                    release[b] = ("gates", l)
                elif name == "kcvc":
                    columns(c, b, xs, None, key)
                    release[b] = ("proj", l, n)
                else:
                    take(b)
                    pe.wait_ge(lo_ready, c + 1)
                    w = split(c, (KD, 256))
                    for k in range(KD):
                        three(bank[b][:, 0:T], [a[:, k, 0:P] for a in w], [a[:, k, :] for a in xs], k == 0, k == KD - 1)
                    for t in range(TB):
                        for k in range(KD):
                            last = three(bank[b][:, T + t * P:T + (t + 1) * P], [a[:, k, t * P:(t + 1) * P] for a in xs],
                                         [a[:, k, P:2 * P] for a in w], k == 0, k == KD - 1)
                    last.then_inc(*did(pe_groups, key))
                    at[("chunk", c)] = at[key]
                    release[b] = ("proj", l, n)
                if name in ("ksvs", "gl"):
                    half_ = 0 if name == "ksvs" else 1
                    take(half_)
                    pe.wait_ge(*when(("kA", l, half_)))
                    mm(bank[half_][:, :], const[:, C_SWAP:C_SWAP + P], kA[:, 2 * half_:2 * half_ + 2, :].rearrange("p a n -> p (a n)"),
                       start=True, stop=True).then_inc(*did(pe_groups, ("kB", l, half_)))
                    release[half_] = ("kB_used", l, half_)
            take(0)
            pe.wait_ge(sem["cmp_landed"], 80 * (l + 1))
            for kv in range(2):
                pe.wait_ge(*when(("windows", l, kv)))
                for r in range(16):
                    last = mm(bank[0][0:DH, 30 * kv:30 * kv + 30], wc1[:, kv, r, :], win[:, kv, r, :], start=(r == 0), stop=(r == 15))
            last.then_inc(*did(pe_groups, ("hid", l)))
            release[0] = ("gelu", l)
            take(1)
            pe.wait_ge(*when(("gelu", l)))
            mm(bank[1][:, 0:30], wc2[:, 0:2, :].rearrange("p a n -> p (a n)"), gh[:, 0:30], start=True, stop=True).then_inc(*did(pe_groups, ("kcmp", l)))
            release[1] = ("kcz", l)
            take(2)
            for g in range(GROUPS):
                last = mm(bank[2][0:CMP_T, g * DH:(g + 1) * DH], gh[:, 30 + 15 * g:45 + 15 * g], wc2[:, 2, :], start=True, stop=True)
            last.then_inc(*did(pe_groups, ("vcmp", l)))
            release[2] = ("vcz", l)

            def scores_c(i):
                kind, m, _, _ = ITEMS[i]
                g = m // 2
                q = qm if kind == "moba" else qs
                b0 = 2 * (i % 2)
                if i == 0:
                    pe.wait_ge(*when(("attn", l)))
                    pe.wait_ge(*when(("z", l, 15)))
                if kind == "cmp":
                    take(b0)
                    for t in range(TB):
                        last = mm(bank[b0][:, t * 2 * CMP_T:(t + 1) * 2 * CMP_T], q[:, m, t * P:(t + 1) * P], kcz[:, g, :, 0:CMP_T], start=True, stop=True)
                    last.then_inc(*did(pe_groups, ("s", ("c", l, i), 1)))
                    release[b0] = ("s", "c", l, i, 1)
                    return
                kz = {"moba": kmz[:, m], "slc": ksz[:, g], "win": kwz[:, g]}[kind]
                for t in range(TB):
                    b, n = b0 + t, (t + 1) * P
                    take(b)
                    mm(bank[b][:, 0:2 * n], q[:, m, t * P:(t + 1) * P], kz[:, :, 0:n], start=True, stop=True).then_inc(*did(pe_groups, ("s", ("c", l, i), t)))
                    release[b] = ("s", "c", l, i, t)

            def transposes_c(i):
                if ITEMS[i][0] != "cmp":
                    return transposes(("c", l, i), sC[:, i % 3])
                for h in range(2):
                    take(4 + h)
                pe.wait_ge(*when(("probs", ("c", l, i))))
                for h in range(2):
                    for t in range(TB):
                        last = nc.tensor.transpose(bank[4 + h][0:16, t * P:(t + 1) * P], sC[:, i % 3, h, 16 * t:16 * t + 16], ident)
                    release[4 + h] = ("ptcopy", ("c", l, i))
                last.then_inc(*did(pe_groups, ("pt", ("c", l, i))))

            def values_c(i):
                kind, m, start, stop = ITEMS[i]
                g = m // 2
                k = m if kind == "moba" else 4 + m
                b = 6 + k % 2
                pe.wait_ge(*when(("ptcopy", ("c", l, i))))
                if start:
                    take(b)
                o = bank[b][:, 0:T]
                for h in range(2):
                    if kind == "cmp":
                        last = mm(o, vcz[0:CMP_T, g, h, :], ptC[0:CMP_T, i % 2, h, 0:T], start=False, stop=(h == 1), skip_group_check=True)
                        continue
                    v = {"moba": [vmz[:, t, 2 * m + h, :] for t in range(TB)],
                         "slc": [vsz[:, t, g, h, :] for t in range(TB)], "win": [vwz[:, t, g, h, :] for t in range(TB)]}[kind]
                    block0 = lambda: mm(o, v[0], ptC[:, i % 2, h, 0:T], start=(start and h == 0), stop=(stop and h == 1), skip_group_check=True)
                    block1 = lambda: mm(o[:, P:T], v[1], ptC[:, i % 2, h, T:T + P], start=False, stop=False, skip_group_check=True)
                    for product in ((block0, block1) if h == 0 else (block1, block0)):
                        last = product()
                last.then_inc(*did(pe_groups, ("oc", l, i)))
                if stop:
                    release[b] = ("y", l, k)

            scores_c(0)
            scores_c(1)
            for i in range(len(ITEMS)):
                if i + 2 < len(ITEMS):
                    scores_c(i + 2)
                if i >= 1:
                    values_c(i - 1)
                transposes_c(i)
            values_c(len(ITEMS) - 1)
            for j in range(4):
                columns(first[f"wout{l}"] + j, j, xs, (lambda k: ("yl", l, k)) if j == 0 else None, ("wout", l, j))
                release[j] = ("y2", l, j)
            sums(s + 1)
        for t in range(TB):
            for m in range(2):
                take(2 * t + m)
                for n in range(4):
                    k = 4 * m + n
                    pe.wait_ge(*when(("x", 11, k // 2)))
                    last = nc.tensor.transpose(bank[2 * t + m][:, n * P:(n + 1) * P], X[:, k, t * P:(t + 1) * P], ident)
                last.then_inc(*did(pe_groups, ("xout", t, m)))

    @block.vector
    def _(dve):
        did = Steps(at)
        V = nc.vector

        def lo(c, it=None):
            if c >= n_chunks:
                return
            dve.wait_ge(hi_ready, c + 1 + (0 if it is None else 4 * it))
            V.tensor_tensor(w_lo[:, c % NSLOT, :], w_raw[:, c % NRAW, :], f32(w_hi[:, c % NSLOT, :]), ALU.subtract).then_inc(*did(lo_ready))

        def norm(nu, gain):
            for k in range(KD):
                dve.wait_ge(*when(("xh", nu, k)))
                V.scalar_tensor_tensor(xl[:, k, :], X[:, k, :], gain(k), f32(xh[:, k, :]), ALU.mult, ALU.subtract).then_inc(*did(dve_steps, ("xl", nu, k)))

        def inv(s):
            dve.wait_ge(*when(("std", s)))
            dve.wait_ge(*did.last)
            V.reciprocal(rs[:, :], std[:, :]).then_inc(*did(dve_steps, ("rs", s)))
            dve.wait_ge(*did.last)

        def modulation(f):
            dve.wait_ge(*when(("modsum", f)))
            n = slice(2 * MOD * f, 2 * MOD * (f + 1))
            V.tensor_tensor(mods[:, :, :].rearrange("p l n -> p (l n)")[:, n], bank[2][:, 0:2 * MOD], col1[:, n], ALU.add).then_inc(*did(dve_steps, ("mod", f)))

        def ffn(f, nu, v, gain, s):
            norm(nu, gain)
            c = first[f"in{f}"]
            n0 = PAIRS * f
            group0 = when(("gate", f))[1]
            up0 = when(("up", f))[1]

            def pair(c, p, it=None):
                o = 0 if it is None else 2 * it
                o4 = 0 if it is None else 4 * it
                b = 2 * (p % 2)
                lo(c + AHEAD, it)
                if it is None and s is not None:
                    inv(s)
                dve.wait_ge(pe_groups, (group0 if p == 0 else up0 + 2 * p - 1) + o4)
                if it is not None or p >= 2:
                    dve.wait_ge(silu_ready, n0 + max(p - 1, 1) + o)
                V.tensor_tensor(gate_t[:, p % 2, :, :], two(bank[b][:, :]), rep(rs[:, :], 2), ALU.mult).then_inc(*did(gate_scaled))
                lo(c + 1 + AHEAD, it)
                dve.wait_ge(pe_groups, up0 + 2 * p + o4)
                if it is not None or p >= 2:
                    dve.wait_ge(hidden_ready, n0 + max(p - 1, 1) + o)
                V.tensor_tensor(up_t[:, p % 2, :, :], two(bank[b + 1][:, :]), rep(rs[:, :], 2), ALU.mult).then_inc(*did(up_scaled))
                dve.wait_ge(silu_ready, n0 + p + 1 + o)
                dve.wait_ge(up_scaled, n0 + p + 1 + o)
                if it is not None or p >= 2:
                    dve.wait_ge(hidden_hi, n0 + max(p - 1, 1) + o)
                    dve.wait_ge(hidden_lo, n0 + max(p - 1, 1) + o)
                V.tensor_tensor(hid_t[:, p % 2, :, :], silu_t[:, p % 2, :, :], up_t[:, p % 2, :, :], ALU.mult).then_inc(*did(hidden_ready))
                dve.wait_ge(hidden_hi, n0 + p + 1 + o)
                k = bass.ds(2 * p + (0 if it is None else 4 * it), 2)
                V.tensor_tensor(hl[:, k, :], hid_t[:, p % 2, :, :], f32(hh[:, k, :]), ALU.subtract).then_inc(*did(hidden_lo))

            pair(c, 0)
            with dve.Fori(0, (PAIRS - 1) // 2) as it:
                for j in range(2):
                    pair(c + 2 + 2 * j, 1 + j, it)
            turns_left = (PAIRS - 1) // 2 - 1
            did.skip(lo_ready, 4 * turns_left)
            for q in (gate_scaled, up_scaled, hidden_ready, hidden_lo):
                did.skip(q, 2 * turns_left)
            for p in (PAIRS - 2, PAIRS - 1):
                at[("ffn_g", f, p)], at[("ffn_u", f, p)] = ("gate_scaled", n0 + p + 1), ("up_scaled", n0 + p + 1)
            c = first[f"out{f}"]
            for q in range(2):
                lo(c + q + AHEAD)
            with dve.Fori(0, 2) as it:
                for q in range(4):
                    lo(c + 2 + q + AHEAD, it)
            did.skip(lo_ready, 4)
            lo(c + 10 + AHEAD)
            for m in range(4):
                dve.wait_ge(*when(("ffn_out", f, m)))
                V.scalar_tensor_tensor(X[:, 2 * m:2 * m + 2, :], two(bank[4 + m][:, :]), 0.5, X[:, 2 * m:2 * m + 2, :], ALU.mult, ALU.add).then_inc(*did(dve_steps, ("x", v + 1, m)))

        dve.wait_ge(sem["setup_landed"], 16 * 15)
        V.tensor_copy(turns[0:1, :], pos_i[0:1, :]).then_inc(*did(dve_steps, "pos_f"))
        for m in range(4):
            dve.wait_ge(*when(("xin", m)))
            V.tensor_copy(X[:, 2 * m:2 * m + 2, :], two(bank[m][:, :])).then_inc(*did(dve_steps, ("x", 0, m)))
        for n, (col, cnt) in enumerate(((col0, 103), (col1, 88), (col2, 64))):
            dve.wait_ge(*when(("cols", n)))
            V.tensor_copy(col[:, 0:cnt], bank[4 + n][:, 0:cnt]).then_inc(*did(dve_steps, ("col", n)))
        dve.wait_ge(*did.last)
        V.tensor_max(small[:, 32:40], col0[:, 64:72], col0[:, 72:80]).then_inc(*did(dve_steps))
        dve.wait_ge(*did.last)
        V.tensor_tensor(two(small[:, 0:16]), two(col0[:, 64:80]), rep(small[:, 32:40], 2), ALU.subtract).then_inc(*did(dve_steps, "lb_shift"))
        for c in range(AHEAD):
            lo(c)
        dve.wait_ge(*when("lb_exp"))
        V.tensor_tensor(small[:, 32:40], small[:, 16:24], small[:, 24:32], ALU.add).then_inc(*did(dve_steps))
        dve.wait_ge(*did.last)
        V.reciprocal(small[:, 40:48], small[:, 32:40]).then_inc(*did(dve_steps))
        dve.wait_ge(*did.last)
        V.tensor_tensor(lb[:, :], small[:, 16:24], small[:, 40:48], ALU.mult).then_inc(*did(dve_steps))
        dve.wait_ge(*did.last)
        V.tensor_scalar(oml[:, :], lb[:, :], -1.0, 1.0, ALU.mult, ALU.add).then_inc(*did(dve_steps, "lb"))
        dve.wait_ge(*when("pos"))
        V.tensor_scalar(ang[:, :], bank[7][:, 0:T], const[:, C_FREQ:C_FREQ + 1], None, ALU.mult).then_inc(*did(dve_steps, "ang0"))
        dve.wait_ge(*did.last)
        V.tensor_scalar(turns[:, :], ang[:, :], float(1 / (2 * np.pi)), None, ALU.mult).then_inc(*did(dve_steps))
        big = float(1.5 * 2 ** 23)
        for step in (big, -big):
            dve.wait_ge(*did.last)
            V.tensor_scalar(turns[:, :], turns[:, :], step, None, ALU.add).then_inc(*did(dve_steps))
        part1 = 6.28125
        part2 = float(np.float32(np.round((2 * np.pi - part1) * 2 ** 20) / 2 ** 20))
        part3 = float(np.float32(2 * np.pi - part1 - part2))
        src = ang
        for part in (part1, part2, part3):
            dve.wait_ge(*did.last)
            V.scalar_tensor_tensor(red[:, :], turns[:, :], -part, src[:, :], ALU.mult, ALU.add).then_inc(*did(dve_steps))
            src = red
        dve.wait_ge(*did.last)
        V.tensor_scalar(red[:, :], red[:, :], 3.1415925, -3.1415925, ALU.min, ALU.max).then_inc(*did(dve_steps, "angles"))
        dve.wait_ge(*did.last)
        V.tensor_scalar(mag[:, :], red[:, :], -1.0, None, ALU.mult).then_inc(*did(dve_steps))
        dve.wait_ge(*did.last)
        V.tensor_tensor(mag[:, :], mag[:, :], red[:, :], ALU.max).then_inc(*did(dve_steps))
        dve.wait_ge(*did.last)
        V.tensor_scalar(mag[:, :], mag[:, :], -1.0, float(np.pi / 2), ALU.mult, ALU.add).then_inc(*did(dve_steps, "quarter"))
        dve.wait_ge(*when("sin"))
        V.tensor_scalar(sin[:, :], sin[:, :], const[:, C_SIGN:C_SIGN + 1], None, ALU.mult).then_inc(*did(dve_steps, "rope"))

        ffn(0, 0, 0, g_norm(0, 0), 0)

        c0 = first["hgrn"]
        norm(1, g_norm(0, 1))
        for j in range(4):
            lo(c0 + j + AHEAD)
            if j == 0:
                inv(1)
            dve.wait_ge(*when(("pf", j)))
            if j == 1:
                modulation(0)
            V.tensor_tensor(hg_a[:, 2 * j:2 * j + 2, :], two(bank[4 + j][:, :]), rep(rs[:, :], 2), ALU.mult).then_inc(*did(dve_steps, ("f", j)))
        for j in range(4):
            lo(c0 + 4 + j + AHEAD)
            dve.wait_ge(*when(("pq", j)))
            V.scalar_tensor_tensor(hg_q[:, 2 * j:2 * j + 2, :], two(bank[4 + j][:, :]), float(P ** -0.5), rep(rs[:, :], 2), ALU.mult, ALU.mult).then_inc(*did(dve_steps, ("q", j)))
            dve.wait_ge(*when(("sg", j)))
            for h in (2 * j, 2 * j + 1):
                V.tensor_scalar(hg_k[:, h, :], hg_k[:, h, :], oml[:, h:h + 1], None, ALU.mult).then_inc(*did(dve_steps, "k"))
        for h in range(HEADS_A):
            dve.wait_ge(*when(("ln", h)))
            V.tensor_tensor_scan(hg_b[:, h, :], const[:, C_RESET:C_RESET + T], hg_a[:, h, :], 0.0, ALU.mult, ALU.add).then_inc(*did(dve_steps, "scans"))
        dve.wait_ge(*when("rst"))
        V.tensor_copy(rst[:, :], two(bank[3][:, 0:T])[:, :, 0:1].rearrange("p a n -> p (a n)")).then_inc(*did(dve_steps, "rst_copy"))
        dve.wait_ge(*did.last)

        def halves(t, L):
            r = t[:, :, :].rearrange("p h n -> p (h n)").rearrange("p (b two n) -> p b two n", two=2, n=L)
            return r[:, :, 0, :], r[:, :, 1, :]

        def factors(n):
            L = LEVELS[n] if n < 7 else P
            f = hg_f[n % 2]
            kl, _ = halves(hg_k, L)
            _, qr_ = halves(hg_q, L)
            fl, fr = halves(f, L)
            dve.wait_ge(*when(("exp", n)))
            V.tensor_tensor(fl, fl, kl, ALU.mult).then_inc(*did(dve_steps))
            V.tensor_tensor(fr, fr, qr_, ALU.mult).then_inc(*did(dve_steps, ("factors", n)))

        def diag_view(m):
            return hg_s[:, 2 * m:2 * m + 2, 0:3:2, :]

        for m in range(4):
            dve.wait_ge(*when(("diag", m)))
            V.tensor_tensor(diag_view(m), bank[m][:, :].rearrange("p (h t n) -> p h t n", h=2, t=2),
                            rep(rep(ident, 2), 2), ALU.mult).then_inc(*did(dve_steps, ("diag_in", m)))
        factors(0)

        def merge(n):
            mask = const[:, C_LVL + n * P:C_LVL + (n + 1) * P].bitcast(U32)
            for m in range(4):
                dve.wait_ge(*when((("lev", n), m)))
                dve.wait_ge(*did.last)
                V.copy_predicated(diag_view(m), rep(rep(mask, 2), 2), bank[m][:, :].rearrange("p (h t n) -> p h t n", h=2, t=2)).then_inc(*did(dve_steps, (("merge", n), m)))

        for n in range(8):
            j = n % 4
            lo(c0 + 8 + n + AHEAD)
            if n < 4:
                dve.wait_ge(*when(("pi", j)))
                for t in range(TB):
                    V.tensor_scalar(hg_v[:, t, 256 * j:256 * j + 256], bank[4 + j][:, t * T:(t + 1) * T], rst[:, t:t + 1], None, ALU.mult).then_inc(*did(dve_steps, ("vi", j)))
            else:
                dve.wait_ge(*when(("pg", j)))
                V.tensor_tensor(hg_g[:, 2 * j:2 * j + 2, :], two(bank[4 + j][:, :]), rep(rs[:, :], 2), ALU.mult).then_inc(*did(dve_steps, ("g", j)))
            if n < 7:
                merge(n)
                factors(n + 1)
        for m in range(2):
            dve.wait_ge(*when(("cross", m)))
            V.tensor_copy(hg_s[:, 4 * m:4 * m + 4, 1, :], bank[m][:, :].rearrange("p (h n) -> p h n", h=4)).then_inc(*did(dve_steps, ("cross_in", m)))
        dve.wait_ge(*when("gate_sg"))
        for m in range(4):
            pair_ = slice(2 * m, 2 * m + 2)
            dve.wait_ge(*when(("osq", m)))
            V.scalar_tensor_tensor(hg_b[:, pair_, :], two(bank[4 + m][:, :]), out_gain, hg_g[:, pair_, :], ALU.mult, ALU.mult).then_inc(*did(dve_steps, ("og1", m)))
        for m in range(4):
            pair_ = slice(2 * m, 2 * m + 2)
            dve.wait_ge(*when(("ors", m)))
            dve.wait_ge(*when(("og1", m)))
            V.tensor_tensor(hg_b[:, pair_, :], hg_b[:, pair_, :], hg_a[:, pair_, :], ALU.mult).then_inc(*did(dve_steps, ("og", m)))
        for m in range(4):
            pair_ = slice(2 * m, 2 * m + 2)
            dve.wait_ge(*when(("oh", m)))
            V.tensor_tensor(xl[:, pair_, :], hg_b[:, pair_, :], f32(xh[:, pair_, :]), ALU.subtract).then_inc(*did(dve_steps, ("ol", m)))

        def add_x(v, name, b0):
            for j in range(4):
                yield j
                dve.wait_ge(*when(name + (j,)))
                V.tensor_tensor(X[:, 2 * j:2 * j + 2, :], X[:, 2 * j:2 * j + 2, :], two(bank[b0 + j][:, :]), ALU.add).then_inc(*did(dve_steps, ("x", v, j)))

        for j in add_x(2, ("aout",), 4):
            lo(first["aout"] + j + AHEAD)

        ffn(1, 3, 2, g_norm(0, 2), 2)

        def ple(l, nu, v, s):
            c = first[f"ple{l}"]
            lo(c + AHEAD)
            dve.wait_ge(*when(("ptin", l)))
            V.tensor_copy(pt[:, :, :], two(bank[4][:, :])).then_inc(*did(dve_steps, ("pt", l)))
            dve.wait_ge(*when(("pth", l)))
            V.tensor_tensor(ptl[:, :, :], pt[:, :, :], f32(pth[:, :, :]), ALU.subtract).then_inc(*did(dve_steps, ("ptl", l)))
            norm(nu, g_norm(l, 3))
            for m in range(4):
                dve.wait_ge(*when(("pp", l, m)))
                V.tensor_copy(pp[:, 2 * m:2 * m + 2, :], two(bank[m][:, :])).then_inc(*did(dve_steps, ("ppc", l, m)))

            def finish(j):
                pair_ = slice(2 * j, 2 * j + 2)
                dve.wait_ge(*when(("pgs", l, j)))
                V.tensor_tensor(pg[:, pair_, :], pg[:, pair_, :], pp[:, pair_, :], ALU.mult).then_inc(*did(dve_steps))
                dve.wait_ge(*did.last)
                V.tensor_tensor(X[:, pair_, :], X[:, pair_, :], pg[:, pair_, :], ALU.add).then_inc(*did(dve_steps, ("x", v + 1, j)))

            for j in range(4):
                lo(c + 1 + j + AHEAD)
                if j == 0:
                    inv(s)
                dve.wait_ge(*when(("pgate", l, j)))
                if j == 1:
                    modulation(2 * l + 1)
                V.tensor_tensor(pg[:, 2 * j:2 * j + 2, :], two(bank[4 + j][:, :]), rep(rs[:, :], 2), ALU.mult).then_inc(*did(dve_steps, ("pg", l, j)))
                finish(j)

        ple(0, 4, 3, 3)

        norm(5, g_kv)
        lo(first["kvd"] + AHEAD)
        inv(4)
        dve.wait_ge(*when("kd0"))
        V.tensor_tensor(ck[:, :, :], two(bank[4][:, :]), rep(rs[:, :], 2), ALU.mult).then_inc(*did(dve_steps, "ck"))
        lo(first["kvd"] + 1 + AHEAD)
        dve.wait_ge(*when(("chunk", first["kvd"] + 1)))
        V.tensor_tensor(kr[:, :], bank[5][:, 0:T], rs[:, :], ALU.mult).then_inc(*did(dve_steps, "kr"))
        dve.wait_ge(*did.last)
        V.tensor_tensor(kr_t[:, 0, :], kr[:, :], cos[:, :], ALU.mult).then_inc(*did(dve_steps))
        dve.wait_ge(*when("ckstd"))
        V.reciprocal(rs2_kv[:, :], std2_kv[:, :]).then_inc(*did(dve_steps))
        dve.wait_ge(*did.last)
        for k in range(2):
            V.scalar_tensor_tensor(ck[:, k, :], ck[:, k, :], g_latent(k), rs2_kv[:, :], ALU.mult, ALU.mult).then_inc(*did(dve_steps, "ckn"))
        dve.wait_ge(*when("krswap"))
        V.tensor_tensor(kr_t[:, 1, :], bank[7][:, 0:T], sin[:, :], ALU.mult).then_inc(*did(dve_steps, "kr_sin"))
        dve.wait_ge(*did.last)
        for h in range(2):
            rows_ = slice(h * ROPE, (h + 1) * ROPE)
            V.tensor_tensor(krz[rows_, h, :], kr_t[rows_, 0, :], kr_t[rows_, 1, :], ALU.add).then_inc(*did(dve_steps))
        dve.wait_ge(*when("ckh"))
        V.tensor_tensor(ckl[:, :, :], ck[:, :, :], f32(ckh[:, :, :]), ALU.subtract).then_inc(*did(dve_steps, "ckl"))

        ffn(2, 6, 4, g_norm(1, 0), None)

        norm(7, g_norm(1, 1))
        for j in range(2):
            lo(first["dq"] + j + AHEAD)
            if j == 0:
                inv(5)
            dve.wait_ge(*when(("dq", j)))
            if j == 1:
                modulation(2)
            V.tensor_tensor(cq[:, 2 * j:2 * j + 2, :], two(bank[4 + j][:, :]), rep(rs[:, :], 2), ALU.mult).then_inc(*did(dve_steps, ("cq", j)))
        for u in range(4):
            lo(first["kvup"] + u + AHEAD)
            for n in range(2):
                dve.wait_ge(*when(("k", u, n)))
                V.tensor_copy(kn[:, 4 * u + 2 * n:4 * u + 2 * n + 2, :], two(bank[4 * (u % 2) + n][:, :])).then_inc(*did(dve_steps, ("kn", u, n)))
            if u == 0:
                dve.wait_ge(*when("cqstd"))
                V.reciprocal(rs2[:, :], std2[:, :]).then_inc(*did(dve_steps))
                dve.wait_ge(*did.last)
                for k in range(4):
                    V.scalar_tensor_tensor(cq[:, k, :], cq[:, k, :], g_q(k), rs2[:, :], ALU.mult, ALU.mult).then_inc(*did(dve_steps, ("cqn", k)))
        for k in range(4):
            dve.wait_ge(*when(("cqh", k)))
            V.tensor_tensor(cql[:, k, :], cq[:, k, :], f32(cqh[:, k, :]), ALU.subtract).then_inc(*did(dve_steps, ("cql", k)))

        def rotate(u):
            dve.wait_ge(*when(("qswap", u)))
            dve.wait_ge(*did.last)
            V.tensor_tensor(qr_t[:, 1, :], bank[4 + u % 2][:, 0:T], sin[:, :], ALU.mult).then_inc(*did(dve_steps, ("q_sin", u)))
            V.tensor_tensor(qr_t[:, 0, :], qraw[:, u % 2, :], cos[:, :], ALU.mult).then_inc(*did(dve_steps))
            dve.wait_ge(*did.last)
            V.tensor_tensor(qr[:, u, :], qr_t[:, 0, :], qr_t[:, 1, :], ALU.add).then_inc(*did(dve_steps, ("qr", u)))

        for u in range(8):
            if u + AHEAD < 8:
                lo(first["uq"] + u + AHEAD)
            dve.wait_ge(*when(("qnope", u)))
            V.tensor_copy(qn[:, 2 * u:2 * u + 2, :], two(bank[2 * (u % 2)][:, :])).then_inc(*did(dve_steps, ("qn", u)))
            dve.wait_ge(*when(("chunk", first["uq"] + u)))
            if u >= 2:
                dve.wait_ge(*when(("qr", u - 2)))
            V.tensor_copy(qraw[:, u % 2, :], bank[2 * (u % 2) + 1][:, 0:T]).then_inc(*did(dve_steps, ("qraw", u)))
            if u >= 1:
                rotate(u - 1)
        rotate(7)

        def maxima(item, s, nm):
            dve.wait_ge(*did.last)
            for t in range(TB):
                cols = slice(0, P) if t == 0 else slice(P, 3 * P)
                V.tensor_reduce(nm[:, 2 * t:2 * t + 2], s[:, :, cols], AX.X, ALU.max, negate=True).then_inc(*did(dve_steps, ("max", item)))

        def masked_b(i):
            s = sB[:, i % 3]
            caus = const[:, C_CAUS:C_CAUS + P]
            dve.wait_ge(*when(("s", ("b", i), 0)))
            if i >= 3:
                dve.wait_ge(*when(("pt", ("b", i - 3))))
            dve.wait_ge(*did.last)
            V.scalar_tensor_tensor(s[:, :, 0:P], two(bank[2 * (i % 2)][:, 0:2 * P]), SCALE_B, rep(caus, 2), ALU.mult, ALU.add).then_inc(*did(dve_steps, ("s", "b", i, 0)))
            dve.wait_ge(*when(("s", ("b", i), 1)))
            b1 = two(bank[2 * (i % 2) + 1][:, :])
            V.scalar_tensor_tensor(s[:, :, 2 * P:3 * P], b1[:, :, P:T], SCALE_B, rep(caus, 2), ALU.mult, ALU.add).then_inc(*did(dve_steps))
            V.tensor_scalar(s[:, :, P:2 * P], b1[:, :, 0:P], SCALE_B, None, ALU.mult).then_inc(*did(dve_steps, ("s", "b", i, 1)))
            maxima(("b", i), s, nmB[:, i % 3])

        def weigh(item, s, den, rd, gate=None, valid=False, width=None):
            dve.wait_ge(*when(("exps", item)))
            dve.wait_ge(*did.last)
            V.reciprocal(rd[:, :], den[:, :]).then_inc(*did(dve_steps))
            if valid:
                dve.wait_ge(*did.last)
                V.tensor_tensor(two(rd[:, :]), two(rd[:, :]), const[:, C_ROWV:C_ROWV + 2].unsqueeze(2).to_broadcast([P, 2, 2]), ALU.mult).then_inc(*did(dve_steps))
            if gate is not None:
                dve.wait_ge(*did.last)
                V.tensor_tensor(two(rd[:, :]), two(rd[:, :]), gate, ALU.mult).then_inc(*did(dve_steps))
            dve.wait_ge(*did.last)
            for h in range(2):
                for t in range(TB):
                    cols = (slice(0, P) if t == 0 else slice(P, 3 * P)) if width is None else slice(16 * t, 16 * t + width)
                    V.tensor_scalar(s[:, h, cols], s[:, h, cols], rd[:, 2 * t + h:2 * t + h + 1], None, ALU.mult).then_inc(*did(dve_steps, ("probs", item)))

        def out_b(i):
            dve.wait_ge(*when(("oh", "b", i)))
            V.tensor_tensor(ol[:, 2 * i:2 * i + 2, :], two(bank[6 + i % 2][:, :]), f32(oh[:, 2 * i:2 * i + 2, :]), ALU.subtract).then_inc(*did(dve_steps, ("ol", "b", i)))

        masked_b(0)
        masked_b(1)
        for i in range(8):
            weigh(("b", i), sB[:, i % 3], denB[:, i % 3], rdB[:, i % 3])
            if i >= 2:
                out_b(i - 2)
            if i < 6:
                masked_b(i + 2)
            if i >= 6:
                lo(first["bout"] + i - 6)
        for i in (6, 7):
            out_b(i)
        lo(first["bout"] + 2)
        for j in range(8):
            lo(first["bout"] + j + AHEAD)
        for m in range(4):
            dve.wait_ge(*when(("bout", m)))
            V.tensor_tensor(X[:, 2 * m:2 * m + 2, :], X[:, 2 * m:2 * m + 2, :], two(bank[m][:, :]), ALU.add).then_inc(*did(dve_steps, ("x", 6, m)))

        ffn(3, 8, 6, g_norm(1, 2), 6)
        ple(1, 9, 7, 7)
        inv(8)
        for k in range(KD):
            V.scalar_tensor_tensor(X[:, k, :], X[:, k, :], g_final(k), rs[:, :], ALU.mult, ALU.mult).then_inc(*did(dve_steps, ("x", 9, k // 2)))

        for l in range(2):
            nu, v, s = 10 + 2 * l, 9 + l, 9 + 2 * l
            inv(s)
            V.scalar_tensor_tensor(gpre[:, :], mods[:, l, 8:16], 1.0, col1[:, 48 + 8 * l:56 + 8 * l], ALU.add, ALU.mult).then_inc(*did(dve_steps))
            V.tensor_tensor(gpost[:, :], mods[:, l, 16:24], col1[:, 64 + 8 * l:72 + 8 * l], ALU.mult).then_inc(*did(dve_steps))
            dve.wait_ge(*did.last)
            dve.wait_ge(*when(("sums", s)))
            for k in range(KD):
                V.scalar_tensor_tensor(sq[:, k, :], X[:, k, :], gpre[:, k:k + 1], rs[:, :], ALU.mult, ALU.mult).then_inc(*did(dve_steps, ("xn", l, k)))
            for k in range(KD):
                dve.wait_ge(*when(("xh", nu, k)))
                V.scalar_tensor_tensor(xl[:, k, :], sq[:, k, :], mods[:, l, k:k + 1], f32(xh[:, k, :]), ALU.add, ALU.subtract).then_inc(*did(dve_steps, ("xl", nu, k)))
            dve.wait_ge(*did.last)
            dve.wait_ge(*when(("zeros", l)))
            def slope(h):
                return float(2.0 ** (-8.0 * (h + 1) / HEADS_C))
            for h in range(HEADS_C):
                V.scalar_tensor_tensor(bias[:, h, :], const[:, C_DIST:C_DIST + T], -slope(h), const[:, C_DMASK:C_DMASK + T], ALU.mult, ALU.add).then_inc(*did(dve_steps))
                V.scalar_tensor_tensor(cbias[:, h, :, :].rearrange("p a n -> p (a n)"), const[:, C_CMPD:C_CMPD + 2 * CMP_T], -slope(h),
                                       const[:, C_CMPM:C_CMPM + 2 * CMP_T], ALU.mult, ALU.add).then_inc(*did(dve_steps))
            c0 = first[f"win{l}"]

            def zero_padded(dst, src, key):
                for h in range(2):
                    rows_ = slice(h * DH, (h + 1) * DH)
                    V.tensor_copy(dst[rows_, :, h, :], src[rows_, :, :]).then_inc(*did(dve_steps, key))

            for n, (name, j) in enumerate(WIN):
                if n + AHEAD < 16:
                    lo(c0 + n + AHEAD)
                b = n % 8
                key, done = ("win", l, n), ("proj", l, n)
                src = two(bank[b][:, :])
                if name in ("qm", "qn"):
                    dve.wait_ge(*when(key))
                    q = qm if name == "qm" else qs
                    V.tensor_scalar(q[:, 2 * j:2 * j + 2, :], src, float(DH ** -0.5), None, ALU.mult).then_inc(*did(dve_steps, done))
                elif name == "km":
                    dve.wait_ge(*when(key))
                    zero_padded(kmz[:, 2 * j:2 * j + 2, :, :], src, done)
                elif name == "vm":
                    dve.wait_ge(*when(key))
                    for t in range(TB):
                        for h in range(2):
                            V.tensor_copy(vmz[:, t, 4 * j + h:4 * j + 4:2, h * DH:(h + 1) * DH],
                                          src[:, t, :].rearrange("p (m h d) -> p m h d", h=2, d=DH)[:, :, h, :]).then_inc(*did(dve_steps, done))
                elif name == "kcvc":
                    dve.wait_ge(*when(key))
                    V.tensor_copy(kA[:, 0:2, :], src).then_inc(*did(dve_steps, ("kA", l, 0)))
                    at[done] = at[("kA", l, 0)]
                elif name in ("ksvs", "kwvw"):
                    dve.wait_ge(*when(key))
                    which = 2 if name == "ksvs" else 3
                    V.tensor_copy(kA[:, which, :], src[:, 0, :]).then_inc(*did(dve_steps, ("kA", l, 1)))
                    vz = vsz if name == "ksvs" else vwz
                    for h in range(2):
                        V.tensor_copy(vz[:, :, :, h, h * DH:(h + 1) * DH],
                                      src[:, 1, :].rearrange("p (t g d) -> p t g d", t=TB, g=GROUPS)).then_inc(*did(dve_steps, done))
                if name == "kwvw":
                    dve.wait_ge(*when(("kB", l, 0)))
                    kB = two(bank[0][:, :])
                    for g, low, high in ((0, kA[:, 0:2, :], kB), (1, kB, kA[:, 0:2, :])):
                        V.tensor_copy(kc2[0:DH, :, g, :], low[0:DH, :, :]).then_inc(*did(dve_steps))
                        V.tensor_copy(kc2[DH:P, :, g, 0:T - 1], high[DH:P, :, 1:T]).then_inc(*did(dve_steps, ("kB_used", l, 0)))
                    dve.wait_ge(*did.last)
                    for kv in range(2):
                        pe_col = col2[:, 32 * kv + 16 * l:32 * kv + 16 * l + 16]
                        for g in range(GROUPS):
                            for a in range(2):
                                toks = kc2[:, kv, g, 16 * a:16 * a + 240].rearrange("p (t r two) -> p t r two", r=8, two=2)[:, :, :, 0]
                                dst = win[:, kv, 8 * a:8 * a + 8, CMP_T * g:CMP_T * (g + 1)].rearrange("p r t -> p t r")
                                V.tensor_tensor(dst, toks, rep(pe_col[:, 8 * a:8 * a + 8], CMP_T), ALU.add).then_inc(*did(dve_steps, ("windows", l, kv)))
            dve.wait_ge(*when(("kB", l, 1)))
            for which, kz in ((0, ksz), (1, kwz)):
                here, there = kA[:, 2 + which, :], bank[1][:, which * T:(which + 1) * T]
                for g in range(GROUPS):
                    for h in range(2):
                        rows_ = slice(h * DH, (h + 1) * DH)
                        V.tensor_copy(kz[rows_, g, h, :], (here if g == h else there)[rows_, :]).then_inc(*did(dve_steps, ("kB_used", l, 1)))
            dve.wait_ge(*when(("kcmp", l)))
            for h in range(2):
                rows_ = slice(h * DH, (h + 1) * DH)
                V.tensor_copy(kcz[rows_, :, h, 0:CMP_T], bank[1][rows_, 0:30].rearrange("p (g t) -> p g t", g=GROUPS)).then_inc(*did(dve_steps, ("kcz", l)))
            dve.wait_ge(*when(("vcmp", l)))
            for h in range(2):
                V.tensor_copy(vcz[0:CMP_T, :, h, h * DH:(h + 1) * DH], bank[2][0:CMP_T, 0:P].rearrange("p (g d) -> p g d", g=GROUPS)).then_inc(*did(dve_steps, ("vcz", l)))
            nc.vector.memset(small[:, 48:49], 0.0).then_inc(*did(dve_steps, ("attn", l)))

            def masked_c(i):
                kind, m, _, _ = ITEMS[i]
                s_, nm = sC[:, i % 3], nmC[:, i % 3]
                b0 = 2 * (i % 2)
                item = ("c", l, i)
                if i >= 3:
                    dve.wait_ge(*when(("pt", ("c", l, i - 3))))
                dve.wait_ge(*did.last)
                if kind == "cmp":
                    dve.wait_ge(*when(("s", item, 1)))
                    V.memset(s_[:, :, 0:32], 0.0).then_inc(*did(dve_steps))
                    dve.wait_ge(*did.last)
                    for t in range(TB):
                        V.tensor_tensor(s_[:, :, 16 * t:16 * t + CMP_T], two(bank[b0][:, 30 * t:30 * t + 30]), cbias[:, 2 * m:2 * m + 2, t, :], ALU.add).then_inc(*did(dve_steps, ("s", "c", l, i, 1)))
                    dve.wait_ge(*did.last)
                    for t in range(TB):
                        V.tensor_reduce(nm[:, 2 * t:2 * t + 2], s_[:, :, 16 * t:16 * t + CMP_T], AX.X, ALU.max, negate=True).then_inc(*did(dve_steps, ("max", item)))
                    return
                dve.wait_ge(*when(("s", item, 0)))
                V.tensor_tensor(s_[:, :, 0:P], two(bank[b0][:, 0:2 * P]), bias[:, 2 * m:2 * m + 2, P:T], ALU.add).then_inc(*did(dve_steps, ("s", "c", l, i, 0)))
                dve.wait_ge(*when(("s", item, 1)))
                V.tensor_tensor(s_[:, :, P:3 * P], two(bank[b0 + 1][:, :]), bias[:, 2 * m:2 * m + 2, :], ALU.add).then_inc(*did(dve_steps, ("s", "c", l, i, 1)))
                maxima(item, s_, nm)

            def weigh_c(i):
                kind, m, _, _ = ITEMS[i]
                gate = None
                if kind != "moba":
                    branch = {"cmp": 0, "slc": 1, "win": 2}[kind]
                    gate = gates[:, :, :].rearrange("p t (h b) -> p t h b", b=3)[:, :, 2 * m:2 * m + 2, branch]
                weigh(("c", l, i), sC[:, i % 3], denC[:, i % 3], rdC[:, i % 3], gate, kind == "cmp", CMP_T if kind == "cmp" else None)

            def gated(i):
                kind, m, _, stop = ITEMS[i]
                if stop:
                    k = m if kind == "moba" else 4 + m
                    z = (zm if kind == "moba" else zn)[:, m, :]
                    dve.wait_ge(*when(("oc", l, i)))
                    dve.wait_ge(*did.last)
                    V.tensor_tensor(yC[:, k % 2, :], bank[6 + k % 2][:, 0:T], z, ALU.mult).then_inc(*did(dve_steps, ("y", l, k)))

            def gated_lo(i):
                kind, m, _, stop = ITEMS[i]
                if stop:
                    k = m if kind == "moba" else 4 + m
                    dve.wait_ge(*when(("yh", l, k)))
                    V.tensor_tensor(xl[:, k, :], yC[:, k % 2, :], f32(xh[:, k, :]), ALU.subtract).then_inc(*did(dve_steps, ("yl", l, k)))

            dve.wait_ge(*when(("gates", l)))
            masked_c(0)
            masked_c(1)
            for i in range(len(ITEMS)):
                weigh_c(i)
                if i >= 2:
                    gated(i - 2)
                if i + 2 < len(ITEMS):
                    masked_c(i + 2)
                if i >= 2:
                    gated_lo(i - 2)
                if i >= 16 - AHEAD:
                    lo(first[f"wout{l}"] + i - 16 + AHEAD)
            for i in (len(ITEMS) - 2, len(ITEMS) - 1):
                gated(i)
                gated_lo(i)
            for j in range(4):
                lo(first[f"wout{l}"] + j + AHEAD)
                dve.wait_ge(*when(("wout", l, j)))
                V.tensor_copy(y2[:, 2 * j:2 * j + 2, :], two(bank[j][:, :])).then_inc(*did(dve_steps, ("y2", l, j)))
            inv(s + 1)
            for k in range(KD):
                V.scalar_tensor_tensor(y2[:, k, :], y2[:, k, :], gpost[:, k:k + 1], rs[:, :], ALU.mult, ALU.mult).then_inc(*did(dve_steps))
            dve.wait_ge(*did.last)
            for j in range(4):
                V.tensor_tensor(X[:, 2 * j:2 * j + 2, :], X[:, 2 * j:2 * j + 2, :], y2[:, 2 * j:2 * j + 2, :], ALU.add).then_inc(*did(dve_steps, ("x", 10 + l, j)))
        for t in range(TB):
            for m in range(2):
                dve.wait_ge(*when(("xout", t, m)))
                V.tensor_copy(otok[:, t, 512 * m:512 * m + 512], bank[2 * t + m][:, :]).then_inc(*did(dve_steps, ("otok", t)))

    block_ctx.__exit__(None, None, None)
    return at


_INS = ['x', 'p', 'positions', 'norm_gains', 'ffn_w_in', 'ffn_w_out', 'ple_w_gate', 'ple_w_in', 'a_w_in', 'a_lb_logits',
        'a_out_gain', 'a_w_out', 'kv_norm_in', 'kv_w_down', 'kv_latent_norm', 'kv_w_up', 'b_w_dq', 'b_q_norm', 'b_w_uq',
        'b_w_out', 'final_norm', 'c_2', 'w_ada_2', 'b_ada_2', 'g_pre_2', 'g_post_2', 'w_in_2', 'w_out_2', 'pe_k_2',
        'pe_v_2', 'w_ck1_2', 'w_ck2_2', 'w_cv1_2', 'w_cv2_2']


def kernel(**inputs):
    import numpy as _np
    import concourse.bacc as _bacc
    from concourse import mybir as _mybir
    from concourse.bass_utils import run_bass_kernel_spmd as _run

    arrays = {f"in_{name}": _np.ascontiguousarray(inputs[name]) for name in _INS}
    arrays["in_consts"] = shape_constants()

    def program(known):
        nc = _bacc.Bacc("TRN2", target_bir_lowering=False, num_devices=1)
        io = {n[3:]: nc.dram_tensor(n, a.shape, _mybir.dt.from_np(a.dtype), kind="ExternalInput").ap() for n, a in arrays.items()}
        io["out"] = nc.dram_tensor("out_0", (1, T, D), _mybir.dt.float32, kind="ExternalOutput").ap()
        return nc, build(nc, io, known)

    _, counts = program({})
    nc, _ = program(counts)
    r = _run(nc, [arrays], core_ids=[0])
    return r.results[0]["out_0"]
```

```python
import numpy as np

import concourse.bass as bass
from concourse import mybir

F32 = mybir.dt.float32
F32R = mybir.dt.float32r
BF16 = mybir.dt.bfloat16
I32 = mybir.dt.int32
U32 = mybir.dt.uint32
ACT = mybir.ActivationFunctionType
ALU = mybir.AluOpType
AX = mybir.AxisListType

P = 128
T = 256
TB = T // P
D = 1024
KD = D // P
FF = 2816
KF = FF // P
PAIRS = KF // 2
EPS = 1e-6
NEG = -1e30

CH = 2048
HC = CH // 2
NRAW = 2
NSLOT = 4
AHEAD = NSLOT - 1
MOD_STEPS = 7
MOD = 2 * 3 * D // 4 // 256

HEADS_A = 8
CHUNK_A = 64
HEADS_B = 16
NOPE, ROPE, VDIM = 128, 64, 128
SCALE_B = float((NOPE + ROPE) ** -0.5)
HEADS_C = 8
DH = 64
GROUPS = 2
CMP_T = 15
OFF = dict(qm=0, km=512, vm=1024, zm=1536, qn=2048, kcvc=2560, ksvs=2816, kwvw=3072, gl=3328, zn=3352)
FOLDED = (0, 1, 2, 3, 5, 6, 7)
LEVELS = [64, 32, 16, 8, 4, 2, 1]

C_IDENT, C_PERM, C_CAUS, C_DIST, C_DMASK, C_RESET = 0, 128, 256, 384, 640, 896
C_CMPD, C_CMPM, C_ROWV, C_FREQ, C_SIGN, C_SWAP, C_LVL = 1152, 1182, 1212, 1214, 1215, 1216, 1344
C_N = C_LVL + P // 2 * len(LEVELS)


def shape_constants():
    c = np.zeros((P, C_N), np.float32)
    p = np.arange(P)
    c[:, C_IDENT:C_IDENT + P] = np.eye(P)
    swap = (p // 64) * 64 + (p % 64 + 32) % 64
    c[swap, C_PERM + p] = 1.0
    c[(p + 64) % P, C_SWAP + p] = 1.0
    c[:, C_CAUS:C_CAUS + P] = np.where(p[:, None] >= p[None, :], 0.0, NEG)
    dist = p[:, None] + P - np.arange(T)[None, :]
    c[:, C_DIST:C_DIST + T] = np.maximum(dist, 0)
    c[:, C_DMASK:C_DMASK + T] = np.where(dist >= 0, 0.0, NEG)
    c[:, C_RESET:C_RESET + T] = (np.arange(T) % CHUNK_A != 0)[None, :]
    for b in range(TB):
        d = (b * P + p)[:, None] - (np.arange(CMP_T) * 16 + 31)[None, :]
        c[:, C_CMPD + b * CMP_T:C_CMPD + (b + 1) * CMP_T] = np.maximum(d, 0)
        c[:, C_CMPM + b * CMP_T:C_CMPM + (b + 1) * CMP_T] = np.where(d >= 0, 0.0, NEG)
        c[:, C_ROWV + b] = (b * P + p) >= 31
    half = ROPE // 2
    freq = np.float32(1.0) / (np.float32(10000.0) ** (np.arange(0, ROPE, 2, dtype=np.float32) / np.float32(ROPE)))
    c[:, C_FREQ] = freq[p % half]
    c[:, C_SIGN] = np.where(p % ROPE < half, -1.0, 1.0)
    for n, L in enumerate(LEVELS):
        s, j = p[:, None], np.arange(P // 2)[None, :]
        c[:, C_LVL + n * P // 2:C_LVL + (n + 1) * P // 2] = (s // (2 * L) == j // L) & (s % (2 * L) < L)
    return c


class Steps:

    def __init__(self, at):
        self.at, self.count, self.last = at, {}, None

    def __call__(self, sem, name=None, by=1):
        n = self.count.get(sem.name, 0) + by
        self.count[sem.name] = n
        self.last = (sem, n)
        if name is not None:
            self.at[name] = (sem.name, n)
        return sem, by

    def skip(self, sem, by):
        self.count[sem.name] = self.count.get(sem.name, 0) + by
        self.last = (sem, self.count[sem.name])


def chunk_table():
    first, n = {}, 0
    sizes = []
    for f, after in ((0, [("hgrn", 16), ("aout", 4)]), (1, [("ple0", 5), ("kvd", 2)]),
                     (2, [("dq", 2), ("kvup", 4), ("uq", 8), ("bout", 8)]), (3, [("ple1", 5)])):
        sizes += [(f"in{f}", 2 * PAIRS), (f"out{f}", PAIRS)] + after
    for l in range(2):
        sizes += [(f"win{l}", 16), (f"wout{l}", 4)]
    for name, size in sizes:
        first[name] = n
        n += size
    return first, n


def build(nc, io, known):
    at = {}
    first, n_chunks = chunk_table()

    used = {first["kvd"] + 1: (HC, 0)}
    parts = {first["kvd"] + 1: (2, 0)}
    for u in range(8):
        used[first["uq"] + u], parts[first["uq"] + u] = (HC, 4 * 2 * (NOPE + ROPE) - HC), (4, 0)
    for l in range(2):
        used[first[f"win{l}"] + 13], parts[first[f"win{l}"] + 13] = (KD * 24, 0), (1, 0)
    landings = []
    for c in range(n_chunks):
        landings.append([(landings[c - NRAW][h] if c >= NRAW else 0) + parts.get(c, (1, 1))[h] for h in range(2)])

    names = ["x_landed", "gains_landed", "others_landed", "ple_landed", "cmp_landed", "out_landed", "landed00", "landed01", "landed10", "landed11",
             "hi_ready", "lo_ready", "pe_groups", "act_steps", "dve_steps", "pool_steps",
             "gate_scaled", "up_scaled", "silu_ready", "hidden_ready", "hidden_hi", "hidden_lo", "mod_landed", "mod_steps"]
    sem = {n: nc.alloc_semaphore(n) for n in names}
    landed = [[sem[f"landed{r}{h}"] for h in range(2)] for r in range(NRAW)]
    hi_ready, lo_ready, pe_groups = sem["hi_ready"], sem["lo_ready"], sem["pe_groups"]
    act_steps, dve_steps, pool_steps = sem["act_steps"], sem["dve_steps"], sem["pool_steps"]
    gate_scaled, up_scaled, silu_ready = sem["gate_scaled"], sem["up_scaled"], sem["silu_ready"]
    hidden_ready, hidden_hi, hidden_lo = sem["hidden_ready"], sem["hidden_hi"], sem["hidden_lo"]

    def when(name):
        s, n = known[name] if known else ("pe_groups", 1)
        return sem[s], n

    base = [(nc.sbuf_base + 63) // 64 * 64]

    def fixed(name, shape, dt=F32):
        size = int(np.prod(shape[1:])) * 4
        t = nc.alloc_sbuf_tensor_at(name, shape, dt, offset=base[0])
        base[0] += (size + 63) // 64 * 64
        return t

    w_raw = fixed("w_raw", [P, NRAW, CH])
    w_hi = fixed("w_hi", [P, NSLOT, CH], F32R)
    w_lo = fixed("w_lo", [P, NSLOT, CH], F32R)
    X = fixed("X", [P, KD, T])
    xh = fixed("xh", [P, KD, T], F32R)
    xl = fixed("xl", [P, KD, T], F32R)
    sq_at = base[0]
    sq = fixed("sq", [P, KD, T])
    rs = fixed("rs", [P, T])
    std = fixed("std", [P, T])
    ones = fixed("ones", [P, P])
    const = fixed("const", [P, C_N])
    ident_bf = fixed("ident_bf", [P, P], BF16)
    caus_bf = fixed("caus_bf", [P, P], BF16)
    cos = fixed("cos", [P, T])
    sin = fixed("sin", [P, T])
    col0 = fixed("col0", [P, 104])
    col1 = fixed("col1", [P, 88])
    col2 = fixed("col2", [P, 64])
    latent_at = base[0]
    ckh = fixed("ckh", [P, 2, T], F32R)
    ckl = fixed("ckl", [P, 2, T], F32R)
    krz = fixed("krz", [P, 2, T])
    eps = fixed("eps", [P, 1])
    lb = fixed("lb", [P, KD])
    oml = fixed("oml", [P, KD])
    small = fixed("small", [P, 64])
    rst = fixed("rst", [P, TB])
    csf = fixed("csf", [P, KD])
    mods = fixed("mods", [P, 2, 24])
    gpre = fixed("gpre", [P, KD])
    gpost = fixed("gpost", [P, KD])
    ptok = fixed("ptok", [P, 2, TB, T])
    region = base[0]

    def at_offset(start):
        pos = [start]

        def place(name, shape, dt=F32):
            size = int(np.prod(shape[1:])) * 4
            t = nc.alloc_sbuf_tensor_at(name, shape, dt, offset=pos[0])
            pos[0] += (size + 63) // 64 * 64
            assert pos[0] <= nc.sbuf_usable_end, (name, pos[0])
            return t
        return place, pos

    place, _ = at_offset(region)
    xtok = place("xtok", [P, TB, D])
    vrow0 = place("vrow0", [P, P])
    place, _ = at_offset(latent_at)
    vrow1 = place("vrow1", [P, P])
    vrow2 = place("vrow2", [P, P])
    pos_i = place("pos_i", [P, T], I32)
    ang = place("ang", [P, T])
    turns = place("turns", [P, T])
    red = place("red", [P, T])
    mag = place("mag", [P, T])
    place, _ = at_offset(region)
    hh = place("hh", [P, KF, T], F32R)
    hl = place("hl", [P, KF, T], F32R)
    gate_t = place("gate_t", [P, 2, 2, T])
    up_t = place("up_t", [P, 2, 2, T])
    silu_t = place("silu_t", [P, 2, 2, T])
    hid_t = place("hid_t", [P, 2, 2, T])
    mod_raw = place("mod_raw", [P, KD // 2, 256])
    mod_acc = place("mod_acc", [P, MOD, 256])
    place, _ = at_offset(region)
    hg_a = place("hg_a", [P, KD, T])
    hg_k = place("hg_k", [P, KD, T])
    hg_b = place("hg_b", [P, KD, T])
    hg_q = place("hg_q", [P, KD, T])
    hg_v = place("hg_v", [P, TB, D])
    hg_g = place("hg_g", [P, KD, T])
    hg_f0 = place("hg_f0", [P, KD, T])
    hg_f = [hg_f0, sq]
    hg_s = place("hg_s", [P, KD, 2, P])
    hg_x = place("hg_x", [P, KD, P])
    hg_t = place("hg_t", [P, KD])
    place, _ = at_offset(region)
    pt = place("pt", [P, 2, T])
    pth = place("pth", [P, 2, T], F32R)
    ptl = place("ptl", [P, 2, T], F32R)
    pp = place("pp", [P, KD, T])
    pg = place("pg", [P, KD, T])
    place, _ = at_offset(region)
    ck = place("ck", [P, 2, T])
    kr = place("kr", [P, T])
    kr_t = place("kr_t", [P, 2, T])
    rs2_kv = place("rs2_kv", [P, T])
    std2_kv = place("std2_kv", [P, T])
    place, posn = at_offset(region)
    oh_at = posn[0]
    qn = place("qn", [P, HEADS_B, T])
    ol_at = posn[0]
    kn = place("kn", [P, HEADS_B, T])
    qr = place("qr", [P, HEADS_B // 2, T])
    vb = place("vb", [P, TB, HEADS_B * VDIM])
    temp_at = posn[0]
    cq = place("cq", [P, 4, T])
    cqh = place("cqh", [P, 4, T], F32R)
    cql = place("cql", [P, 4, T], F32R)
    place, _ = at_offset(sq_at)
    qr_t = place("qr_t", [P, 2, T])
    qraw = place("qraw", [P, 2, T])
    rs2 = place("rs2", [P, T])
    std2 = place("std2", [P, T])
    place, _ = at_offset(oh_at)
    oh = place("oh", [P, HEADS_B, T], F32R)
    place, _ = at_offset(ol_at)
    ol = place("ol", [P, HEADS_B, T], F32R)
    place, _ = at_offset(temp_at)
    sB = place("sB", [P, 3, 2, 3 * P])
    nmB = place("nmB", [P, 3, 4])
    denB = place("denB", [P, 3, 4])
    rdB = place("rdB", [P, 3, 4])
    place, _ = at_offset(sq_at)
    ptB = place("ptB", [P, 2, 2, 3 * P])
    place, posn = at_offset(region)
    qm = place("qm", [P, 4, T])
    qs = place("qs", [P, 4, T])
    kmz = place("kmz", [P, 4, 2, T])
    ksz = place("ksz", [P, GROUPS, 2, T])
    kwz = place("kwz", [P, GROUPS, 2, T])
    y_at = posn[0]
    vmz = place("vmz", [P, TB, HEADS_C, P])
    vsz = place("vsz", [P, TB, GROUPS, 2, P])
    vwz = place("vwz", [P, TB, GROUPS, 2, P])
    zm = place("zm", [P, 4, T])
    zn = place("zn", [P, 4, T])
    kcz = place("kcz", [P, GROUPS, 2, 16])
    vcz = place("vcz", [16, GROUPS, 2, P])
    gates = place("gates", [P, TB, 24])
    cbias = place("cbias", [P, HEADS_C, TB, CMP_T], BF16)
    gh = place("gh", [DH, 64])
    gx = place("gx", [DH, 64])
    wc2 = place("wc2", [DH, 3, DH])
    temp_at = posn[0]
    kA = place("kA", [P, 4, T])
    win = place("win", [P, 2, 16, 2 * CMP_T])
    wc1 = place("wc1", [P, 2, 16, DH])
    place, _ = at_offset(temp_at)
    sC = place("sC", [P, 3, 2, 3 * P])
    ptC = place("ptC", [P, 2, 2, 3 * P])
    nmC = place("nmC", [P, 3, 4])
    denC = place("denC", [P, 3, 4])
    rdC = place("rdC", [P, 3, 4])
    yC = place("yC", [P, 2, T])
    place, _ = at_offset(latent_at)
    kc2 = place("kc2", [P, 2, GROUPS, T])
    place, _ = at_offset(y_at)
    y2 = place("y2", [P, KD, T])
    place, _ = at_offset(sq_at)
    bias = place("bias", [P, HEADS_C, T], BF16)
    place, _ = at_offset(region)
    otok = place("otok", [P, TB, D])

    bank = [nc.alloc_psum_tensor(f"bank{i}", [P, 512], F32) for i in range(8)]
    ident = const[:, C_IDENT:C_IDENT + P]

    def g_norm(l, g):
        return lambda k: col0[:, (l * 4 + g) * KD + k:(l * 4 + g) * KD + k + 1]

    def g_kv(k):
        return col0[:, 81 + k:82 + k]

    def g_latent(k):
        return col0[:, 89 + k:90 + k]

    def g_q(k):
        return col0[:, 91 + k:92 + k]

    def g_final(k):
        return col0[:, 95 + k:96 + k]

    out_gain = col0[:, 80:81]

    def sums_bank(s):
        return 4 if s in (0, 2, 6) else 3

    def rep(ap, n):
        shape = list(ap.shape)
        return ap.unsqueeze(1).to_broadcast([shape[0], n] + shape[1:])

    def two(ap):
        return ap.rearrange("p (a n) -> p a n", a=2)

    def f32(ap):
        return ap.bitcast(F32)

    def half_columns(c, h):
        return slice(HC * h, HC * h + (used[c][h] or 8)) if c in used else slice(HC * h, HC * (h + 1))

    def slot(w, c, k):
        rows, cols = k
        return w[:, c % NSLOT, 0:rows * cols].rearrange("p (k n) -> p k n", k=rows)

    WIN = ([("qm", j) for j in range(2)] + [("km", j) for j in range(2)] + [("vm", j) for j in range(2)]
           + [("zm", j) for j in range(2)] + [("qn", j) for j in range(2)]
           + [("kcvc", 0), ("ksvs", 0), ("kwvw", 0), ("gl", 0)] + [("zn", j) for j in range(2)])

    ITEMS = [("moba", m, True, True) for m in range(4)]
    for m in range(4):
        ITEMS += [("win", m, True, False), ("slc", m, False, False), ("cmp", m, False, True)]

    block_ctx = nc.Block()
    block = block_ctx.__enter__()

    @block.sync
    def _(sp):
        def half_free(c, h, i2=0):
            if c >= NRAW:
                sp.wait_ge(lo_ready, 2 * (c - NRAW) + h + 1 + i2)

        def load(c, k, src):
            r, n = k
            if c in used:
                half_free(c, 1)
                dst = w_raw[:, c % NRAW, 0:r * n].rearrange("p (k n) -> p k n", k=r)
                sp.dma_start(dst, src.rearrange("(k p) n -> p k n", p=P)).then_inc(landed[c % NRAW][0], 16)
                return
            for h in range(2):
                load_half(c, h, r, src[r // 2 * P * h:r // 2 * P * (h + 1), :])

        def load_half(c, h, r, src, i2=0):
            half_free(c, h, i2)
            sp.dma_start(w_raw[:, c % NRAW, HC * h:HC * (h + 1)].rearrange("p (k n) -> p k n", k=r // 2),
                         src.rearrange("(k p) n -> p k n", p=P)).then_inc(landed[c % NRAW][h], 16)

        def load_ffn(f):
            l, w = f // 2, f % 2
            c = first[f"in{f}"]
            w_in, w_out = io["ffn_w_in"][l, w], io["ffn_w_out"][l, w]

            def pair(c, p, it):
                for part in range(2):
                    cols = bass.ds(part * FF + 256 * p + (0 if it is None else 256 * it), 256)
                    for h in range(2):
                        load_half(c + part, h, KD, w_in[D // 2 * h:D // 2 * (h + 1), cols], 0 if it is None else 4 * it)

            pair(c, 0, None)
            with sp.Fori(0, PAIRS - 1) as it:
                pair(c + 2, 1, it)
            c = first[f"out{f}"]
            load(c, (2, D), w_out[0:256, :])
            with sp.Fori(0, (PAIRS - 1) // 2) as it:
                for j in range(2):
                    for h in range(2):
                        load_half(c + 1 + j, h, 2, w_out[bass.ds(256 * (1 + j) + P * h + 512 * it, P), :], 4 * it)

        def load_cols(name, w, width, cols, count=None):
            c = first[name]
            for j in range(count if count is not None else cols // width):
                load(c + j, (w.shape[0] // P, width), w[:, j * width:(j + 1) * width])

        def load_rows(name, w):
            c = first[name]
            for j in range(w.shape[0] // 256):
                load(c + j, (2, w.shape[1]), w[256 * j:256 * j + 256, :])

        sp.dma_start(xtok[:, :, :], io["x"][0].rearrange("(b p) n -> p b n", p=P)).then_inc(sem["x_landed"], 16)
        load_ffn(0)
        a_in = io["a_w_in"][0]
        for n, seg in enumerate((1, 0, 2, 3)):
            for j in range(4):
                load(first["hgrn"] + 4 * n + j, (KD, 256), a_in[:, seg * D + 256 * j:seg * D + 256 * j + 256])
        load_cols("aout", io["a_w_out"][0], 256, D)
        load_ffn(1)

        def load_ple(l):
            c = first[f"ple{l}"]
            load(c, (2, D), io["ple_w_in"][l])
            for j in range(4):
                load(c + 1 + j, (KD, 256), io["ple_w_gate"][l][:, 256 * j:256 * j + 256])

        load_ple(0)
        load(first["kvd"], (KD, 256), io["kv_w_down"][:, 0:256])
        c = first["kvd"] + 1
        half_free(c, 1)
        for h in range(2):
            sp.dma_start(w_raw[:, c % NRAW, 0:KD * P].rearrange("p (k h n) -> p k h n", k=KD, h=2)[:, :, h, :],
                         io["kv_w_down"][:, 256:320].rearrange("(k p) n -> p k n", p=P)).then_inc(landed[c % NRAW][0], 16)
        load_ffn(2)
        load_cols("dq", io["b_w_dq"][0], 256, 512)
        for j in range(4):
            load(first["kvup"] + j, (2, D), io["kv_w_up"][:, D * j:D * j + D])
        for u in range(8):
            c = first["uq"] + u
            half_free(c, 1)
            for at_, width in ((0, NOPE), (NOPE, ROPE)):
                for h in range(2):
                    src = io["b_w_uq"][0][:, (2 * u + h) * (NOPE + ROPE) + at_:(2 * u + h) * (NOPE + ROPE) + at_ + width]
                    col = 2 * at_ + h * width
                    sp.dma_start(w_raw[:, c % NRAW, 0:4 * 384].rearrange("p (k n) -> p k n", k=4)[:, :, col:col + width],
                                 src.rearrange("(k p) n -> p k n", p=P)).then_inc(landed[c % NRAW][0], 16)
        load_rows("bout", io["b_w_out"][0])
        load_ffn(3)
        load_ple(1)
        for l in range(2):
            w = io["w_in_2"][l]
            for n, (name, j) in enumerate(WIN):
                width = 24 if name == "gl" else 256
                load(first[f"win{l}"] + n, (KD, width), w[:, OFF[name] + 256 * j:OFF[name] + 256 * j + width])
            load_cols(f"wout{l}", io["w_out_2"][l], 256, D)
        for m in range(4):
            sp.wait_ge(*when(("otok", m)))
            sp.dma_start(io["out"][0].rearrange("(b p) n -> p b n", p=P)[:, :, T * m:T * m + T], otok[:, :, T * m:T * m + T]).then_inc(sem["out_landed"], 16)
        sp.wait_ge(sem["out_landed"], 16 * 4)

    @block.gpsimd
    def _(pool):
        did = Steps(at)
        nc.gpsimd.memset(ones[:, :], 1.0).then_inc(*did(pool_steps))
        nc.gpsimd.memset(eps[:, :], EPS).then_inc(*did(pool_steps, "memsets"))
        G = nc.gpsimd

        def modulation(f):
            l = f // 2
            steps, landed_ = sem["mod_steps"], sem["mod_landed"]
            pool.wait_ge(*when({0: "csf", 1: ("x", 2, 3), 2: "ckl", 3: ("x", 6, 3)}[f]))
            if f:
                pool.wait_ge(*when(("modsum", f - 1)))
            for j in range(MOD):
                acc = mod_acc[:, j, :]
                n = MOD_STEPS * (MOD * f + j)
                for half in range(2):
                    if n:
                        pool.wait_ge(steps, n)
                    cols = slice(256 * (MOD * (f % 2) + j), 256 * (MOD * (f % 2) + j + 1))
                    pool.dma_start(mod_raw[:, :, :], io["w_ada_2"][l][512 * half:512 * half + 512, cols].rearrange("(k p) n -> p k n", p=P)).then_inc(landed_, 16)
                    pool.wait_ge(landed_, 16 * (2 * (MOD * f + j) + half + 1))
                    c = csf[:, KD // 2 * half:KD // 2 * (half + 1)].unsqueeze(2).to_broadcast([P, KD // 2, 256])
                    G.tensor_tensor(mod_raw[:, :, :], mod_raw[:, :, :], c, ALU.mult).then_inc(steps, 1)
                    pool.wait_ge(steps, n + 1)
                    G.tensor_tensor(mod_raw[:, 0:2, :], mod_raw[:, 0:2, :], mod_raw[:, 2:4, :], ALU.add).then_inc(steps, 1)
                    pool.wait_ge(steps, n + 2)
                    if half == 0:
                        G.tensor_tensor(acc, mod_raw[:, 0, :], mod_raw[:, 1, :], ALU.add).then_inc(steps, 1)
                    else:
                        G.tensor_tensor(mod_raw[:, 0, :], mod_raw[:, 0, :], mod_raw[:, 1, :], ALU.add).then_inc(steps, 1)
                        pool.wait_ge(steps, n + 3)
                        G.tensor_tensor(acc, acc, mod_raw[:, 0, :], ALU.add).then_inc(steps, 1)
                    n += 3

        def levels():
            pool.wait_ge(*when("scans"))

            def halves(t, L, hs):
                r = t[:, hs, :].rearrange("p h n -> p (h n)").rearrange("p (b two n) -> p b two n", two=2, n=L)
                return r[:, :, 0, :], r[:, :, 1, :]

            for n, L in enumerate(LEVELS):
                for half, hs in enumerate((slice(0, 4), slice(4, 8))):
                    bl, br = halves(hg_b, L, hs)
                    al, ar = halves(hg_a, L, hs)
                    end = bl[:, :, L - 1:L].to_broadcast([P, HEADS_A // 2 * T // (2 * L), L])
                    if n == 0:
                        G.tensor_copy(ar, br).then_inc(*did(pool_steps))
                    else:
                        pool.wait_ge(*when(("exp", n - 1, half)))
                        G.tensor_tensor(ar, br, end, ALU.subtract).then_inc(*did(pool_steps))
                    G.tensor_tensor(al, end, bl, ALU.subtract).then_inc(*did(pool_steps, ("diff", n, half)))
            G.tensor_tensor(hg_t[:, :].unsqueeze(2), hg_b[:, :, CHUNK_A - 1:CHUNK_A], hg_b[:, :, 2 * CHUNK_A - 1:2 * CHUNK_A], ALU.add).then_inc(*did(pool_steps))
            for half, hs in enumerate((slice(0, 4), slice(4, 8))):
                b = hg_b[:, hs, :].rearrange("p h (c n) -> p h c n", n=CHUNK_A)
                a = hg_a[:, hs, :].rearrange("p h (c n) -> p h c n", n=CHUNK_A)
                def end(c):
                    return b[:, :, c, CHUNK_A - 1:CHUNK_A].to_broadcast([P, HEADS_A // 2, CHUNK_A])
                pool.wait_ge(*did.last)
                pool.wait_ge(*when(("exp", 6, half)))
                G.tensor_tensor(a[:, :, 0, :], hg_t[:, hs].unsqueeze(2).to_broadcast([P, HEADS_A // 2, CHUNK_A]), b[:, :, 0, :], ALU.subtract).then_inc(*did(pool_steps))
                G.tensor_tensor(a[:, :, 1, :], end(1), b[:, :, 1, :], ALU.subtract).then_inc(*did(pool_steps))
                G.tensor_copy(a[:, :, 2, :], b[:, :, 2, :]).then_inc(*did(pool_steps))
                G.tensor_tensor(a[:, :, 3, :], b[:, :, 3, :], end(2), ALU.add).then_inc(*did(pool_steps, ("diff", 7, half)))

        def fold(s):
            pool.wait_ge(*when(("sq", s, 3)))
            G.tensor_tensor(sq[:, 0:4, :], sq[:, 0:4, :], sq[:, 4:8, :], ALU.add).then_inc(*did(pool_steps))
            pool.wait_ge(*did.last)
            G.tensor_tensor(sq[:, 0:2, :], sq[:, 0:2, :], sq[:, 2:4, :], ALU.add).then_inc(*did(pool_steps, ("folded", s)))

        fold(0)
        modulation(0)
        fold(1)
        levels()
        fold(2)
        modulation(1)
        pool.wait_ge(*when("rope"))
        G.memset(krz[:, :, :], 0.0).then_inc(*did(pool_steps))
        fold(3)
        modulation(2)
        fold(5)
        fold(6)
        modulation(3)
        fold(7)
        for l in range(2):
            pool.wait_ge(*when(("x", 9 + l, 3)))
            for z in (kmz, vmz, ksz, kwz, vsz, vwz, kcz, vcz):
                last = nc.gpsimd.memset(z[tuple(slice(None) for _ in z.shape)], 0.0).then_inc(*did(pool_steps))
            nc.gpsimd.memset(small[:, 32:33], 0.0).then_inc(*did(pool_steps, ("zeros", l)))
            for kv, name in enumerate(("ck", "cv")):
                pool.dma_start(wc1[:, kv, :, :], io[f"w_{name}1_2"][l].rearrange("(r p) e -> p r e", p=P)).then_inc(sem["cmp_landed"], 16)
                for n in ((0, 1), (2,))[kv]:
                    pool.dma_start(wc2[:, n, :], io[f"w_{name}2_2"][l]).then_inc(sem["cmp_landed"], 16)

    @block.scalar
    def _(act):
        did = Steps(at)
        A = nc.scalar.activation

        gains = [(const[:, 0:P], io["consts"][:, 0:P]),
                 (vrow0[0:64, :], io["norm_gains"].rearrange("l g (k p) -> (l g k) p", p=P)),
                 (vrow0[64:80, :], io["a_lb_logits"].rearrange("r (k p) -> (r k) p", p=P)),
                 (vrow0[80:81, :], io["a_out_gain"]),
                 (vrow0[81:89, :], io["kv_norm_in"].rearrange("(k p) -> k p", p=P)),
                 (vrow0[89:91, :], io["kv_latent_norm"].rearrange("(k p) -> k p", p=P)),
                 (vrow0[91:95, :], io["b_q_norm"].rearrange("l (k p) -> (l k) p", p=P)),
                 (vrow0[95:103, :], io["final_norm"].rearrange("(k p) -> k p", p=P))]
        others = [(pos_i[0:1, :], io["positions"]),
                 (const[:, P:], io["consts"][:, P:]),
                 (vrow1[0:48, :], io["b_ada_2"].rearrange("l (k p) -> (l k) p", p=P)),
                 (vrow1[48:64, :], io["g_pre_2"].rearrange("l (k p) -> (l k) p", p=P)),
                 (vrow1[64:80, :], io["g_post_2"].rearrange("l (k p) -> (l k) p", p=P)),
                 (vrow1[80:88, :], io["c_2"].rearrange("l (k p) -> (l k) p", p=P)),
                 (vrow2[0:32, :], io["pe_k_2"].rearrange("l (r a) d -> (l r) (a d)", a=2)),
                 (vrow2[32:64, :], io["pe_v_2"].rearrange("l (r a) d -> (l r) (a d)", a=2))]
        for dst, src in gains:
            act.dma_start(dst, src).then_inc(sem["gains_landed"], 16)

        def load_others():
            for dst, src in others:
                act.dma_start(dst, src).then_inc(sem["others_landed"], 16)
            for l in range(2):
                act.dma_start(ptok[:, l, :, :], io["p"][l, 0].rearrange("(b p) n -> p b n", p=P)).then_inc(sem["ple_landed"], 16)

        def hi(c, it=None):
            if c >= n_chunks:
                return
            i2 = 0 if it is None else 32 * it
            i4 = 0 if it is None else 4 * it
            for h in range(2):
                act.wait_ge(landed[c % NRAW][h], 16 * landings[c][h] + i2)
                if c >= NSLOT and h == 0:
                    act.wait_ge(pe_groups, when(("chunk", c - NSLOT))[1] + i4)
                cols = half_columns(c, h)
                A(w_hi[:, c % NSLOT, cols], w_raw[:, c % NRAW, cols], ACT.Copy).then_inc(*did(hi_ready))

        def norm(nu, v, gain, s, free, late=()):
            if free is not None:
                act.wait_ge(*when(free))
            for m in range(4):
                act.wait_ge(*when(("x", v, m)))
                for k in (2 * m, 2 * m + 1):
                    A(xh[:, k, :], X[:, k, :], ACT.Copy, scale=gain(k)).then_inc(*did(act_steps, ("xh", nu, k)))
            if s is not None:
                if s > 0:
                    act.wait_ge(*when(("sums", s - 1)))
                for m in range(4):
                    A(sq[:, 2 * m:2 * m + 2, :], X[:, 2 * m:2 * m + 2, :], ACT.Square).then_inc(*did(act_steps, ("sq", s, m)))
            for c in late:
                hi(c)

        def root(s):
            act.wait_ge(*when(("sums", s)))
            if s > 0:
                act.wait_ge(*when(("rs", s - 1)))
            A(std[:, :], bank[sums_bank(s)][:, 0:T], ACT.Sqrt, bias=eps[:, :], scale=1.0 / D).then_inc(*did(act_steps, ("std", s)))

        def ffn(f, nu, v, gain, s, free, late=(), aside=None):
            norm(nu, v, gain, s, free, late)
            c = first[f"in{f}"]
            n0 = PAIRS * f

            def pair(c, p, it=None):
                o = 0 if it is None else 2 * it
                hi(c + AHEAD, it)
                act.wait_ge(gate_scaled, n0 + p + 2 + o)
                if it is not None or p >= 2:
                    act.wait_ge(hidden_ready, n0 + max(p - 1, 1) + o)
                A(silu_t[:, p % 2, :, :], gate_t[:, p % 2, :, :], ACT.Silu).then_inc(*did(silu_ready))
                hi(c + 1 + AHEAD, it)
                act.wait_ge(hidden_ready, n0 + p + 1 + o)
                k = bass.ds(2 * p + (0 if it is None else 4 * it), 2)
                A(hh[:, k, :], hid_t[:, p % 2, :, :], ACT.Copy).then_inc(*did(hidden_hi))

            def first_pair():
                hi(c + AHEAD)
                hi(c + 1 + AHEAD)
                if s is not None:
                    root(s)
                act.wait_ge(gate_scaled, n0 + 2)
                A(silu_t[:, 0, :, :], gate_t[:, 0, :, :], ACT.Silu).then_inc(*did(silu_ready))
                act.wait_ge(hidden_ready, n0 + 1)
                A(hh[:, 0:2, :], hid_t[:, 0, :, :], ACT.Copy).then_inc(*did(hidden_hi))

            first_pair()
            if aside is not None:
                aside()
            with act.Fori(0, (PAIRS - 1) // 2) as it:
                for j in range(2):
                    pair(c + 2 + 2 * j, 1 + j, it)
            turns_left = (PAIRS - 1) // 2 - 1
            did.skip(hi_ready, 8 * turns_left)
            did.skip(silu_ready, 2 * turns_left)
            did.skip(hidden_hi, 2 * turns_left)
            c = first[f"out{f}"]
            for q in range(2):
                hi(c + q + AHEAD)
            with act.Fori(0, 2) as it:
                for q in range(4):
                    hi(c + 2 + q + AHEAD, it)
            did.skip(hi_ready, 8)

        def rope_tables():
            act.wait_ge(*when("angles"))
            A(sin[:, :], red[:, :], ACT.Sin).then_inc(*did(act_steps))
            act.wait_ge(*when("quarter"))
            A(cos[:, :], mag[:, :], ACT.Sin).then_inc(*did(act_steps, "sin"))

        hi(0)
        load_others()

        def aside():
            act.wait_ge(*when(("col", 1)))
            A(csf[:, :], col1[:, 80:88], ACT.Silu).then_inc(*did(act_steps, "csf"))
            act.wait_ge(*when("lb_shift"))
            A(small[:, 16:32], small[:, 0:16], ACT.Exp).then_inc(*did(act_steps, "lb_exp"))

        act.wait_ge(*when("memsets"))
        ffn(0, 0, 0, g_norm(0, 0), 0, None, range(1, AHEAD), aside)

        c0 = first["hgrn"]
        norm(1, 1, g_norm(0, 1), 1, ("chunk", first["out0"] - 1), [c0 - 1 + AHEAD])
        for j in range(4):
            if j != 1:
                hi(c0 + j + AHEAD)
            if j == 0:
                hi(c0 + 1 + AHEAD)
                root(1)
            act.wait_ge(*when(("f", j)))
            A(hg_k[:, 2 * j:2 * j + 2, :], hg_a[:, 2 * j:2 * j + 2, :], ACT.Sigmoid, scale=-1.0).then_inc(*did(act_steps))
            act.wait_ge(*did.last)
            A(hg_a[:, 2 * j:2 * j + 2, :], hg_a[:, 2 * j:2 * j + 2, :], ACT.Sigmoid).then_inc(*did(act_steps, ("sg", j)))
        act.wait_ge(*did.last)
        act.wait_ge(*when("lb"))
        for h in range(HEADS_A):
            A(hg_a[:, h, :], hg_a[:, h, :], ACT.Ln, bias=lb[:, h:h + 1], scale=oml[:, h:h + 1]).then_inc(*did(act_steps, ("ln", h)))
        for j in range(4):
            hi(c0 + 4 + j + AHEAD)

        def level_exp(n):
            for half, hs in enumerate((slice(0, 4), slice(4, 8))):
                act.wait_ge(*when(("diff", n, half)))
                if n >= 2:
                    act.wait_ge(*when((("lev", n - 2), half)))
                elif n == 1 and half == 0:
                    act.wait_ge(*when(("sums", 1)))
                A(hg_f[n % 2][:, hs, :], hg_a[:, hs, :], ACT.Exp).then_inc(*did(act_steps, ("exp", n, half)))

        level_exp(0)
        for n in range(8):
            hi(c0 + 8 + n + AHEAD)
            if n < 7:
                level_exp(n + 1)
        act.wait_ge(*when(("g", 3)))
        A(hg_g[:, :, :], hg_g[:, :, :], ACT.Sigmoid).then_inc(*did(act_steps, "gate_sg"))
        for m in range(4):
            act.wait_ge(*when(("o", m)))
            A(sq[:, 2 * m:2 * m + 2, :], two(bank[4 + m][:, :]), ACT.Square).then_inc(*did(act_steps, ("osq", m)))
        for m in range(4):
            act.wait_ge(*when(("osum", m)))
            A(hg_a[:, 2 * m:2 * m + 2, :], two(bank[m][:, :]), ACT.Ln, bias=eps[:, :], scale=1.0 / P).then_inc(*did(act_steps, ("oln", m)))
        for m in range(4):
            act.wait_ge(*when(("oln", m)))
            A(hg_a[:, 2 * m:2 * m + 2, :], hg_a[:, 2 * m:2 * m + 2, :], ACT.Exp, scale=-0.5).then_inc(*did(act_steps, ("ors", m)))
        for m in range(4):
            act.wait_ge(*when(("og", m)))
            A(xh[:, 2 * m:2 * m + 2, :], hg_b[:, 2 * m:2 * m + 2, :], ACT.Copy).then_inc(*did(act_steps, ("oh", m)))
        for j in range(3):
            hi(first["aout"] + j + AHEAD)

        ffn(1, 3, 2, g_norm(0, 2), 2, ("chunk", first["in1"] - 1), [first["in1"] - 1 + AHEAD], rope_tables)

        def ple(l, nu, v, s):
            c = first[f"ple{l}"]
            act.wait_ge(*when(("pt", l)))
            A(pth[:, :, :], pt[:, :, :], ACT.Copy).then_inc(*did(act_steps, ("pth", l)))
            norm(nu, v, g_norm(l, 3), s, ("chunk", c - 1), [c - 1 + AHEAD, c + AHEAD])
            for j in range(4):
                if j != 1:
                    hi(c + 1 + j + AHEAD)
                if j == 0:
                    hi(c + 2 + AHEAD)
                    root(s)
                act.wait_ge(*when(("pg", l, j)))
                A(pg[:, 2 * j:2 * j + 2, :], pg[:, 2 * j:2 * j + 2, :], ACT.Sigmoid).then_inc(*did(act_steps, ("pgs", l, j)))

        ple(0, 4, 3, 3)

        norm(5, 4, g_kv, 4, ("chunk", first["kvd"] - 1))
        hi(first["kvd"] + AHEAD)
        root(4)
        act.wait_ge(*when("ck"))
        A(sq[:, 0:2, :], ck[:, :, :], ACT.Square).then_inc(*did(act_steps, "cksq"))
        hi(first["kvd"] + 1 + AHEAD)
        act.wait_ge(*when("cksum"))
        A(std2_kv[:, :], bank[6][:, 0:T], ACT.Sqrt, bias=eps[:, :], scale=1.0 / 256).then_inc(*did(act_steps, "ckstd"))
        act.wait_ge(*when("ckn"))
        A(ckh[:, :, :], ck[:, :, :], ACT.Copy).then_inc(*did(act_steps, "ckh"))

        ffn(2, 6, 4, g_norm(1, 0), None, ("chunk", first["in2"] - 1))

        norm(7, 5, g_norm(1, 1), 5, ("chunk", first["out2"] - 1), [first["dq"] - 1 + AHEAD])
        c0 = first["dq"]
        for j in range(2):
            if j == 0:
                hi(c0 + AHEAD)
                hi(c0 + 1 + AHEAD)
                root(5)
            act.wait_ge(*when(("cq", j)))
            A(sq[:, 2 * j:2 * j + 2, :], cq[:, 2 * j:2 * j + 2, :], ACT.Square).then_inc(*did(act_steps, ("cqsq", j)))
        for u in range(4):
            hi(first["kvup"] + u + AHEAD)
            for b in range(TB):
                act.wait_ge(*when(("v", u, b)))
                A(vb[:, b, 512 * u:512 * u + 512], bank[4 * (u % 2) + 2 + b][:, :], ACT.Copy).then_inc(*did(act_steps, ("vb", u, b)))
            if u == 0:
                act.wait_ge(*when("cqsum"))
                A(std2[:, :], bank[4][:, 0:T], ACT.Sqrt, bias=eps[:, :], scale=1.0 / 512).then_inc(*did(act_steps, "cqstd"))
            if u == 1:
                for j in range(4):
                    act.wait_ge(*when(("cqn", j)))
                    A(cqh[:, j, :], cq[:, j, :], ACT.Copy).then_inc(*did(act_steps, ("cqh", j)))
        for u in range(8 - AHEAD):
            hi(first["uq"] + u + AHEAD)

        def exps(item, b0, s, nm, den, width=None):
            act.wait_ge(*when(("max", item)))
            i = item[-1]
            if i >= 3:
                act.wait_ge(*when(("pt", item[:-1] + (i - 3,))))
            for h in range(2):
                for t in range(TB):
                    n = (t + 1) * P
                    if width is None:
                        src, cols = bank[b0 + t][:, h * n:(h + 1) * n], slice(t * P, t * P + n)
                    else:
                        src, cols = bank[b0][:, (2 * t + h) * width:(2 * t + h + 1) * width], slice(16 * t, 16 * t + width)
                    A(s[:, h, cols], src, ACT.Exp, bias=nm[:, 2 * t + h:2 * t + h + 1],
                      accum_out=den[:, 2 * t + h:2 * t + h + 1]).then_inc(*did(act_steps, ("exps", item)))

        def probs_t(item, buf, width):
            act.wait_ge(*when(("pt", item)))
            for h in range(2):
                A(buf[:, h, 0:width], bank[4 + h][:, 0:width], ACT.Copy).then_inc(*did(act_steps, ("ptcopy", item)))

        for i in range(8):
            exps(("b", i), 2 * (i % 2), sB[:, i % 3], nmB[:, i % 3], denB[:, i % 3])
            if i >= 6:
                hi(first["bout"] + i - 6)
            if i >= 1:
                probs_t(("b", i - 1), ptB[:, (i - 1) % 2], 3 * P)
            if i >= 2:
                act.wait_ge(*when(("ob", i - 2)))
                A(oh[:, 2 * (i - 2):2 * (i - 2) + 2, :], two(bank[6 + i % 2][:, :]), ACT.Copy).then_inc(*did(act_steps, ("oh", "b", i - 2)))
        probs_t(("b", 7), ptB[:, 1], 3 * P)
        hi(first["bout"] + 2)
        for i in (6, 7):
            act.wait_ge(*when(("ob", i)))
            A(oh[:, 2 * i:2 * i + 2, :], two(bank[6 + i % 2][:, :]), ACT.Copy).then_inc(*did(act_steps, ("oh", "b", i)))
        for j in range(7):
            hi(first["bout"] + j + AHEAD)

        ffn(3, 8, 6, g_norm(1, 2), 6, ("chunk", first["in3"] - 1), [first["in3"] - 1 + AHEAD])
        ple(1, 9, 7, 7)

        def squares(v, s):
            for m in range(4):
                act.wait_ge(*when(("x", v, m)))
                if m == 0:
                    act.wait_ge(*when(("sums", s - 1)))
                A(sq[:, 2 * m:2 * m + 2, :], X[:, 2 * m:2 * m + 2, :], ACT.Square).then_inc(*did(act_steps, ("sq", s, m)))
            root(s)

        squares(8, 8)

        for l in range(2):
            nu, v, s = 10 + 2 * l, 9 + l, 9 + 2 * l
            squares(v, s)
            for k in range(KD):
                act.wait_ge(*when(("xn", l, k)))
                A(xh[:, k, :], sq[:, k, :], ACT.Identity, bias=mods[:, l, k:k + 1]).then_inc(*did(act_steps, ("xh", nu, k)))
            c0 = first[f"win{l}"]
            for n, (name, j) in enumerate(WIN):
                if n + AHEAD < 16:
                    hi(c0 + n + AHEAD)
                if name in ("zm", "zn"):
                    act.wait_ge(*when(("win", l, n)))
                    z = zm if name == "zm" else zn
                    A(z[:, 2 * j:2 * j + 2, :], two(bank[n % 8][:, :]), ACT.Silu).then_inc(*did(act_steps, ("z", l, n)))
                if name == "gl":
                    act.wait_ge(*when(("win", l, n)))
                    A(gates[:, :, :], two(bank[n % 8][:, 0:64])[:, :, 0:24], ACT.Sigmoid).then_inc(*did(act_steps, ("gates", l)))
            act.wait_ge(*when(("hid", l)))
            A(gh[:, 0:60], bank[0][0:DH, 0:60], ACT.Gelu_apprx_tanh).then_inc(*did(act_steps, ("gelu", l)))

            def tail(i):
                kind, m, start, stop = ITEMS[i]
                probs_t(("c", l, i), ptC[:, i % 2], 2 * P if kind == "cmp" else 3 * P)

            def y_hi(i):
                kind, m, start, stop = ITEMS[i]
                if stop:
                    k = m if kind == "moba" else 4 + m
                    act.wait_ge(*when(("y", l, k)))
                    A(xh[:, k, :], yC[:, k % 2, :], ACT.Copy).then_inc(*did(act_steps, ("yh", l, k)))

            for i, (kind, m, start, stop) in enumerate(ITEMS):
                exps(("c", l, i), 2 * (i % 2), sC[:, i % 3], nmC[:, i % 3], denC[:, i % 3], CMP_T if kind == "cmp" else None)
                if i >= 16 - AHEAD:
                    hi(first[f"wout{l}"] + i - 16 + AHEAD)
                if i >= 1:
                    tail(i - 1)
                if i >= 3:
                    y_hi(i - 3)
            tail(len(ITEMS) - 1)
            for i in range(len(ITEMS) - 3, len(ITEMS)):
                y_hi(i)
            s += 1
            for j in range(4):
                hi(first[f"wout{l}"] + j + AHEAD)
                act.wait_ge(*when(("y2", l, j)))
                A(sq[:, 2 * j:2 * j + 2, :], y2[:, 2 * j:2 * j + 2, :], ACT.Square).then_inc(*did(act_steps, ("sq", s, j)))
            root(s)
        for m in range(4):
            act.wait_ge(*when(("xout", m)))
            A(otok[:, :, T * m:T * m + T], two(bank[m][:, :]), ACT.Copy).then_inc(*did(act_steps, ("otok", m)))

    @block.tensor
    def _(pe):
        did = Steps(at)
        mm = nc.tensor.matmul
        release = {}

        def take(b):
            if b in release:
                pe.wait_ge(*when(release[b]))

        def three(out, lhs, rhs, start, stop, skip=False):
            mm(out, lhs[1], rhs[0], start=start, stop=False, skip_group_check=skip)
            mm(out, lhs[0], rhs[1], start=False, stop=False, skip_group_check=skip)
            return mm(out, lhs[0], rhs[0], start=False, stop=stop, skip_group_check=skip)

        def split(c, k, cols=None):
            pair = [slot(w, c, k) for w in (w_hi, w_lo)]
            return pair

        def sums(s):
            b = sums_bank(s)
            take(b)
            tiles = 2 if s in FOLDED else KD
            for k in range(tiles):
                pe.wait_ge(*when(("folded", s) if s in FOLDED else ("sq", s, k // 2)))
                last = mm(bank[b][:, 0:T], ones[:, :], sq[:, k, :], start=(k == 0), stop=(k == tiles - 1))
            last.then_inc(*did(pe_groups, ("sums", s)))
            release[b] = ("std", s)

        def as_they_come(b, w, waits):
            for k in range(KD):
                pe.wait_ge(*when(waits(k)))
                for n in range(2):
                    last = three(bank[b][:, n * T:(n + 1) * T], [a[:, k, n * P:(n + 1) * P] for a in w],
                                 [a[:, k, :] for a in (xh, xl)], k == 0 and n == 0, k == KD - 1, True)
            return last

        def columns(c, b, xs, waits, name, tiles=2, kd=KD, width=256):
            take(b)
            pe.wait_ge(lo_ready, 2 * (c + 1))
            w = split(c, (kd, width))
            if waits is not None:
                last = as_they_come(b, w, waits)
            else:
                for n in range(tiles):
                    for k in range(kd):
                        last = three(bank[b][:, n * T:(n + 1) * T], [a[:, k, n * P:(n + 1) * P] for a in w],
                                     [a[:, k, :] for a in xs], k == 0, k == kd - 1)
            last.then_inc(*did(pe_groups, name))
            at[("chunk", c)] = at[name]

        def tokens(c, b, xs, name, cols, kd=KD, width=256):
            take(b)
            pe.wait_ge(lo_ready, 2 * (c + 1))
            w = split(c, (kd, width))
            n = cols.stop - cols.start
            for t in range(TB):
                for k in range(kd):
                    last = three(bank[b][:, t * (512 // TB if n > 32 else 32):t * (512 // TB if n > 32 else 32) + n],
                                 [a[:, k, t * P:(t + 1) * P] for a in xs], [a[:, k, cols] for a in w], k == 0, k == kd - 1)
            last.then_inc(*did(pe_groups, name))
            at[("chunk", c)] = at[name]

        def mod_sums(f):
            take(2)
            pe.wait_ge(sem["mod_steps"], MOD_STEPS * MOD * (f + 1))
            for n in range(2 * MOD):
                last = mm(bank[2][:, n:n + 1], mod_acc[:, n // 2, n % 2 * P:n % 2 * P + P], ones[:, 0:1], start=True, stop=True)
            last.then_inc(*did(pe_groups, ("modsum", f)))
            release[2] = ("mod", f)

        xs = (xh, xl)

        def xwait(nu):
            return lambda k: ("xl", nu, k)

        def ffn(f, nu, s, aside=None):
            c = first[f"in{f}"]
            n0 = PAIRS * f
            for b in range(4):
                take(b)

            def half(c, b, waits, it=None):
                pe.wait_ge(lo_ready, 2 * (c + 1) + (0 if it is None else 8 * it))
                w = split(c, (KD, 256))
                if waits:
                    return as_they_come(b, w, xwait(nu))
                for n in range(2):
                    for k in range(KD):
                        last = three(bank[b][:, n * T:(n + 1) * T], [a[:, k, n * P:(n + 1) * P] for a in w],
                                     [a[:, k, :] for a in xs], k == 0, k == KD - 1)
                return last

            half(c, 0, True).then_inc(*did(pe_groups, ("gate", f)))
            at[("chunk", c)] = at[("gate", f)]
            half(c + 1, 1, False).then_inc(*did(pe_groups, ("up", f)))
            at[("chunk", c + 1)] = at[("up", f)]
            if s is not None:
                sums(s)
            if aside is not None:
                aside()
            with pe.Fori(0, (PAIRS - 1) // 2) as it:
                for j in range(2):
                    p = 1 + j
                    b = 2 * (p % 2)
                    pe.wait_ge(gate_scaled, n0 + p + 2 * it)
                    half(c + 2 + 2 * j, b, False, it).then_inc(*did(pe_groups))
                    pe.wait_ge(up_scaled, n0 + p + 2 * it)
                    half(c + 3 + 2 * j, b + 1, False, it).then_inc(*did(pe_groups))
            start = did.count["pe_groups"] - 4
            for n in range(2 * (PAIRS - 1)):
                at[("chunk", c + 2 + n)] = ("pe_groups", start + 1 + n)
            did.skip(pe_groups, 2 * (PAIRS - 1) - 4)
            for b in range(2):
                release[b], release[2 + b] = ("ffn_" + "gu"[b], f, PAIRS - 1), ("ffn_" + "gu"[b], f, PAIRS - 2)
            c = first[f"out{f}"]
            for b in range(4, 8):
                take(b)

            def rows(c, q, it=None, only=None):
                pe.wait_ge(lo_ready, 2 * (c + 1) + (0 if it is None else 8 * it))
                pe.wait_ge(hidden_lo, n0 + q + 1 + (0 if it is None else 4 * it))
                w = split(c, (2, D))
                for n in range(KD):
                    for k in range(2):
                        kk = 2 * q + k if it is None else bass.ds(2 * q + k + 8 * it, 1)
                        xk = [a[:, kk, :] if it is None else a[:, kk, :].rearrange("p a n -> p (a n)") for a in (hh, hl)]
                        last = three(bank[4 + n // 2][:, (n % 2) * T:(n % 2 + 1) * T], [a[:, k, n * P:(n + 1) * P] for a in w],
                                     xk, it is None and q == 0 and n % 2 == 0 and k == 0, q == PAIRS - 1 and k == 1, True)
                    if q == PAIRS - 1 and n % 2:
                        last.then_inc(*did(pe_groups, ("ffn_out", f, n // 2)))
                return last

            for q in range(2):
                rows(c + q, q).then_inc(*did(pe_groups, ("chunk", c + q)))
            with pe.Fori(0, 2) as it:
                for q in range(4):
                    rows(c + 2 + q, 2 + q, it).then_inc(*did(pe_groups))
            start = at[("chunk", c + 1)][1]
            for n in range(8):
                at[("chunk", c + 2 + n)] = ("pe_groups", start + 1 + n)
            did.skip(pe_groups, 4)
            rows(c + PAIRS - 1, PAIRS - 1)
            at[("chunk", c + PAIRS - 1)] = at[("ffn_out", f, 3)]
            for m in range(4):
                release[4 + m] = ("x", {0: 1, 1: 3, 2: 5, 3: 7}[f], m)

        pe.wait_ge(sem["gains_landed"], 16 * 8)
        nc.tensor.transpose(bank[4][:, 0:103], vrow0[0:103, :], ident[0:103, 0:103]).then_inc(*did(pe_groups, ("cols", 0)))
        release[4] = ("col", 0)
        pe.wait_ge(sem["x_landed"], 16)
        for m in range(4):
            for n in range(2):
                for t in range(TB):
                    k = 2 * m + n
                    last = nc.tensor.transpose(bank[m][:, n * T + t * P:n * T + t * P + P], xtok[:, t, k * P:(k + 1) * P], ident)
            last.then_inc(*did(pe_groups, ("xin", m)))
            release[m] = ("x", 0, m)
        pe.wait_ge(*when("memsets"))

        def aside():
            pe.wait_ge(sem["others_landed"], 16 * 8)
            for n, (rows_, cnt) in ((1, (vrow1, 88)), (2, (vrow2, 64))):
                nc.tensor.transpose(bank[4 + n][:, 0:cnt], rows_[0:cnt, :], ident[0:cnt, 0:cnt]).then_inc(*did(pe_groups, ("cols", n)))
                release[4 + n] = ("col", n)

        def positions():
            take(7)
            pe.wait_ge(*when("pos_f"))
            mm(bank[7][:, 0:T], ones[0:1, :], turns[0:1, :], start=True, stop=True).then_inc(*did(pe_groups, "pos"))
            release[7] = "ang0"

        ffn(0, 0, 0, aside)

        c0 = first["hgrn"]
        for j in range(4):
            columns(c0 + j, 4 + j, xs, xwait(1) if j == 0 else None, ("pf", j))
            release[4 + j] = ("f", j)
            if j == 1:
                sums(1)
                mod_sums(0)
        for j in range(4):
            columns(c0 + 4 + j, 4 + j, xs, None, ("pq", j))
            release[4 + j] = ("q", j)
        pe.wait_ge(*when(("rs", 1)))
        take(3)
        for t in range(TB):
            last = nc.tensor.transpose(bank[3][:, t * P:(t + 1) * P], rs[:, t * P:(t + 1) * P], ident)
        last.then_inc(*did(pe_groups, "rst"))
        release[3] = "rst_copy"

        def scores(name, lhs, rhs, done):
            for m in range(4):
                take(m)
                for n in range(4):
                    h, t = 2 * m + n // 2, n % 2
                    last = mm(bank[m][:, n * P:(n + 1) * P], lhs[:, h, t * P:(t + 1) * P], rhs[:, h, t * P:(t + 1) * P], start=True, stop=True)
                last.then_inc(*did(pe_groups, (name, m)))
                release[m] = (done, m)

        pe.wait_ge(*when("k"))
        scores("diag", hg_k, hg_q, "diag_in")

        def level(n):
            L, f = LEVELS[n], hg_f[n % 2]
            for m in range(2):
                pe.wait_ge(*when(("factors", n, m)))
                b = 2 * (n % 2) + m
                take(b)
                for i in range(8):
                    h, t = 4 * m + i // 2, i % 2
                    keys = f[:, h, t * P:(t + 1) * P]
                    queries = keys.rearrange("p (b two n) -> p b two n", two=2, n=L)[:, :, 1, :]
                    last = mm(bank[b][:, i * P // 2:(i + 1) * P // 2], keys, queries, start=True, stop=True)
                last.then_inc(*did(pe_groups, (("lev", n), m)))
                release[b] = (("merge", n), m)

        for n in range(8):
            c, j = c0 + 8 + n, n % 4
            if n < 4:
                tokens(c, 4 + j, xs, ("pi", j), slice(0, 256))
                release[4 + j] = ("vi", j)
            else:
                columns(c, 4 + j, xs, None, ("pg", j))
                release[4 + j] = ("g", j)
            if n < 7:
                level(n)
        for m in range(2):
            pe.wait_ge(*when(("factors", 7, m)))
            take(m)
            for n in range(4):
                h = 4 * m + n
                last = mm(bank[m][:, n * P:(n + 1) * P], hg_f[1][:, h, 0:P], hg_f[1][:, h, P:T], start=True, stop=True)
            last.then_inc(*did(pe_groups, ("cross", m)))
            release[m] = ("cross_in", m)
        pe.wait_ge(*when(("cross_in", 1)))
        for m in range(4):
            take(4 + m)
            for n in range(2):
                h = 2 * m + n
                o = bank[4 + m][:, n * T:(n + 1) * T]
                v = [hg_v[:, t, h * P:(h + 1) * P] for t in range(TB)]
                mm(o[:, 0:P], v[0], hg_s[:, h, 0, :], start=True, stop=True)
                mm(o[:, P:T], v[0], hg_x[:, h, :], start=True, stop=False)
                last = mm(o[:, P:T], v[1], hg_s[:, h, 1, :], start=False, stop=True)
            last.then_inc(*did(pe_groups, ("o", m)))
            release[4 + m] = ("og1", m)
        for m in range(4):
            take(m)
            pe.wait_ge(*when(("osq", m)))
            mm(bank[m][:, :], ones[:, :], sq[:, 2 * m:2 * m + 2, :].rearrange("p a n -> p (a n)"), start=True, stop=True).then_inc(*did(pe_groups, ("osum", m)))
            release[m] = ("oln", m)
        for j in range(4):
            columns(first["aout"] + j, 4 + j, xs, (lambda k: ("ol", k // 2)) if j == 0 else None, ("aout", j))
            release[4 + j] = ("x", 2, j)

        ffn(1, 3, 2, positions)

        def ple(l, nu, v, s):
            c = first[f"ple{l}"]
            pe.wait_ge(sem["ple_landed"], 32)
            take(4)
            for k in range(2):
                for t in range(TB):
                    last = nc.tensor.transpose(bank[4][:, k * T + t * P:k * T + t * P + P], ptok[:, l, t, k * P:(k + 1) * P], ident)
            last.then_inc(*did(pe_groups, ("ptin", l)))
            release[4] = ("pt", l)
            pe.wait_ge(lo_ready, 2 * (c + 1))
            pe.wait_ge(*when(("ptl", l)))
            w = split(c, (2, D))
            for m in range(4):
                take(m)
                for n in (2 * m, 2 * m + 1):
                    for k in range(2):
                        last = three(bank[m][:, (n % 2) * T:(n % 2 + 1) * T], [a[:, k, n * P:(n + 1) * P] for a in w],
                                     [pth[:, k, :], ptl[:, k, :]], k == 0, k == 1)
                last.then_inc(*did(pe_groups, ("pp", l, m)))
                release[m] = ("ppc", l, m)
            at[("chunk", c)] = at[("pp", l, 3)]
            for j in range(4):
                columns(c + 1 + j, 4 + j, xs, xwait(nu) if j == 0 else None, ("pgate", l, j))
                release[4 + j] = ("pg", l, j)
                if j == 1:
                    sums(s)
                    mod_sums(2 * l + 1)

        ple(0, 4, 3, 3)

        c = first["kvd"]
        columns(c, 4, xs, xwait(5), "kd0")
        release[4] = "ck"
        sums(4)
        take(5)
        pe.wait_ge(lo_ready, 2 * (c + 2))
        w = split(c + 1, (KD, P))
        for k in range(KD):
            last = three(bank[5][:, 0:T], [a[:, k, :] for a in w], [a[:, k, :] for a in xs], k == 0, k == KD - 1)
        last.then_inc(*did(pe_groups, ("chunk", c + 1)))
        release[5] = "kr"
        take(6)
        pe.wait_ge(*when("cksq"))
        for k in range(2):
            last = mm(bank[6][:, 0:T], ones[:, :], sq[:, k, :], start=(k == 0), stop=(k == 1))
        last.then_inc(*did(pe_groups, "cksum"))
        release[6] = "ckstd"
        take(7)
        pe.wait_ge(*when("kr"))
        mm(bank[7][:, 0:T], const[:, C_PERM:C_PERM + P], kr[:, :], start=True, stop=True).then_inc(*did(pe_groups, "krswap"))
        release[7] = "kr_sin"

        ffn(2, 6, None)

        for j in range(2):
            columns(first["dq"] + j, 4 + j, xs, xwait(7) if j == 0 else None, ("dq", j))
            release[4 + j] = ("cq", j)
            if j == 1:
                sums(5)
                mod_sums(2)
        pe.wait_ge(*when("ckl"))
        for u in range(4):
            c = first["kvup"] + u
            pe.wait_ge(lo_ready, 2 * (c + 1))
            w = split(c, (2, D))
            b0 = 4 * (u % 2)
            for n in range(2):
                take(b0 + n)
                for h in (2 * n, 2 * n + 1):
                    for k in range(2):
                        last = three(bank[b0 + n][:, (h % 2) * T:(h % 2 + 1) * T], [a[:, k, h * 256:h * 256 + P] for a in w],
                                     [ckh[:, k, :], ckl[:, k, :]], k == 0, k == 1)
                last.then_inc(*did(pe_groups, ("k", u, n)))
                release[b0 + n] = ("kn", u, n)
            for t in range(TB):
                take(b0 + 2 + t)
                for k in range(2):
                    vw = [a[:, k, :].rearrange("p (h e) -> p h e", h=4)[:, :, NOPE:NOPE + VDIM] for a in w]
                    last = three(bank[b0 + 2 + t][:, :], [a[:, k, t * P:(t + 1) * P] for a in (ckh, ckl)], vw, k == 0, k == 1)
                last.then_inc(*did(pe_groups, ("v", u, t)))
                release[b0 + 2 + t] = ("vb", u, t)
            at[("chunk", c)] = at[("v", u, 1)]
            if u == 0:
                take(4)
                for k in range(4):
                    pe.wait_ge(*when(("cqsq", k // 2)))
                    last = mm(bank[4][:, 0:T], ones[:, :], sq[:, k, :], start=(k == 0), stop=(k == 3))
                last.then_inc(*did(pe_groups, "cqsum"))
                release[4] = "cqstd"

        def swap(u):
            b = 4 + u % 2
            take(b)
            pe.wait_ge(*when(("qraw", u)))
            mm(bank[b][:, 0:T], const[:, C_PERM:C_PERM + P], qraw[:, u % 2, :], start=True, stop=True).then_inc(*did(pe_groups, ("qswap", u)))
            release[b] = ("q_sin", u)

        for u in range(8):
            c = first["uq"] + u
            pe.wait_ge(lo_ready, 2 * (c + 1))
            w = split(c, (4, 384))
            b0 = 2 * (u % 2)
            take(b0)
            for h in range(2):
                for k in range(4):
                    if u == 0 and h == 0:
                        pe.wait_ge(*when(("cql", k)))
                    last = three(bank[b0][:, h * T:(h + 1) * T], [a[:, k, h * NOPE:(h + 1) * NOPE] for a in w],
                                 [cqh[:, k, :], cql[:, k, :]], k == 0, k == 3)
            last.then_inc(*did(pe_groups, ("qnope", u)))
            release[b0] = ("qn", u)
            take(b0 + 1)
            for k in range(4):
                last = three(bank[b0 + 1][:, 0:T], [a[:, k, 2 * NOPE:] for a in w], [cqh[:, k, :], cql[:, k, :]], k == 0, k == 3)
            last.then_inc(*did(pe_groups, ("chunk", c)))
            release[b0 + 1] = ("qraw", u)
            if u >= 1:
                swap(u - 1)
        swap(7)

        def transposes(item, p):
            for h in range(2):
                take(4 + h)
            pe.wait_ge(*when(("probs", item)))
            for h in range(2):
                for n, (src, dst) in enumerate(((0, 0), (1, 1), (2, 2))):
                    last = nc.tensor.transpose(bank[4 + h][:, dst * P:(dst + 1) * P], p[:, h, src * P:(src + 1) * P], ident)
                release[4 + h] = ("ptcopy", item)
            last.then_inc(*did(pe_groups, ("pt", item)))

        def scores_b(i):
            pe.wait_ge(*when(("qr", i)))
            b0 = 2 * (i % 2)
            for t in range(TB):
                b = b0 + t
                take(b)
                n = (t + 1) * P
                o = bank[b][:, 0:2 * n]
                mm(o, qr[:, i, t * P:(t + 1) * P], krz[:, :, 0:n], start=True, stop=False, skip_group_check=True)
                for h in range(2):
                    mm(o[:, h * n:(h + 1) * n], qn[:, 2 * i + h, t * P:(t + 1) * P], kn[:, 2 * i + h, 0:n],
                       start=False, stop=(t == 1), skip_group_check=True)
                own = two(o)[:, :, t * P:n]
                last = mm(own, ident_bf[:, :], rep(caus_bf[:, :], 2), start=False, stop=True, skip_group_check=True)
                last.then_inc(*did(pe_groups, ("s", ("b", i), t)))
                release[b] = ("exps", ("b", i))

        def values_b(i):
            pe.wait_ge(*when(("ptcopy", ("b", i))))
            b = 6 + i % 2
            take(b)
            for h in range(2):
                o = bank[b][:, h * T:(h + 1) * T]
                v = [vb[:, t, (2 * i + h) * VDIM:(2 * i + h + 1) * VDIM] for t in range(TB)]
                mm(o[:, 0:P], v[0], ptB[:, i % 2, h, 0:P], start=True, stop=True)
                mm(o[:, P:T], v[0], ptB[:, i % 2, h, P:T], start=True, stop=False)
                last = mm(o[:, P:T], v[1], ptB[:, i % 2, h, T:T + P], start=False, stop=True)
            last.then_inc(*did(pe_groups, ("ob", i)))
            release[b] = ("ol", "b", i)

        scores_b(0)
        scores_b(1)
        for i in range(8):
            if i < 6:
                scores_b(i + 2)
            if i >= 1:
                values_b(i - 1)
            transposes(("b", i), sB[:, i % 3])
        values_b(7)
        c0 = first["bout"]
        for b in range(4):
            take(b)
        for q in range(8):
            pe.wait_ge(lo_ready, 2 * (c0 + q + 1))
            pe.wait_ge(*when(("ol", "b", q)))
            w = split(c0 + q, (2, D))
            for n in range(KD):
                for k in range(2):
                    last = three(bank[n // 2][:, (n % 2) * T:(n % 2 + 1) * T], [a[:, k, n * P:(n + 1) * P] for a in w],
                                 [oh[:, 2 * q + k, :], ol[:, 2 * q + k, :]], q == 0 and n % 2 == 0 and k == 0, q == 7 and k == 1, True)
                if q == 7 and n % 2:
                    last.then_inc(*did(pe_groups, ("bout", n // 2)))
            if q < 7:
                last.then_inc(*did(pe_groups, ("chunk", c0 + q)))
        at[("chunk", c0 + 7)] = at[("bout", 3)]
        for m in range(4):
            release[m] = ("x", 6, m)

        ffn(3, 8, 6)
        ple(1, 9, 7, 7)
        sums(8)

        for l in range(2):
            nu, v, s = 10 + 2 * l, 9 + l, 9 + 2 * l
            sums(s)
            c0 = first[f"win{l}"]
            for n, (name, j) in enumerate(WIN):
                c, b = c0 + n, n % 8
                key = ("win", l, n)
                if name in ("qm", "km", "qn", "zm", "zn"):
                    columns(c, b, xs, xwait(nu) if n == 0 else None, key)
                    release[b] = ("z", l, n) if name[0] == "z" else ("proj", l, n)
                elif name == "vm":
                    tokens(c, b, xs, key, slice(0, 256))
                    release[b] = ("proj", l, n)
                elif name == "gl":
                    tokens(c, b, xs, key, slice(0, 24), width=24)
                    release[b] = ("gates", l)
                elif name == "kcvc":
                    columns(c, b, xs, None, key)
                    release[b] = ("proj", l, n)
                else:
                    take(b)
                    pe.wait_ge(lo_ready, 2 * (c + 1))
                    w = split(c, (KD, 256))
                    for k in range(KD):
                        three(bank[b][:, 0:T], [a[:, k, 0:P] for a in w], [a[:, k, :] for a in xs], k == 0, k == KD - 1)
                    for t in range(TB):
                        for k in range(KD):
                            last = three(bank[b][:, T + t * P:T + (t + 1) * P], [a[:, k, t * P:(t + 1) * P] for a in xs],
                                         [a[:, k, P:2 * P] for a in w], k == 0, k == KD - 1)
                    last.then_inc(*did(pe_groups, key))
                    at[("chunk", c)] = at[key]
                    release[b] = ("proj", l, n)
                if name in ("ksvs", "gl"):
                    half_ = 0 if name == "ksvs" else 1
                    take(half_)
                    pe.wait_ge(*when(("kA", l, half_)))
                    mm(bank[half_][:, :], const[:, C_SWAP:C_SWAP + P], kA[:, 2 * half_:2 * half_ + 2, :].rearrange("p a n -> p (a n)"),
                       start=True, stop=True).then_inc(*did(pe_groups, ("kB", l, half_)))
                    release[half_] = ("kB_used", l, half_)
            take(0)
            pe.wait_ge(sem["cmp_landed"], 80 * (l + 1))
            for kv in range(2):
                pe.wait_ge(*when(("windows", l, kv)))
                for r in range(16):
                    last = mm(bank[0][0:DH, 30 * kv:30 * kv + 30], wc1[:, kv, r, :], win[:, kv, r, :], start=(r == 0), stop=(r == 15))
            last.then_inc(*did(pe_groups, ("hid", l)))
            release[0] = ("gelu", l)
            take(1)
            pe.wait_ge(*when(("gelu", l)))
            mm(bank[1][:, 0:30], wc2[:, 0:2, :].rearrange("p a n -> p (a n)"), gh[:, 0:30], start=True, stop=True).then_inc(*did(pe_groups, ("kcmp", l)))
            release[1] = ("kcz", l)
            take(2)
            for g in range(GROUPS):
                last = mm(bank[2][0:CMP_T, g * DH:(g + 1) * DH], gh[:, 30 + 15 * g:45 + 15 * g], wc2[:, 2, :], start=True, stop=True)
            last.then_inc(*did(pe_groups, ("vcmp", l)))
            release[2] = ("vcz", l)

            def scores_c(i):
                kind, m, _, _ = ITEMS[i]
                g = m // 2
                q = qm if kind == "moba" else qs
                b0 = 2 * (i % 2)
                if i == 0:
                    pe.wait_ge(*when(("attn", l)))
                    pe.wait_ge(*when(("z", l, 15)))
                if kind == "cmp":
                    take(b0)
                    for t in range(TB):
                        last = mm(bank[b0][:, t * 2 * CMP_T:(t + 1) * 2 * CMP_T], q[:, m, t * P:(t + 1) * P], kcz[:, g, :, 0:CMP_T], start=True, stop=False)
                        last = mm(bank[b0][:, t * 2 * CMP_T:(t + 1) * 2 * CMP_T], ident_bf[:, :], cbias[:, 2 * m:2 * m + 2, t, :], start=False, stop=True)
                    last.then_inc(*did(pe_groups, ("s", ("c", l, i), 1)))
                    release[b0] = ("exps", ("c", l, i))
                    return
                kz = {"moba": kmz[:, m], "slc": ksz[:, g], "win": kwz[:, g]}[kind]
                for t in range(TB):
                    b, n = b0 + t, (t + 1) * P
                    take(b)
                    mm(bank[b][:, 0:2 * n], q[:, m, t * P:(t + 1) * P], kz[:, :, 0:n], start=True, stop=False)
                    mm(bank[b][:, 0:2 * n], ident_bf[:, :], bias[:, 2 * m:2 * m + 2, T - n:T], start=False, stop=True).then_inc(*did(pe_groups, ("s", ("c", l, i), t)))
                    release[b] = ("exps", ("c", l, i))

            def transposes_c(i):
                if ITEMS[i][0] != "cmp":
                    return transposes(("c", l, i), sC[:, i % 3])
                for h in range(2):
                    take(4 + h)
                pe.wait_ge(*when(("probs", ("c", l, i))))
                for h in range(2):
                    for t in range(TB):
                        last = nc.tensor.transpose(bank[4 + h][0:16, t * P:(t + 1) * P], sC[:, i % 3, h, 16 * t:16 * t + 16], ident)
                    release[4 + h] = ("ptcopy", ("c", l, i))
                last.then_inc(*did(pe_groups, ("pt", ("c", l, i))))

            def values_c(i):
                kind, m, start, stop = ITEMS[i]
                g = m // 2
                k = m if kind == "moba" else 4 + m
                b = 6 + k % 2
                pe.wait_ge(*when(("ptcopy", ("c", l, i))))
                if start:
                    take(b)
                o = bank[b][:, 0:T]
                for h in range(2):
                    if kind == "cmp":
                        last = mm(o, vcz[0:CMP_T, g, h, :], ptC[0:CMP_T, i % 2, h, 0:T], start=False, stop=(h == 1), skip_group_check=True)
                        continue
                    v = {"moba": [vmz[:, t, 2 * m + h, :] for t in range(TB)],
                         "slc": [vsz[:, t, g, h, :] for t in range(TB)], "win": [vwz[:, t, g, h, :] for t in range(TB)]}[kind]
                    block0 = lambda: mm(o, v[0], ptC[:, i % 2, h, 0:T], start=(start and h == 0), stop=(stop and h == 1), skip_group_check=True)
                    block1 = lambda: mm(o[:, P:T], v[1], ptC[:, i % 2, h, T:T + P], start=False, stop=False, skip_group_check=True)
                    for product in ((block0, block1) if h == 0 else (block1, block0)):
                        last = product()
                last.then_inc(*did(pe_groups, ("oc", l, i)))
                if stop:
                    release[b] = ("y", l, k)

            scores_c(0)
            scores_c(1)
            for i in range(len(ITEMS)):
                if i + 2 < len(ITEMS):
                    scores_c(i + 2)
                if i >= 1:
                    values_c(i - 1)
                transposes_c(i)
            values_c(len(ITEMS) - 1)
            for j in range(4):
                columns(first[f"wout{l}"] + j, j, xs, (lambda k: ("yl", l, k)) if j == 0 else None, ("wout", l, j))
                release[j] = ("y2", l, j)
            sums(s + 1)
        for m in range(4):
            take(m)
            pe.wait_ge(*when(("x", 11, m)))
            for t in range(TB):
                for k in (2 * m, 2 * m + 1):
                    last = nc.tensor.transpose(bank[m][:, t * T + k % 2 * P:t * T + k % 2 * P + P], X[:, k, t * P:(t + 1) * P], ident)
            last.then_inc(*did(pe_groups, ("xout", m)))

    @block.vector
    def _(dve):
        did = Steps(at)
        V = nc.vector

        def lo(c, it=None):
            if c >= n_chunks:
                return
            for h in range(2):
                dve.wait_ge(hi_ready, 2 * c + h + 1 + (0 if it is None else 8 * it))
                cols = half_columns(c, h)
                V.tensor_tensor(w_lo[:, c % NSLOT, cols], w_raw[:, c % NRAW, cols], f32(w_hi[:, c % NSLOT, cols]), ALU.subtract).then_inc(*did(lo_ready))

        def norm(nu, gain, late=()):
            for k in range(KD):
                dve.wait_ge(*when(("xh", nu, k)))
                V.scalar_tensor_tensor(xl[:, k, :], X[:, k, :], gain(k), f32(xh[:, k, :]), ALU.mult, ALU.subtract).then_inc(*did(dve_steps, ("xl", nu, k)))
            for c in late:
                lo(c)

        def inv(s):
            dve.wait_ge(*when(("std", s)))
            dve.wait_ge(*did.last)
            V.reciprocal(rs[:, :], std[:, :]).then_inc(*did(dve_steps, ("rs", s)))
            dve.wait_ge(*did.last)

        def modulation(f):
            dve.wait_ge(*when(("modsum", f)))
            n = slice(2 * MOD * f, 2 * MOD * (f + 1))
            V.tensor_tensor(mods[:, :, :].rearrange("p l n -> p (l n)")[:, n], bank[2][:, 0:2 * MOD], col1[:, n], ALU.add).then_inc(*did(dve_steps, ("mod", f)))

        def ffn(f, nu, v, gain, s, late=(), aside=None):
            norm(nu, gain, late)
            c = first[f"in{f}"]
            n0 = PAIRS * f
            group0 = when(("gate", f))[1]
            up0 = when(("up", f))[1]
            pairs0 = when(("chunk", c + 2))[1] - 1

            def pair(c, p, it=None):
                o = 0 if it is None else 2 * it
                o4 = 0 if it is None else 4 * it
                b = 2 * (p % 2)
                lo(c + AHEAD, it)
                if it is None:
                    lo(c + 1 + AHEAD)
                    if s is not None:
                        inv(s)
                dve.wait_ge(pe_groups, (group0 if p == 0 else pairs0 + 2 * p - 1) + o4)
                if it is not None or p >= 2:
                    dve.wait_ge(silu_ready, n0 + max(p - 1, 1) + o)
                V.tensor_tensor(gate_t[:, p % 2, :, :], two(bank[b][:, :]), rep(rs[:, :], 2), ALU.mult).then_inc(*did(gate_scaled))
                if it is not None:
                    lo(c + 1 + AHEAD, it)
                dve.wait_ge(pe_groups, (up0 if p == 0 else pairs0 + 2 * p) + o4)
                if it is not None or p >= 2:
                    dve.wait_ge(hidden_ready, n0 + max(p - 1, 1) + o)
                V.tensor_tensor(up_t[:, p % 2, :, :], two(bank[b + 1][:, :]), rep(rs[:, :], 2), ALU.mult).then_inc(*did(up_scaled))
                dve.wait_ge(silu_ready, n0 + p + 1 + o)
                dve.wait_ge(up_scaled, n0 + p + 2 + o)
                if it is not None or p >= 2:
                    dve.wait_ge(hidden_hi, n0 + max(p - 1, 1) + o)
                    dve.wait_ge(hidden_lo, n0 + max(p - 1, 1) + o)
                V.tensor_tensor(hid_t[:, p % 2, :, :], silu_t[:, p % 2, :, :], up_t[:, p % 2, :, :], ALU.mult).then_inc(*did(hidden_ready))
                dve.wait_ge(hidden_hi, n0 + p + 1 + o)
                k = bass.ds(2 * p + (0 if it is None else 4 * it), 2)
                V.tensor_tensor(hl[:, k, :], hid_t[:, p % 2, :, :], f32(hh[:, k, :]), ALU.subtract).then_inc(*did(hidden_lo))

            pair(c, 0)
            if aside is not None:
                aside()
            with dve.Fori(0, (PAIRS - 1) // 2) as it:
                for j in range(2):
                    pair(c + 2 + 2 * j, 1 + j, it)
            turns_left = (PAIRS - 1) // 2 - 1
            did.skip(lo_ready, 8 * turns_left)
            for q in (gate_scaled, up_scaled, hidden_ready, hidden_lo):
                did.skip(q, 2 * turns_left)
            for p in (PAIRS - 2, PAIRS - 1):
                at[("ffn_g", f, p)], at[("ffn_u", f, p)] = ("gate_scaled", n0 + p + 2), ("up_scaled", n0 + p + 2)
            c = first[f"out{f}"]
            for q in range(2):
                lo(c + q + AHEAD)
            with dve.Fori(0, 2) as it:
                for q in range(4):
                    lo(c + 2 + q + AHEAD, it)
            did.skip(lo_ready, 8)
            for m in range(4):
                dve.wait_ge(*when(("ffn_out", f, m)))
                V.scalar_tensor_tensor(X[:, 2 * m:2 * m + 2, :], two(bank[4 + m][:, :]), 0.5, X[:, 2 * m:2 * m + 2, :], ALU.mult, ALU.add).then_inc(*did(dve_steps, ("x", v + 1, m)))

        dve.wait_ge(*when(("cols", 0)))
        V.tensor_copy(col0[:, 0:103], bank[4][:, 0:103]).then_inc(*did(dve_steps, ("col", 0)))
        for m in range(4):
            dve.wait_ge(*when(("xin", m)))
            V.tensor_copy(X[:, 2 * m:2 * m + 2, :], two(bank[m][:, :])).then_inc(*did(dve_steps, ("x", 0, m)))
        V.memset(small[:, 50:51], 0.0).then_inc(*did(gate_scaled))
        V.memset(small[:, 51:52], 0.0).then_inc(*did(up_scaled))
        lo(0)

        def aside():
            dve.wait_ge(sem["others_landed"], 16 * 8)
            V.tensor_copy(turns[0:1, :], pos_i[0:1, :]).then_inc(*did(dve_steps, "pos_f"))
            V.tensor_copy(ident_bf[:, :], ident).then_inc(*did(dve_steps))
            V.tensor_copy(caus_bf[:, :], const[:, C_CAUS:C_CAUS + P]).then_inc(*did(dve_steps))
            for n, (col, cnt) in ((1, (col1, 88)), (2, (col2, 64))):
                dve.wait_ge(*when(("cols", n)))
                V.tensor_copy(col[:, 0:cnt], bank[4 + n][:, 0:cnt]).then_inc(*did(dve_steps, ("col", n)))
            V.tensor_max(small[:, 32:40], col0[:, 64:72], col0[:, 72:80]).then_inc(*did(dve_steps))
            dve.wait_ge(*did.last)
            V.tensor_tensor(two(small[:, 0:16]), two(col0[:, 64:80]), rep(small[:, 32:40], 2), ALU.subtract).then_inc(*did(dve_steps, "lb_shift"))
            dve.wait_ge(*when("lb_exp"))
            V.tensor_tensor(small[:, 32:40], small[:, 16:24], small[:, 24:32], ALU.add).then_inc(*did(dve_steps))
            dve.wait_ge(*did.last)
            V.reciprocal(small[:, 40:48], small[:, 32:40]).then_inc(*did(dve_steps))
            dve.wait_ge(*did.last)
            V.tensor_tensor(lb[:, :], small[:, 16:24], small[:, 40:48], ALU.mult).then_inc(*did(dve_steps))
            dve.wait_ge(*did.last)
            V.tensor_scalar(oml[:, :], lb[:, :], -1.0, 1.0, ALU.mult, ALU.add).then_inc(*did(dve_steps, "lb"))

        def angles():
            dve.wait_ge(*when("pos"))
            V.tensor_scalar(ang[:, :], bank[7][:, 0:T], const[:, C_FREQ:C_FREQ + 1], None, ALU.mult).then_inc(*did(dve_steps, "ang0"))
            dve.wait_ge(*did.last)
            V.tensor_scalar(turns[:, :], ang[:, :], float(1 / (2 * np.pi)), None, ALU.mult).then_inc(*did(dve_steps))
            big = float(1.5 * 2 ** 23)
            for step in (big, -big):
                dve.wait_ge(*did.last)
                V.tensor_scalar(turns[:, :], turns[:, :], step, None, ALU.add).then_inc(*did(dve_steps))
            part1 = 6.28125
            part2 = float(np.float32(np.round((2 * np.pi - part1) * 2 ** 20) / 2 ** 20))
            part3 = float(np.float32(2 * np.pi - part1 - part2))
            src = ang
            for part in (part1, part2, part3):
                dve.wait_ge(*did.last)
                V.scalar_tensor_tensor(red[:, :], turns[:, :], -part, src[:, :], ALU.mult, ALU.add).then_inc(*did(dve_steps))
                src = red
            dve.wait_ge(*did.last)
            V.tensor_scalar(red[:, :], red[:, :], 3.1415925, -3.1415925, ALU.min, ALU.max).then_inc(*did(dve_steps, "angles"))
            dve.wait_ge(*did.last)
            V.tensor_scalar(mag[:, :], red[:, :], -1.0, None, ALU.mult).then_inc(*did(dve_steps))
            dve.wait_ge(*did.last)
            V.tensor_tensor(mag[:, :], mag[:, :], red[:, :], ALU.max).then_inc(*did(dve_steps))
            dve.wait_ge(*did.last)
            V.tensor_scalar(mag[:, :], mag[:, :], -1.0, float(np.pi / 2), ALU.mult, ALU.add).then_inc(*did(dve_steps, "quarter"))
            dve.wait_ge(*when("sin"))
            V.tensor_scalar(sin[:, :], sin[:, :], const[:, C_SIGN:C_SIGN + 1], None, ALU.mult).then_inc(*did(dve_steps, "rope"))

        ffn(0, 0, 0, g_norm(0, 0), 0, range(1, AHEAD), aside)

        c0 = first["hgrn"]
        norm(1, g_norm(0, 1), [c0 - 1 + AHEAD])
        for j in range(4):
            if j != 1:
                lo(c0 + j + AHEAD)
            if j == 0:
                lo(c0 + 1 + AHEAD)
                inv(1)
            dve.wait_ge(*when(("pf", j)))
            if j == 2:
                modulation(0)
            V.tensor_tensor(hg_a[:, 2 * j:2 * j + 2, :], two(bank[4 + j][:, :]), rep(rs[:, :], 2), ALU.mult).then_inc(*did(dve_steps, ("f", j)))
        for j in range(4):
            lo(c0 + 4 + j + AHEAD)
            dve.wait_ge(*when(("pq", j)))
            V.scalar_tensor_tensor(hg_q[:, 2 * j:2 * j + 2, :], two(bank[4 + j][:, :]), float(P ** -0.5), rep(rs[:, :], 2), ALU.mult, ALU.mult).then_inc(*did(dve_steps, ("q", j)))
            dve.wait_ge(*when(("sg", j)))
            for h in (2 * j, 2 * j + 1):
                V.tensor_scalar(hg_k[:, h, :], hg_k[:, h, :], oml[:, h:h + 1], None, ALU.mult).then_inc(*did(dve_steps, "k"))
        for h in range(HEADS_A):
            dve.wait_ge(*when(("ln", h)))
            V.tensor_tensor_scan(hg_b[:, h, :], const[:, C_RESET:C_RESET + T], hg_a[:, h, :], 0.0, ALU.mult, ALU.add).then_inc(*did(dve_steps, "scans"))
        dve.wait_ge(*when("rst"))
        V.tensor_copy(rst[:, :], two(bank[3][:, 0:T])[:, :, 0:1].rearrange("p a n -> p (a n)")).then_inc(*did(dve_steps, "rst_copy"))
        dve.wait_ge(*did.last)

        def factors(n):
            L = LEVELS[n] if n < 7 else P
            for half, hs in enumerate((slice(0, 4), slice(4, 8))):
                dve.wait_ge(*when(("exp", n, half)))
                halves = [t[:, hs, :].rearrange("p h n -> p (h n)").rearrange("p (b two n) -> p b two n", two=2, n=L) for t in (hg_f[n % 2], hg_k, hg_q)]
                V.tensor_tensor(halves[0][:, :, 0, :], halves[0][:, :, 0, :], halves[1][:, :, 0, :], ALU.mult).then_inc(*did(dve_steps))
                V.tensor_tensor(halves[0][:, :, 1, :], halves[0][:, :, 1, :], halves[2][:, :, 1, :], ALU.mult).then_inc(*did(dve_steps, ("factors", n, half)))

        def diag_view(m):
            return hg_s[:, 2 * m:2 * m + 2, :, :]

        for m in range(4):
            dve.wait_ge(*when(("diag", m)))
            V.tensor_tensor(diag_view(m), bank[m][:, :].rearrange("p (h t n) -> p h t n", h=2, t=2),
                            rep(rep(ident, 2), 2), ALU.mult).then_inc(*did(dve_steps, ("diag_in", m)))
        factors(0)

        def merge(n):
            L = LEVELS[n]
            mask = const[:, C_LVL + n * P // 2:C_LVL + (n + 1) * P // 2].bitcast(U32).rearrange("p (b n) -> p b n", n=L)
            for m in range(2):
                dve.wait_ge(*when((("lev", n), m)))
                dve.wait_ge(*did.last)
                right = hg_s[:, 4 * m:4 * m + 4, :, :].rearrange("p h t n -> p (h t) n").rearrange("p x (b two n) -> p x b two n", two=2, n=L)[:, :, :, 1, :]
                V.copy_predicated(right, rep(mask, 8), bank[2 * (n % 2) + m][:, :].rearrange("p (x b n) -> p x b n", x=8, n=L)).then_inc(*did(dve_steps, (("merge", n), m)))

        for n in range(8):
            j = n % 4
            lo(c0 + 8 + n + AHEAD)
            if n < 4:
                dve.wait_ge(*when(("pi", j)))
                for t in range(TB):
                    V.tensor_scalar(hg_v[:, t, 256 * j:256 * j + 256], bank[4 + j][:, t * T:(t + 1) * T], rst[:, t:t + 1], None, ALU.mult).then_inc(*did(dve_steps, ("vi", j)))
            else:
                dve.wait_ge(*when(("pg", j)))
                V.tensor_tensor(hg_g[:, 2 * j:2 * j + 2, :], two(bank[4 + j][:, :]), rep(rs[:, :], 2), ALU.mult).then_inc(*did(dve_steps, ("g", j)))
            if n < 7:
                merge(n)
                factors(n + 1)
        for m in range(2):
            dve.wait_ge(*when(("cross", m)))
            V.tensor_copy(hg_x[:, 4 * m:4 * m + 4, :], bank[m][:, :].rearrange("p (h n) -> p h n", h=4)).then_inc(*did(dve_steps, ("cross_in", m)))
        dve.wait_ge(*when("gate_sg"))
        for m in range(4):
            pair_ = slice(2 * m, 2 * m + 2)
            dve.wait_ge(*when(("osq", m)))
            V.scalar_tensor_tensor(hg_b[:, pair_, :], two(bank[4 + m][:, :]), out_gain, hg_g[:, pair_, :], ALU.mult, ALU.mult).then_inc(*did(dve_steps, ("og1", m)))
        for m in range(4):
            pair_ = slice(2 * m, 2 * m + 2)
            dve.wait_ge(*when(("ors", m)))
            dve.wait_ge(*when(("og1", m)))
            V.tensor_tensor(hg_b[:, pair_, :], hg_b[:, pair_, :], hg_a[:, pair_, :], ALU.mult).then_inc(*did(dve_steps, ("og", m)))
        for m in range(4):
            pair_ = slice(2 * m, 2 * m + 2)
            dve.wait_ge(*when(("oh", m)))
            V.tensor_tensor(xl[:, pair_, :], hg_b[:, pair_, :], f32(xh[:, pair_, :]), ALU.subtract).then_inc(*did(dve_steps, ("ol", m)))

        def add_x(v, name, b0):
            for j in range(4):
                if j < 3:
                    yield j
                dve.wait_ge(*when(name + (j,)))
                V.tensor_tensor(X[:, 2 * j:2 * j + 2, :], X[:, 2 * j:2 * j + 2, :], two(bank[b0 + j][:, :]), ALU.add).then_inc(*did(dve_steps, ("x", v, j)))

        for j in add_x(2, ("aout",), 4):
            lo(first["aout"] + j + AHEAD)

        ffn(1, 3, 2, g_norm(0, 2), 2, [first["in1"] - 1 + AHEAD], angles)

        def ple(l, nu, v, s):
            c = first[f"ple{l}"]
            dve.wait_ge(*when(("ptin", l)))
            V.tensor_copy(pt[:, :, :], two(bank[4][:, :])).then_inc(*did(dve_steps, ("pt", l)))
            dve.wait_ge(*when(("pth", l)))
            V.tensor_tensor(ptl[:, :, :], pt[:, :, :], f32(pth[:, :, :]), ALU.subtract).then_inc(*did(dve_steps, ("ptl", l)))
            norm(nu, g_norm(l, 3), [c - 1 + AHEAD, c + AHEAD])
            for m in range(4):
                dve.wait_ge(*when(("pp", l, m)))
                V.tensor_copy(pp[:, 2 * m:2 * m + 2, :], two(bank[m][:, :])).then_inc(*did(dve_steps, ("ppc", l, m)))

            def finish(j):
                pair_ = slice(2 * j, 2 * j + 2)
                dve.wait_ge(*when(("pgs", l, j)))
                V.tensor_tensor(pg[:, pair_, :], pg[:, pair_, :], pp[:, pair_, :], ALU.mult).then_inc(*did(dve_steps))
                dve.wait_ge(*did.last)
                V.tensor_tensor(X[:, pair_, :], X[:, pair_, :], pg[:, pair_, :], ALU.add).then_inc(*did(dve_steps, ("x", v + 1, j)))

            for j in range(4):
                if j != 1:
                    lo(c + 1 + j + AHEAD)
                if j == 0:
                    lo(c + 2 + AHEAD)
                    inv(s)
                dve.wait_ge(*when(("pgate", l, j)))
                if j == 2:
                    modulation(2 * l + 1)
                V.tensor_tensor(pg[:, 2 * j:2 * j + 2, :], two(bank[4 + j][:, :]), rep(rs[:, :], 2), ALU.mult).then_inc(*did(dve_steps, ("pg", l, j)))
                finish(j)

        ple(0, 4, 3, 3)

        norm(5, g_kv)
        lo(first["kvd"] + AHEAD)
        inv(4)
        dve.wait_ge(*when("kd0"))
        V.tensor_tensor(ck[:, :, :], two(bank[4][:, :]), rep(rs[:, :], 2), ALU.mult).then_inc(*did(dve_steps, "ck"))
        lo(first["kvd"] + 1 + AHEAD)
        dve.wait_ge(*when(("chunk", first["kvd"] + 1)))
        V.tensor_tensor(kr[:, :], bank[5][:, 0:T], rs[:, :], ALU.mult).then_inc(*did(dve_steps, "kr"))
        dve.wait_ge(*did.last)
        V.tensor_tensor(kr_t[:, 0, :], kr[:, :], cos[:, :], ALU.mult).then_inc(*did(dve_steps))
        dve.wait_ge(*when("ckstd"))
        V.reciprocal(rs2_kv[:, :], std2_kv[:, :]).then_inc(*did(dve_steps))
        dve.wait_ge(*did.last)
        for k in range(2):
            V.scalar_tensor_tensor(ck[:, k, :], ck[:, k, :], g_latent(k), rs2_kv[:, :], ALU.mult, ALU.mult).then_inc(*did(dve_steps, "ckn"))
        dve.wait_ge(*when("krswap"))
        V.tensor_tensor(kr_t[:, 1, :], bank[7][:, 0:T], sin[:, :], ALU.mult).then_inc(*did(dve_steps, "kr_sin"))
        dve.wait_ge(*did.last)
        for h in range(2):
            rows_ = slice(h * ROPE, (h + 1) * ROPE)
            V.tensor_tensor(krz[rows_, h, :], kr_t[rows_, 0, :], kr_t[rows_, 1, :], ALU.add).then_inc(*did(dve_steps))
        dve.wait_ge(*when("ckh"))
        V.tensor_tensor(ckl[:, :, :], ck[:, :, :], f32(ckh[:, :, :]), ALU.subtract).then_inc(*did(dve_steps, "ckl"))

        ffn(2, 6, 4, g_norm(1, 0), None)

        norm(7, g_norm(1, 1), [first["dq"] - 1 + AHEAD])
        for j in range(2):
            if j == 0:
                lo(first["dq"] + AHEAD)
                lo(first["dq"] + 1 + AHEAD)
                inv(5)
            dve.wait_ge(*when(("dq", j)))
            if j == 1:
                modulation(2)
            V.tensor_tensor(cq[:, 2 * j:2 * j + 2, :], two(bank[4 + j][:, :]), rep(rs[:, :], 2), ALU.mult).then_inc(*did(dve_steps, ("cq", j)))
        for u in range(4):
            lo(first["kvup"] + u + AHEAD)
            for n in range(2):
                dve.wait_ge(*when(("k", u, n)))
                V.tensor_copy(kn[:, 4 * u + 2 * n:4 * u + 2 * n + 2, :], two(bank[4 * (u % 2) + n][:, :])).then_inc(*did(dve_steps, ("kn", u, n)))
            if u == 0:
                dve.wait_ge(*when("cqstd"))
                V.reciprocal(rs2[:, :], std2[:, :]).then_inc(*did(dve_steps))
                dve.wait_ge(*did.last)
                for k in range(4):
                    V.scalar_tensor_tensor(cq[:, k, :], cq[:, k, :], g_q(k), rs2[:, :], ALU.mult, ALU.mult).then_inc(*did(dve_steps, ("cqn", k)))
        for k in range(4):
            dve.wait_ge(*when(("cqh", k)))
            V.tensor_tensor(cql[:, k, :], cq[:, k, :], f32(cqh[:, k, :]), ALU.subtract).then_inc(*did(dve_steps, ("cql", k)))

        def rotate(u):
            dve.wait_ge(*when(("qswap", u)))
            dve.wait_ge(*did.last)
            V.tensor_tensor(qr_t[:, 1, :], bank[4 + u % 2][:, 0:T], sin[:, :], ALU.mult).then_inc(*did(dve_steps, ("q_sin", u)))
            V.tensor_tensor(qr_t[:, 0, :], qraw[:, u % 2, :], cos[:, :], ALU.mult).then_inc(*did(dve_steps))
            dve.wait_ge(*did.last)
            V.tensor_tensor(qr[:, u, :], qr_t[:, 0, :], qr_t[:, 1, :], ALU.add).then_inc(*did(dve_steps, ("qr", u)))

        for u in range(8):
            if u + AHEAD < 8:
                lo(first["uq"] + u + AHEAD)
            dve.wait_ge(*when(("qnope", u)))
            V.tensor_scalar(qn[:, 2 * u:2 * u + 2, :], two(bank[2 * (u % 2)][:, :]), SCALE_B, None, ALU.mult).then_inc(*did(dve_steps, ("qn", u)))
            dve.wait_ge(*when(("chunk", first["uq"] + u)))
            if u >= 2:
                dve.wait_ge(*when(("qr", u - 2)))
            V.tensor_scalar(qraw[:, u % 2, :], bank[2 * (u % 2) + 1][:, 0:T], SCALE_B, None, ALU.mult).then_inc(*did(dve_steps, ("qraw", u)))
            if u >= 1:
                rotate(u - 1)
        rotate(7)

        def maxima(item, b0, nm):
            for t in range(TB):
                dve.wait_ge(*when(("s", item, t)))
                V.tensor_reduce(nm[:, 2 * t:2 * t + 2], two(bank[b0 + t][:, 0:2 * (t + 1) * P]), AX.X, ALU.max, negate=True).then_inc(*did(dve_steps, ("max", item)))

        def maxima_b(i):
            maxima(("b", i), 2 * (i % 2), nmB[:, i % 3])

        def weigh(item, s, den, rd, gate=None, valid=False, width=None):
            dve.wait_ge(*when(("exps", item)))
            dve.wait_ge(*did.last)
            V.reciprocal(rd[:, :], den[:, :]).then_inc(*did(dve_steps))
            if valid:
                dve.wait_ge(*did.last)
                V.tensor_tensor(two(rd[:, :]), two(rd[:, :]), const[:, C_ROWV:C_ROWV + 2].unsqueeze(2).to_broadcast([P, 2, 2]), ALU.mult).then_inc(*did(dve_steps))
            if gate is not None:
                dve.wait_ge(*did.last)
                V.tensor_tensor(two(rd[:, :]), two(rd[:, :]), gate, ALU.mult).then_inc(*did(dve_steps))
            dve.wait_ge(*did.last)
            for h in range(2):
                for t in range(TB):
                    cols = (slice(0, P) if t == 0 else slice(P, 3 * P)) if width is None else slice(16 * t, 16 * t + width)
                    V.tensor_scalar(s[:, h, cols], s[:, h, cols], rd[:, 2 * t + h:2 * t + h + 1], None, ALU.mult).then_inc(*did(dve_steps, ("probs", item)))

        def out_b(i):
            dve.wait_ge(*when(("oh", "b", i)))
            V.tensor_tensor(ol[:, 2 * i:2 * i + 2, :], two(bank[6 + i % 2][:, :]), f32(oh[:, 2 * i:2 * i + 2, :]), ALU.subtract).then_inc(*did(dve_steps, ("ol", "b", i)))

        maxima_b(0)
        maxima_b(1)
        for i in range(8):
            weigh(("b", i), sB[:, i % 3], denB[:, i % 3], rdB[:, i % 3])
            if i >= 2:
                out_b(i - 2)
            if i < 6:
                maxima_b(i + 2)
            if i >= 6:
                lo(first["bout"] + i - 6)
        for i in (6, 7):
            out_b(i)
        lo(first["bout"] + 2)
        for j in range(7):
            lo(first["bout"] + j + AHEAD)
        for m in range(4):
            dve.wait_ge(*when(("bout", m)))
            V.tensor_tensor(X[:, 2 * m:2 * m + 2, :], X[:, 2 * m:2 * m + 2, :], two(bank[m][:, :]), ALU.add).then_inc(*did(dve_steps, ("x", 6, m)))

        ffn(3, 8, 6, g_norm(1, 2), 6, [first["in3"] - 1 + AHEAD])
        ple(1, 9, 7, 7)
        inv(8)
        for k in range(KD):
            V.scalar_tensor_tensor(X[:, k, :], X[:, k, :], g_final(k), rs[:, :], ALU.mult, ALU.mult).then_inc(*did(dve_steps, ("x", 9, k // 2)))

        for l in range(2):
            nu, v, s = 10 + 2 * l, 9 + l, 9 + 2 * l
            inv(s)
            V.scalar_tensor_tensor(gpre[:, :], mods[:, l, 8:16], 1.0, col1[:, 48 + 8 * l:56 + 8 * l], ALU.add, ALU.mult).then_inc(*did(dve_steps))
            V.tensor_tensor(gpost[:, :], mods[:, l, 16:24], col1[:, 64 + 8 * l:72 + 8 * l], ALU.mult).then_inc(*did(dve_steps))
            dve.wait_ge(*did.last)
            dve.wait_ge(*when(("sums", s)))
            def scaled(k):
                V.scalar_tensor_tensor(sq[:, k, :], X[:, k, :], gpre[:, k:k + 1], rs[:, :], ALU.mult, ALU.mult).then_inc(*did(dve_steps, ("xn", l, k)))

            scaled(0)
            scaled(1)
            for k in range(KD):
                if k + 2 < KD:
                    scaled(k + 2)
                dve.wait_ge(*when(("xh", nu, k)))
                V.scalar_tensor_tensor(xl[:, k, :], sq[:, k, :], mods[:, l, k:k + 1], f32(xh[:, k, :]), ALU.add, ALU.subtract).then_inc(*did(dve_steps, ("xl", nu, k)))
            dve.wait_ge(*did.last)
            dve.wait_ge(*when(("zeros", l)))
            def slope(h):
                return float(2.0 ** (-8.0 * (h + 1) / HEADS_C))
            for h in range(HEADS_C):
                V.scalar_tensor_tensor(bias[:, h, :], const[:, C_DIST:C_DIST + T], -slope(h), const[:, C_DMASK:C_DMASK + T], ALU.mult, ALU.add).then_inc(*did(dve_steps))
                V.scalar_tensor_tensor(cbias[:, h, :, :].rearrange("p a n -> p (a n)"), const[:, C_CMPD:C_CMPD + 2 * CMP_T], -slope(h),
                                       const[:, C_CMPM:C_CMPM + 2 * CMP_T], ALU.mult, ALU.add).then_inc(*did(dve_steps))
            c0 = first[f"win{l}"]

            def zero_padded(dst, src, key):
                for h in range(2):
                    rows_ = slice(h * DH, (h + 1) * DH)
                    V.tensor_copy(dst[rows_, :, h, :], src[rows_, :, :]).then_inc(*did(dve_steps, key))

            for n, (name, j) in enumerate(WIN):
                if n + AHEAD < 16:
                    lo(c0 + n + AHEAD)
                b = n % 8
                key, done = ("win", l, n), ("proj", l, n)
                src = two(bank[b][:, :])
                if name in ("qm", "qn"):
                    dve.wait_ge(*when(key))
                    q = qm if name == "qm" else qs
                    V.tensor_scalar(q[:, 2 * j:2 * j + 2, :], src, float(DH ** -0.5), None, ALU.mult).then_inc(*did(dve_steps, done))
                elif name == "km":
                    dve.wait_ge(*when(key))
                    zero_padded(kmz[:, 2 * j:2 * j + 2, :, :], src, done)
                elif name == "vm":
                    dve.wait_ge(*when(key))
                    for t in range(TB):
                        for h in range(2):
                            V.tensor_copy(vmz[:, t, 4 * j + h:4 * j + 4:2, h * DH:(h + 1) * DH],
                                          src[:, t, :].rearrange("p (m h d) -> p m h d", h=2, d=DH)[:, :, h, :]).then_inc(*did(dve_steps, done))
                elif name == "kcvc":
                    dve.wait_ge(*when(key))
                    V.tensor_copy(kA[:, 0:2, :], src).then_inc(*did(dve_steps, ("kA", l, 0)))
                    at[done] = at[("kA", l, 0)]
                elif name in ("ksvs", "kwvw"):
                    dve.wait_ge(*when(key))
                    which = 2 if name == "ksvs" else 3
                    V.tensor_copy(kA[:, which, :], src[:, 0, :]).then_inc(*did(dve_steps, ("kA", l, 1)))
                    vz = vsz if name == "ksvs" else vwz
                    for h in range(2):
                        V.tensor_copy(vz[:, :, :, h, h * DH:(h + 1) * DH],
                                      src[:, 1, :].rearrange("p (t g d) -> p t g d", t=TB, g=GROUPS)).then_inc(*did(dve_steps, done))
                if name == "kwvw":
                    dve.wait_ge(*when(("kB", l, 0)))
                    kB = two(bank[0][:, :])
                    for g, low, high in ((0, kA[:, 0:2, :], kB), (1, kB, kA[:, 0:2, :])):
                        V.tensor_copy(kc2[0:DH, :, g, :], low[0:DH, :, :]).then_inc(*did(dve_steps))
                        V.tensor_copy(kc2[DH:P, :, g, 0:T - 1], high[DH:P, :, 1:T]).then_inc(*did(dve_steps, ("kB_used", l, 0)))
                    dve.wait_ge(*did.last)
                    for kv in range(2):
                        pe_col = col2[:, 32 * kv + 16 * l:32 * kv + 16 * l + 16]
                        for g in range(GROUPS):
                            for a in range(2):
                                toks = kc2[:, kv, g, 16 * a:16 * a + 240].rearrange("p (t r two) -> p t r two", r=8, two=2)[:, :, :, 0]
                                dst = win[:, kv, 8 * a:8 * a + 8, CMP_T * g:CMP_T * (g + 1)].rearrange("p r t -> p t r")
                                V.tensor_tensor(dst, toks, rep(pe_col[:, 8 * a:8 * a + 8], CMP_T), ALU.add).then_inc(*did(dve_steps, ("windows", l, kv)))
            dve.wait_ge(*when(("kB", l, 1)))
            for which, kz in ((0, ksz), (1, kwz)):
                here, there = kA[:, 2 + which, :], bank[1][:, which * T:(which + 1) * T]
                for g in range(GROUPS):
                    for h in range(2):
                        rows_ = slice(h * DH, (h + 1) * DH)
                        V.tensor_copy(kz[rows_, g, h, :], (here if g == h else there)[rows_, :]).then_inc(*did(dve_steps, ("kB_used", l, 1)))
            dve.wait_ge(*when(("kcmp", l)))
            for h in range(2):
                rows_ = slice(h * DH, (h + 1) * DH)
                V.tensor_copy(kcz[rows_, :, h, 0:CMP_T], bank[1][rows_, 0:30].rearrange("p (g t) -> p g t", g=GROUPS)).then_inc(*did(dve_steps, ("kcz", l)))
            dve.wait_ge(*when(("vcmp", l)))
            for h in range(2):
                V.tensor_copy(vcz[0:CMP_T, :, h, h * DH:(h + 1) * DH], bank[2][0:CMP_T, 0:P].rearrange("p (g d) -> p g d", g=GROUPS)).then_inc(*did(dve_steps, ("vcz", l)))
            nc.vector.memset(small[:, 48:49], 0.0).then_inc(*did(dve_steps, ("attn", l)))

            def maxima_c(i):
                kind, m, _, _ = ITEMS[i]
                s_, nm = sC[:, i % 3], nmC[:, i % 3]
                b0 = 2 * (i % 2)
                item = ("c", l, i)
                if kind != "cmp":
                    return maxima(item, b0, nm)
                if i >= 3:
                    dve.wait_ge(*when(("pt", ("c", l, i - 3))))
                V.memset(s_[:, :, 0:32], 0.0).then_inc(*did(dve_steps))
                dve.wait_ge(*when(("s", item, 1)))
                for t in range(TB):
                    V.tensor_reduce(nm[:, 2 * t:2 * t + 2], two(bank[b0][:, 30 * t:30 * t + 30]), AX.X, ALU.max, negate=True).then_inc(*did(dve_steps, ("max", item)))

            def weigh_c(i):
                kind, m, _, _ = ITEMS[i]
                gate = None
                if kind != "moba":
                    branch = {"cmp": 0, "slc": 1, "win": 2}[kind]
                    gate = gates[:, :, :].rearrange("p t (h b) -> p t h b", b=3)[:, :, 2 * m:2 * m + 2, branch]
                weigh(("c", l, i), sC[:, i % 3], denC[:, i % 3], rdC[:, i % 3], gate, kind == "cmp", CMP_T if kind == "cmp" else None)

            def gated(i):
                kind, m, _, stop = ITEMS[i]
                if stop:
                    k = m if kind == "moba" else 4 + m
                    z = (zm if kind == "moba" else zn)[:, m, :]
                    dve.wait_ge(*when(("oc", l, i)))
                    dve.wait_ge(*did.last)
                    V.tensor_tensor(yC[:, k % 2, :], bank[6 + k % 2][:, 0:T], z, ALU.mult).then_inc(*did(dve_steps, ("y", l, k)))

            def gated_lo(i):
                kind, m, _, stop = ITEMS[i]
                if stop:
                    k = m if kind == "moba" else 4 + m
                    dve.wait_ge(*when(("yh", l, k)))
                    V.tensor_tensor(xl[:, k, :], yC[:, k % 2, :], f32(xh[:, k, :]), ALU.subtract).then_inc(*did(dve_steps, ("yl", l, k)))

            dve.wait_ge(*when(("gates", l)))
            maxima_c(0)
            maxima_c(1)
            for i in range(len(ITEMS)):
                weigh_c(i)
                if i >= 2:
                    gated(i - 2)
                if i + 2 < len(ITEMS):
                    maxima_c(i + 2)
                if i >= 3:
                    gated_lo(i - 3)
                if i >= 16 - AHEAD:
                    lo(first[f"wout{l}"] + i - 16 + AHEAD)
            gated(len(ITEMS) - 2)
            gated(len(ITEMS) - 1)
            for i in range(len(ITEMS) - 3, len(ITEMS)):
                gated_lo(i)
            for j in range(4):
                lo(first[f"wout{l}"] + j + AHEAD)
                dve.wait_ge(*when(("wout", l, j)))
                V.tensor_copy(y2[:, 2 * j:2 * j + 2, :], two(bank[j][:, :])).then_inc(*did(dve_steps, ("y2", l, j)))
            inv(s + 1)
            for j in range(4):
                for k in (2 * j, 2 * j + 1):
                    V.scalar_tensor_tensor(y2[:, k, :], y2[:, k, :], gpost[:, k:k + 1], rs[:, :], ALU.mult, ALU.mult).then_inc(*did(dve_steps))
                dve.wait_ge(*did.last)
                V.tensor_tensor(X[:, 2 * j:2 * j + 2, :], X[:, 2 * j:2 * j + 2, :], y2[:, 2 * j:2 * j + 2, :], ALU.add).then_inc(*did(dve_steps, ("x", 10 + l, j)))

    block_ctx.__exit__(None, None, None)
    return at


_INS = ['x', 'p', 'positions', 'norm_gains', 'ffn_w_in', 'ffn_w_out', 'ple_w_gate', 'ple_w_in', 'a_w_in', 'a_lb_logits',
        'a_out_gain', 'a_w_out', 'kv_norm_in', 'kv_w_down', 'kv_latent_norm', 'kv_w_up', 'b_w_dq', 'b_q_norm', 'b_w_uq',
        'b_w_out', 'final_norm', 'c_2', 'w_ada_2', 'b_ada_2', 'g_pre_2', 'g_post_2', 'w_in_2', 'w_out_2', 'pe_k_2',
        'pe_v_2', 'w_ck1_2', 'w_ck2_2', 'w_cv1_2', 'w_cv2_2']


def kernel(**inputs):
    import numpy as _np
    import concourse.bacc as _bacc
    from concourse import mybir as _mybir
    from concourse.bass_utils import run_bass_kernel_spmd as _run

    arrays = {f"in_{name}": _np.ascontiguousarray(inputs[name]) for name in _INS}
    arrays["in_consts"] = shape_constants()

    def program(known):
        nc = _bacc.Bacc("TRN2", target_bir_lowering=False, num_devices=1)
        io = {n[3:]: nc.dram_tensor(n, a.shape, _mybir.dt.from_np(a.dtype), kind="ExternalInput").ap() for n, a in arrays.items()}
        io["out"] = nc.dram_tensor("out_0", (1, T, D), _mybir.dt.float32, kind="ExternalOutput").ap()
        return nc, build(nc, io, known)

    _, counts = program({})
    nc, _ = program(counts)
    r = _run(nc, [arrays], core_ids=[0])
    return r.results[0]["out_0"]
```

```python
import numpy as np

import concourse.bass as bass
from concourse import mybir

F32 = mybir.dt.float32
F32R = mybir.dt.float32r
BF16 = mybir.dt.bfloat16
I32 = mybir.dt.int32
U32 = mybir.dt.uint32
ACT = mybir.ActivationFunctionType
ALU = mybir.AluOpType
AX = mybir.AxisListType

P = 128
T = 256
TB = T // P
D = 1024
KD = D // P
FF = 2816
KF = FF // P
PAIRS = KF // 2
EPS = 1e-6
NEG = -1e30

CH = 2048
HC = CH // 2
NRAW = 2
NSLOT = 4
AHEAD = NSLOT - 1
MOD_STEPS = 7
MOD = 2 * 3 * D // 4 // 256

HEADS_A = 8
CHUNK_A = 64
HEADS_B = 16
NOPE, ROPE, VDIM = 128, 64, 128
SCALE_B = float((NOPE + ROPE) ** -0.5)
HEADS_C = 8
DH = 64
GROUPS = 2
CMP_T = 15
OFF = dict(qm=0, km=512, vm=1024, zm=1536, qn=2048, kcvc=2560, ks=2816, vs=2944, kw=3072, vw=3200, gl=3328, zn=3352)
FOLDED = (0, 1, 2, 3, 5, 6, 7)
FIRST_HALF = 4
LEVELS = [64, 32, 16, 8, 4, 2, 1]

C_IDENT, C_PERM, C_CAUS, C_DIST, C_DMASK, C_RESET = 0, 128, 256, 384, 640, 896
C_CMPD, C_CMPM, C_ROWV, C_FREQ, C_SIGN, C_SWAP, C_LVL = 1152, 1182, 1212, 1214, 1215, 1216, 1344
C_N = C_LVL + P // 2 * len(LEVELS)


def shape_constants():
    c = np.zeros((P, C_N), np.float32)
    p = np.arange(P)
    c[:, C_IDENT:C_IDENT + P] = np.eye(P)
    swap = (p // 64) * 64 + (p % 64 + 32) % 64
    c[swap, C_PERM + p] = 1.0
    c[(p + 64) % P, C_SWAP + p] = 1.0
    c[:, C_CAUS:C_CAUS + P] = np.where(p[:, None] >= p[None, :], 0.0, NEG)
    dist = p[:, None] + P - np.arange(T)[None, :]
    c[:, C_DIST:C_DIST + T] = np.maximum(dist, 0)
    c[:, C_DMASK:C_DMASK + T] = np.where(dist >= 0, 0.0, NEG)
    c[:, C_RESET:C_RESET + T] = (np.arange(T) % CHUNK_A != 0)[None, :]
    for b in range(TB):
        d = (b * P + p)[:, None] - (np.arange(CMP_T) * 16 + 31)[None, :]
        c[:, C_CMPD + b * CMP_T:C_CMPD + (b + 1) * CMP_T] = np.maximum(d, 0)
        c[:, C_CMPM + b * CMP_T:C_CMPM + (b + 1) * CMP_T] = np.where(d >= 0, 0.0, NEG)
        c[:, C_ROWV + b] = (b * P + p) >= 31
    half = ROPE // 2
    freq = np.float32(1.0) / (np.float32(10000.0) ** (np.arange(0, ROPE, 2, dtype=np.float32) / np.float32(ROPE)))
    c[:, C_FREQ] = freq[p % half]
    c[:, C_SIGN] = np.where(p % ROPE < half, -1.0, 1.0)
    for n, L in enumerate(LEVELS):
        s, j = p[:, None], np.arange(P // 2)[None, :]
        c[:, C_LVL + n * P // 2:C_LVL + (n + 1) * P // 2] = (s // (2 * L) == j // L) & (s % (2 * L) < L)
    return c


class Steps:

    def __init__(self, at):
        self.at, self.count, self.last = at, {}, None

    def __call__(self, sem, name=None, by=1):
        n = self.count.get(sem.name, 0) + by
        self.count[sem.name] = n
        self.last = (sem, n)
        if name is not None:
            self.at[name] = (sem.name, n)
        return sem, by

    def skip(self, sem, by):
        self.count[sem.name] = self.count.get(sem.name, 0) + by
        self.last = (sem, self.count[sem.name])


def chunk_table():
    first, n = {}, 0
    sizes = []
    for f, after in ((0, [("hgrn", 16), ("aout", 4)]), (1, [("ple0", 5), ("kvd", 2)]),
                     (2, [("dq", 2), ("kvup", 4), ("uq", 8), ("bout", 8)]), (3, [("ple1", 5)])):
        sizes += [(f"in{f}", 2 * PAIRS), (f"out{f}", PAIRS)] + after
    for l in range(2):
        sizes += [(f"win{l}", 16), (f"wout{l}", 4)]
    for name, size in sizes:
        first[name] = n
        n += size
    return first, n


def build(nc, io, known):
    at = {}
    first, n_chunks = chunk_table()

    used = {first["kvd"] + 1: (HC, 0)}
    parts = {first["kvd"] + 1: (2, 0)}
    for u in range(8):
        used[first["uq"] + u], parts[first["uq"] + u] = (HC, 4 * 2 * (NOPE + ROPE) - HC), (4, 0)
    for l in range(2):
        used[first[f"win{l}"] + 13], parts[first[f"win{l}"] + 13] = (KD * 24, 0), (1, 0)
        for n in (11, 12):
            parts[first[f"win{l}"] + n] = (2, 2)
    landings = []
    for c in range(n_chunks):
        landings.append([(landings[c - NRAW][h] if c >= NRAW else 0) + parts.get(c, (1, 1))[h] for h in range(2)])

    names = ["x_landed", "ident_landed", "const_landed", "gains_landed", "others_landed", "ple_landed", "cmp_landed", "out_landed", "landed00", "landed01", "landed10", "landed11",
             "hi_ready", "lo_ready", "pe_groups", "act_steps", "dve_steps", "pool_steps",
             "gate_scaled", "up_scaled", "silu_ready", "hidden_ready", "hidden_hi", "hidden_lo", "mod_landed", "mod_steps"]
    sem = {n: nc.alloc_semaphore(n) for n in names}
    landed = [[sem[f"landed{r}{h}"] for h in range(2)] for r in range(NRAW)]
    hi_ready, lo_ready, pe_groups = sem["hi_ready"], sem["lo_ready"], sem["pe_groups"]
    act_steps, dve_steps, pool_steps = sem["act_steps"], sem["dve_steps"], sem["pool_steps"]
    gate_scaled, up_scaled, silu_ready = sem["gate_scaled"], sem["up_scaled"], sem["silu_ready"]
    hidden_ready, hidden_hi, hidden_lo = sem["hidden_ready"], sem["hidden_hi"], sem["hidden_lo"]

    def when(name):
        s, n = known[name] if known else ("pe_groups", 1)
        return sem[s], n

    base = [(nc.sbuf_base + 63) // 64 * 64]

    def fixed(name, shape, dt=F32):
        size = int(np.prod(shape[1:])) * 4
        t = nc.alloc_sbuf_tensor_at(name, shape, dt, offset=base[0])
        base[0] += (size + 63) // 64 * 64
        return t

    w_raw = fixed("w_raw", [P, NRAW, CH])
    w_hi = fixed("w_hi", [P, NSLOT, CH], F32R)
    w_lo = fixed("w_lo", [P, NSLOT, CH], F32R)
    X = fixed("X", [P, KD, T])
    xh = fixed("xh", [P, KD, T], F32R)
    xl = fixed("xl", [P, KD, T], F32R)
    sq_at = base[0]
    sq = fixed("sq", [P, KD, T])
    rs = fixed("rs", [P, T])
    std = fixed("std", [P, T])
    ones = fixed("ones", [P, P])
    const = fixed("const", [P, C_N])
    ident_bf = fixed("ident_bf", [P, P], BF16)
    caus_bf = fixed("caus_bf", [P, P], BF16)
    cos = fixed("cos", [P, T])
    sin = fixed("sin", [P, T])
    col0 = fixed("col0", [P, 104])
    col1 = fixed("col1", [P, 88])
    col2 = fixed("col2", [P, 64])
    latent_at = base[0]
    ckh = fixed("ckh", [P, 2, T], F32R)
    ckl = fixed("ckl", [P, 2, T], F32R)
    krz = fixed("krz", [P, 2, T])
    eps = fixed("eps", [P, 1])
    lb = fixed("lb", [P, KD])
    oml = fixed("oml", [P, KD])
    small = fixed("small", [P, 64])
    rst = fixed("rst", [P, TB])
    csf = fixed("csf", [P, KD])
    mods = fixed("mods", [P, 2, 24])
    gpre = fixed("gpre", [P, KD])
    gpost = fixed("gpost", [P, KD])
    ptok = fixed("ptok", [P, 2, TB, T])
    region = base[0]

    def at_offset(start):
        pos = [start]

        def place(name, shape, dt=F32):
            size = int(np.prod(shape[1:])) * 4
            t = nc.alloc_sbuf_tensor_at(name, shape, dt, offset=pos[0])
            pos[0] += (size + 63) // 64 * 64
            assert pos[0] <= nc.sbuf_usable_end, (name, pos[0])
            return t
        return place, pos

    place, _ = at_offset(region)
    xtok = place("xtok", [P, TB, D])
    vrow0 = place("vrow0", [P, P])
    place, _ = at_offset(latent_at)
    vrow1 = place("vrow1", [P, P])
    vrow2 = place("vrow2", [P, P])
    pos_i = place("pos_i", [P, T], I32)
    ang = place("ang", [P, T])
    turns = place("turns", [P, T])
    red = place("red", [P, T])
    mag = place("mag", [P, T])
    place, _ = at_offset(region)
    hh = place("hh", [P, KF, T], F32R)
    hl = place("hl", [P, KF, T], F32R)
    gate_t = place("gate_t", [P, 2, 2, T])
    up_t = place("up_t", [P, 2, 2, T])
    silu_t = place("silu_t", [P, 2, 2, T])
    hid_t = place("hid_t", [P, 2, 2, T])
    mod_raw = place("mod_raw", [P, KD // 2, 256])
    mod_acc = place("mod_acc", [P, MOD, 256])
    place, _ = at_offset(region)
    hg_a = place("hg_a", [P, KD, T])
    hg_k = place("hg_k", [P, KD, T])
    hg_b = place("hg_b", [P, KD, T])
    hg_q = place("hg_q", [P, KD, T])
    hg_v = place("hg_v", [P, TB, D])
    hg_g = place("hg_g", [P, KD, T])
    hg_f0 = place("hg_f0", [P, KD, T])
    hg_f = [hg_f0, sq]
    hg_s = place("hg_s", [P, KD, 2, P])
    hg_x = place("hg_x", [P, KD, P])
    hg_t = place("hg_t", [P, KD])
    place, _ = at_offset(region + KD * T * 4)
    hg_oh = place("hg_oh", [P, KD, T], F32R)
    place, _ = at_offset(region + 3 * KD * T * 4)
    hg_ol = place("hg_ol", [P, KD, T], F32R)
    place, _ = at_offset(region + 2 * KF * T * 4)
    pt = place("pt", [P, 2, T])
    pth = place("pth", [P, 2, T], F32R)
    ptl = place("ptl", [P, 2, T], F32R)
    place, _ = at_offset(region)
    pp = place("pp", [P, KD, T])
    pg = place("pg", [P, KD, T])
    sq_f = place("sq_f", [P, KD, T])
    place, _ = at_offset(sq_at + 2 * T * 4)
    ck = place("ck", [P, 2, T])
    kr = place("kr", [P, T])
    kr_t = place("kr_t", [P, 2, T])
    rs2_kv = place("rs2_kv", [P, T])
    place, posn = at_offset(region)
    oh_at = posn[0]
    qn = place("qn", [P, HEADS_B, T])
    ol_at = posn[0]
    kn = place("kn", [P, HEADS_B, T])
    qr = place("qr", [P, HEADS_B // 2, T])
    vb = place("vb", [P, TB, HEADS_B * VDIM])
    temp_at = posn[0]
    cq = place("cq", [P, 4, T])
    cqh = place("cqh", [P, 4, T], F32R)
    cql = place("cql", [P, 4, T], F32R)
    place, _ = at_offset(sq_at)
    qr_t = place("qr_t", [P, 2, T])
    qraw = place("qraw", [P, 2, T])
    rs2 = place("rs2", [P, T])
    std2 = place("std2", [P, T])
    place, _ = at_offset(oh_at)
    oh = place("oh", [P, HEADS_B, T], F32R)
    place, _ = at_offset(ol_at)
    ol = place("ol", [P, HEADS_B, T], F32R)
    place, _ = at_offset(temp_at)
    sB = place("sB", [P, 3, 2, 3 * P])
    nmB = place("nmB", [P, 3, 4])
    denB = place("denB", [P, 3, 4])
    rdB = place("rdB", [P, 3, 4])
    place, _ = at_offset(sq_at)
    ptB = place("ptB", [P, 2, 2, 3 * P])
    place, posn = at_offset(region)
    qm = place("qm", [P, 4, T])
    qs = place("qs", [P, 4, T])
    kmz = place("kmz", [P, 4, 2, T])
    ksz = place("ksz", [P, GROUPS, 2, T])
    kwz = place("kwz", [P, GROUPS, 2, T])
    y_at = posn[0]
    vmz = place("vmz", [P, TB, HEADS_C, P])
    vsz = place("vsz", [P, TB, GROUPS, 2, P])
    vwz = place("vwz", [P, TB, GROUPS, 2, P])
    zm = place("zm", [P, 4, T])
    zn = place("zn", [P, 4, T])
    kcz = place("kcz", [P, GROUPS, 2, 16])
    vcz = place("vcz", [16, GROUPS, 2, P])
    gates = place("gates", [P, TB, 24])
    cbias = place("cbias", [P, HEADS_C, TB, CMP_T], BF16)
    gh = place("gh", [DH, 64])
    gx = place("gx", [DH, 64])
    wc2 = place("wc2", [DH, 3, DH])
    temp_at = posn[0]
    kA = place("kA", [P, 4, T])
    win = place("win", [P, 2, 16, 2 * CMP_T])
    wc1 = place("wc1", [P, 2, 16, DH])
    place, _ = at_offset(temp_at)
    sC = place("sC", [P, 3, 2, 3 * P])
    ptC = place("ptC", [P, 2, 2, 3 * P])
    nmC = place("nmC", [P, 3, 4])
    denC = place("denC", [P, 3, 4])
    rdC = place("rdC", [P, 3, 4])
    yC = place("yC", [P, 2, T])
    place, _ = at_offset(latent_at)
    kc2 = place("kc2", [P, 2, GROUPS, T])
    place, _ = at_offset(y_at)
    y2 = place("y2", [P, KD, T])
    place, _ = at_offset(sq_at)
    bias = place("bias", [P, HEADS_C, T], BF16)
    place, _ = at_offset(sq_at + HEADS_C * T * 2)
    gates_f = place("gates_f", [24, T])
    place, _ = at_offset(region)
    otok = place("otok", [P, TB, D])

    bank = [nc.alloc_psum_tensor(f"bank{i}", [P, 512], F32) for i in range(8)]
    ident = const[:, C_IDENT:C_IDENT + P]

    def g_norm(l, g):
        return lambda k: col0[:, (l * 4 + g) * KD + k:(l * 4 + g) * KD + k + 1]

    def g_kv(k):
        return col0[:, 81 + k:82 + k]

    def g_latent(k):
        return col0[:, 89 + k:90 + k]

    def g_q(k):
        return col0[:, 91 + k:92 + k]

    def g_final(k):
        return col0[:, 95 + k:96 + k]

    out_gain = col0[:, 80:81]

    def sums_bank(s):
        if s in (4, 8):
            return {4: 6, 8: 2}[s]
        return 4 if s in (0, 2, 6, 10, 12) else 3

    def rep(ap, n):
        shape = list(ap.shape)
        return ap.unsqueeze(1).to_broadcast([shape[0], n] + shape[1:])

    def two(ap):
        return ap.rearrange("p (a n) -> p a n", a=2)

    def f32(ap):
        return ap.bitcast(F32)

    def half_columns(c, h):
        return slice(HC * h, HC * h + (used[c][h] or 8)) if c in used else slice(HC * h, HC * (h + 1))

    def slot(w, c, k):
        rows, cols = k
        return w[:, c % NSLOT, 0:rows * cols].rearrange("p (k n) -> p k n", k=rows)

    WIN = ([("qm", j) for j in range(2)] + [("km", j) for j in range(2)] + [("vm", j) for j in range(2)]
           + [("zm", j) for j in range(2)] + [("qn", j) for j in range(2)]
           + [("kcvc", 0), ("kskw", 0), ("vsvw", 0), ("gl", 0)] + [("zn", j) for j in range(2)])

    ITEMS = [("moba", m, True, True) for m in range(4)]
    for m in range(4):
        ITEMS += [("win", m, True, False), ("slc", m, False, False), ("cmp", m, False, True)]

    block_ctx = nc.Block()
    block = block_ctx.__enter__()

    @block.sync
    def _(sp):
        def half_free(c, h, i2=0):
            if c >= NRAW:
                sp.wait_ge(lo_ready, 2 * (c - NRAW) + h + 1 + i2)

        def load(c, k, src):
            r, n = k
            if c in used:
                half_free(c, 1)
                dst = w_raw[:, c % NRAW, 0:r * n].rearrange("p (k n) -> p k n", k=r)
                sp.dma_start(dst, src.rearrange("(k p) n -> p k n", p=P)).then_inc(landed[c % NRAW][0], 16)
                return
            for h in range(2):
                load_half(c, h, r, src[r // 2 * P * h:r // 2 * P * (h + 1), :])

        def load_half(c, h, r, src, i2=0):
            half_free(c, h, i2)
            sp.dma_start(w_raw[:, c % NRAW, HC * h:HC * (h + 1)].rearrange("p (k n) -> p k n", k=r // 2),
                         src.rearrange("(k p) n -> p k n", p=P)).then_inc(landed[c % NRAW][h], 16)

        def load_ffn(f):
            l, w = f // 2, f % 2
            c = first[f"in{f}"]
            w_in, w_out = io["ffn_w_in"][l, w], io["ffn_w_out"][l, w]

            def pair(c, p, it):
                for part in range(2):
                    cols = bass.ds(part * FF + 256 * p + (0 if it is None else 256 * it), 256)
                    for h in range(2):
                        load_half(c + part, h, KD, w_in[D // 2 * h:D // 2 * (h + 1), cols], 0 if it is None else 4 * it)

            pair(c, 0, None)
            with sp.Fori(0, PAIRS - 1) as it:
                pair(c + 2, 1, it)
            c = first[f"out{f}"]
            load(c, (2, D), w_out[0:256, :])
            with sp.Fori(0, (PAIRS - 1) // 2) as it:
                for j in range(2):
                    for h in range(2):
                        load_half(c + 1 + j, h, 2, w_out[bass.ds(256 * (1 + j) + P * h + 512 * it, P), :], 4 * it)

        def load_cols(name, w, width, cols, count=None):
            c = first[name]
            for j in range(count if count is not None else cols // width):
                load(c + j, (w.shape[0] // P, width), w[:, j * width:(j + 1) * width])

        def load_rows(name, w):
            c = first[name]
            for j in range(w.shape[0] // 256):
                load(c + j, (2, w.shape[1]), w[256 * j:256 * j + 256, :])

        sp.dma_start(xtok[:, :, :], io["x"][0].rearrange("(b p) n -> p b n", p=P)).then_inc(sem["x_landed"], 16)
        load_ffn(0)
        a_in = io["a_w_in"][0]
        for n, seg in enumerate((1, 0, 2, 3)):
            for j in range(4):
                load(first["hgrn"] + 4 * n + j, (KD, 256), a_in[:, seg * D + 256 * j:seg * D + 256 * j + 256])
        load_cols("aout", io["a_w_out"][0], 256, D)
        load_ffn(1)

        def load_ple(l):
            c = first[f"ple{l}"]
            load(c, (2, D), io["ple_w_in"][l])
            for j in range(4):
                load(c + 1 + j, (KD, 256), io["ple_w_gate"][l][:, 256 * j:256 * j + 256])

        load_ple(0)
        load(first["kvd"], (KD, 256), io["kv_w_down"][:, 0:256])
        c = first["kvd"] + 1
        half_free(c, 1)
        for h in range(2):
            sp.dma_start(w_raw[:, c % NRAW, 0:KD * P].rearrange("p (k h n) -> p k h n", k=KD, h=2)[:, :, h, :],
                         io["kv_w_down"][:, 256:320].rearrange("(k p) n -> p k n", p=P)).then_inc(landed[c % NRAW][0], 16)
        load_ffn(2)
        load_cols("dq", io["b_w_dq"][0], 256, 512)
        for j in range(4):
            load(first["kvup"] + j, (2, D), io["kv_w_up"][:, D * j:D * j + D])
        for u in range(8):
            c = first["uq"] + u
            half_free(c, 1)
            for at_, width in ((0, NOPE), (NOPE, ROPE)):
                for h in range(2):
                    src = io["b_w_uq"][0][:, (2 * u + h) * (NOPE + ROPE) + at_:(2 * u + h) * (NOPE + ROPE) + at_ + width]
                    col = 2 * at_ + h * width
                    sp.dma_start(w_raw[:, c % NRAW, 0:4 * 384].rearrange("p (k n) -> p k n", k=4)[:, :, col:col + width],
                                 src.rearrange("(k p) n -> p k n", p=P)).then_inc(landed[c % NRAW][0], 16)
        load_rows("bout", io["b_w_out"][0])
        load_ffn(3)
        load_ple(1)
        for l in range(2):
            w = io["w_in_2"][l]
            for n, (name, j) in enumerate(WIN):
                if name in ("kskw", "vsvw"):
                    c = first[f"win{l}"] + n
                    for h in range(2):
                        half_free(c, h)
                        for i in range(2):
                            off = OFF[name[2 * i:2 * i + 2]]
                            dst = w_raw[:, c % NRAW, HC * h:HC * (h + 1)].rearrange("p (k n) -> p k n", n=256)[:, :, P * i:P * (i + 1)]
                            sp.dma_start(dst, w[D // 2 * h:D // 2 * (h + 1), off:off + P].rearrange("(k p) n -> p k n", p=P)).then_inc(landed[c % NRAW][h], 16)
                    continue
                width = 24 if name == "gl" else 256
                load(first[f"win{l}"] + n, (KD, width), w[:, OFF[name] + 256 * j:OFF[name] + 256 * j + width])
            load_cols(f"wout{l}", io["w_out_2"][l], 256, D)
        for m in range(4):
            sp.wait_ge(*when(("otok", m)))
            sp.dma_start(io["out"][0].rearrange("(b p) n -> p b n", p=P)[:, :, T * m:T * m + T], otok[:, :, T * m:T * m + T]).then_inc(sem["out_landed"], 16)
        sp.wait_ge(sem["out_landed"], 16 * 4)

    @block.gpsimd
    def _(pool):
        did = Steps(at)
        nc.gpsimd.memset(ones[:, :], 1.0).then_inc(*did(pool_steps))
        nc.gpsimd.memset(eps[:, :], EPS).then_inc(*did(pool_steps, "memsets"))
        G = nc.gpsimd

        def modulation(f):
            l = f // 2
            steps, landed_ = sem["mod_steps"], sem["mod_landed"]
            pool.wait_ge(*when({0: "csf", 1: ("x", 2, 3), 2: ("x", 4, 3), 3: ("x", 6, 3)}[f]))
            if f:
                pool.wait_ge(*when(("modsum", f - 1)))
            for j in range(MOD):
                acc = mod_acc[:, j, :]
                n = MOD_STEPS * (MOD * f + j)
                for half in range(2):
                    if n:
                        pool.wait_ge(steps, n)
                    cols = slice(256 * (MOD * (f % 2) + j), 256 * (MOD * (f % 2) + j + 1))
                    pool.dma_start(mod_raw[:, :, :], io["w_ada_2"][l][512 * half:512 * half + 512, cols].rearrange("(k p) n -> p k n", p=P)).then_inc(landed_, 16)
                    pool.wait_ge(landed_, 16 * (2 * (MOD * f + j) + half + 1))
                    c = csf[:, KD // 2 * half:KD // 2 * (half + 1)].unsqueeze(2).to_broadcast([P, KD // 2, 256])
                    G.tensor_tensor(mod_raw[:, :, :], mod_raw[:, :, :], c, ALU.mult).then_inc(steps, 1)
                    pool.wait_ge(steps, n + 1)
                    G.tensor_tensor(mod_raw[:, 0:2, :], mod_raw[:, 0:2, :], mod_raw[:, 2:4, :], ALU.add).then_inc(steps, 1)
                    pool.wait_ge(steps, n + 2)
                    if half == 0:
                        G.tensor_tensor(acc, mod_raw[:, 0, :], mod_raw[:, 1, :], ALU.add).then_inc(steps, 1)
                    else:
                        G.tensor_tensor(mod_raw[:, 0, :], mod_raw[:, 0, :], mod_raw[:, 1, :], ALU.add).then_inc(steps, 1)
                        pool.wait_ge(steps, n + 3)
                        G.tensor_tensor(acc, acc, mod_raw[:, 0, :], ALU.add).then_inc(steps, 1)
                    n += 3

        def levels():
            pool.wait_ge(*when("scans"))

            def halves(t, L, hs):
                r = t[:, hs, :].rearrange("p h n -> p (h n)").rearrange("p (b two n) -> p b two n", two=2, n=L)
                return r[:, :, 0, :], r[:, :, 1, :]

            for n, L in enumerate(LEVELS):
                for half, hs in enumerate((slice(0, 4), slice(4, 8))):
                    bl, br = halves(hg_b, L, hs)
                    al, ar = halves(hg_a, L, hs)
                    end = bl[:, :, L - 1:L].to_broadcast([P, HEADS_A // 2 * T // (2 * L), L])
                    if n == 0:
                        G.tensor_copy(ar, br).then_inc(*did(pool_steps))
                    else:
                        pool.wait_ge(*when(("exp", n - 1, half)))
                        G.tensor_tensor(ar, br, end, ALU.subtract).then_inc(*did(pool_steps))
                    G.tensor_tensor(al, end, bl, ALU.subtract).then_inc(*did(pool_steps, ("diff", n, half)))
            G.tensor_tensor(hg_t[:, :].unsqueeze(2), hg_b[:, :, CHUNK_A - 1:CHUNK_A], hg_b[:, :, 2 * CHUNK_A - 1:2 * CHUNK_A], ALU.add).then_inc(*did(pool_steps))
            for half, hs in enumerate((slice(0, 4), slice(4, 8))):
                b = hg_b[:, hs, :].rearrange("p h (c n) -> p h c n", n=CHUNK_A)
                a = hg_a[:, hs, :].rearrange("p h (c n) -> p h c n", n=CHUNK_A)
                def end(c):
                    return b[:, :, c, CHUNK_A - 1:CHUNK_A].to_broadcast([P, HEADS_A // 2, CHUNK_A])
                pool.wait_ge(*did.last)
                pool.wait_ge(*when(("exp", 6, half)))
                G.tensor_tensor(a[:, :, 0, :], hg_t[:, hs].unsqueeze(2).to_broadcast([P, HEADS_A // 2, CHUNK_A]), b[:, :, 0, :], ALU.subtract).then_inc(*did(pool_steps))
                G.tensor_tensor(a[:, :, 1, :], end(1), b[:, :, 1, :], ALU.subtract).then_inc(*did(pool_steps))
                G.tensor_copy(a[:, :, 2, :], b[:, :, 2, :]).then_inc(*did(pool_steps))
                G.tensor_tensor(a[:, :, 3, :], b[:, :, 3, :], end(2), ALU.add).then_inc(*did(pool_steps, ("diff", 7, half)))

        def fold(s):
            pool.wait_ge(*when(("sq", s, 3)))
            G.tensor_tensor(sq[:, 0:4, :], sq[:, 0:4, :], sq[:, 4:8, :], ALU.add).then_inc(*did(pool_steps))
            pool.wait_ge(*did.last)
            G.tensor_tensor(sq[:, 0:2, :], sq[:, 0:2, :], sq[:, 2:4, :], ALU.add).then_inc(*did(pool_steps, ("folded", s)))

        fold(0)
        modulation(0)
        fold(1)
        levels()
        fold(2)
        modulation(1)
        pool.wait_ge(*when("rope"))
        G.memset(krz[:, :, :], 0.0).then_inc(*did(pool_steps))
        fold(3)
        modulation(2)
        fold(5)
        fold(6)
        modulation(3)
        fold(7)
        for m in range(4):
            pool.wait_ge(*when(("sq", 9, m)))
            gain = col0[:, 95 + 2 * m:97 + 2 * m].unsqueeze(2).to_broadcast([P, 2, T])
            G.tensor_tensor(X[:, 2 * m:2 * m + 2, :], X[:, 2 * m:2 * m + 2, :], gain, ALU.mult).then_inc(*did(pool_steps, ("x_gain", m)))
        pool.wait_ge(*when(("rs", 8)))
        for m in (2, 3):
            pool.wait_ge(*when(("x_gain", m)))
            G.tensor_tensor(X[:, 2 * m:2 * m + 2, :], X[:, 2 * m:2 * m + 2, :], rep(rs[:, :], 2), ALU.mult).then_inc(*did(pool_steps, ("x", 9, m)))
        pool.wait_ge(*when(("sums", 9)))
        for l in range(2):
            pool.wait_ge(*when(("x", 9 + l, 3)))
            for z in (kmz, vmz, ksz, kwz, vsz, vwz, kcz, vcz):
                last = nc.gpsimd.memset(z[tuple(slice(None) for _ in z.shape)], 0.0).then_inc(*did(pool_steps))
            nc.gpsimd.memset(small[:, 32:33], 0.0).then_inc(*did(pool_steps, ("zeros", l)))
            for kv, name in enumerate(("ck", "cv")):
                pool.dma_start(wc1[:, kv, :, :], io[f"w_{name}1_2"][l].rearrange("(r p) e -> p r e", p=P)).then_inc(sem["cmp_landed"], 16)
                for n in ((0, 1), (2,))[kv]:
                    pool.dma_start(wc2[:, n, :], io[f"w_{name}2_2"][l]).then_inc(sem["cmp_landed"], 16)
            pool.wait_ge(*when(("rs", 10 + 2 * l)))
            for j in (2, 3):
                G.tensor_tensor(y2[:, 2 * j:2 * j + 2, :], y2[:, 2 * j:2 * j + 2, :], rep(rs[:, :], 2), ALU.mult).then_inc(*did(pool_steps, ("y2_scaled", l, j)))

    @block.scalar
    def _(act):
        did = Steps(at)
        A = nc.scalar.activation

        others = [(pos_i[0:1, :], io["positions"]), (vrow1[0:88, :], io["rows1"]), (vrow2[0:64, :], io["rows2"])]
        act.dma_start(const[:, 0:P], io["consts"][:, 0:P]).then_inc(sem["ident_landed"], 16)
        act.dma_start(vrow0[0:103, :], io["rows0"]).then_inc(sem["gains_landed"], 16)

        def load_others():
            for dst, src in others:
                act.dma_start(dst, src).then_inc(sem["others_landed"], 16)

        def load_late():
            act.dma_start(const[:, P:], io["consts"][:, P:]).then_inc(sem["const_landed"], 16)
            for l in range(2):
                act.dma_start(ptok[:, l, :, :], io["p"][l, 0].rearrange("(b p) n -> p b n", p=P)).then_inc(sem["ple_landed"], 16)

        def hi(c, it=None, halves=(0, 1)):
            if c >= n_chunks:
                return
            i2 = 0 if it is None else 32 * it
            i4 = 0 if it is None else 4 * it
            for h in halves:
                act.wait_ge(landed[c % NRAW][h], 16 * landings[c][h] + i2)
                if c >= NSLOT and h == 0:
                    act.wait_ge(pe_groups, when(("chunk", c - NSLOT))[1] + i4)
                cols = half_columns(c, h)
                A(w_hi[:, c % NSLOT, cols], w_raw[:, c % NRAW, cols], ACT.Copy).then_inc(*did(hi_ready))

        def norm(nu, v, gain, s, free, late=()):
            if free is not None:
                act.wait_ge(*when(free))
            else:
                act.wait_ge(*when(("col", 0)))
            for m in range(4):
                act.wait_ge(*when(("x", v, m)))
                for k in (2 * m, 2 * m + 1):
                    A(xh[:, k, :], X[:, k, :], ACT.Copy, scale=gain(k)).then_inc(*did(act_steps, ("xh", nu, k)))
            if free is None:
                hi(1)
            if s is not None:
                if s > 0:
                    act.wait_ge(*when(("sums", s - 1)))
                for m in range(4):
                    A(sq[:, 2 * m:2 * m + 2, :], X[:, 2 * m:2 * m + 2, :], ACT.Square).then_inc(*did(act_steps, ("sq", s, m)))
            for c in late:
                hi(c)

        def root(s):
            act.wait_ge(*when(("sums", s)))
            if s > 0:
                act.wait_ge(*when(("rs", s - 1)))
            A(std[:, :], bank[sums_bank(s)][:, 0:T], ACT.Sqrt, bias=eps[:, :], scale=1.0 / D).then_inc(*did(act_steps, ("std", s)))

        def ffn(f, nu, v, gain, s, free, late=(), aside=None, before_out=None, summed=False):
            norm(nu, v, gain, None if summed else s, free, late)
            c = first[f"in{f}"]
            n0 = PAIRS * f

            def pair(c, p, it=None):
                o = 0 if it is None else 2 * it
                hi(c + AHEAD, it)
                act.wait_ge(gate_scaled, n0 + p + 2 + o)
                if it is not None or p >= 2:
                    act.wait_ge(hidden_ready, n0 + max(p - 1, 1) + o)
                A(silu_t[:, p % 2, :, :], gate_t[:, p % 2, :, :], ACT.Silu).then_inc(*did(silu_ready))
                hi(c + 1 + AHEAD, it)
                act.wait_ge(hidden_ready, n0 + p + 1 + o)
                k = bass.ds(2 * p + (0 if it is None else 4 * it), 2)
                A(hh[:, k, :], hid_t[:, p % 2, :, :], ACT.Copy).then_inc(*did(hidden_hi))

            def first_pair():
                hi(c + AHEAD)
                hi(c + 1 + AHEAD)
                if s is not None:
                    root(s)
                act.wait_ge(gate_scaled, n0 + 2)
                A(silu_t[:, 0, :, :], gate_t[:, 0, :, :], ACT.Silu).then_inc(*did(silu_ready))
                act.wait_ge(hidden_ready, n0 + 1)
                A(hh[:, 0:2, :], hid_t[:, 0, :, :], ACT.Copy).then_inc(*did(hidden_hi))

            first_pair()
            if aside is not None:
                aside()
            with act.Fori(0, (PAIRS - 1) // 2) as it:
                for j in range(2):
                    pair(c + 2 + 2 * j, 1 + j, it)
            turns_left = (PAIRS - 1) // 2 - 1
            did.skip(hi_ready, 8 * turns_left)
            did.skip(silu_ready, 2 * turns_left)
            did.skip(hidden_hi, 2 * turns_left)
            c = first[f"out{f}"]
            for q in range(2):
                hi(c + q + AHEAD)
            if before_out is not None:
                before_out()
            with act.Fori(0, 2) as it:
                for q in range(4):
                    hi(c + 2 + q + AHEAD, it)
            did.skip(hi_ready, 8)

        def rope_tables():
            act.wait_ge(*when("angles"))
            A(sin[:, :], red[:, :], ACT.Sin).then_inc(*did(act_steps))
            act.wait_ge(*when("quarter"))
            A(cos[:, :], mag[:, :], ACT.Sin).then_inc(*did(act_steps, "sin"))

        hi(0)
        load_others()

        def aside():
            act.wait_ge(*when("lb_shift"))
            A(small[:, 16:32], small[:, 0:16], ACT.Exp).then_inc(*did(act_steps, "lb_exp"))
            act.wait_ge(*when(("col", 1)))
            A(csf[:, :], col1[:, 80:88], ACT.Silu).then_inc(*did(act_steps, "csf"))

        act.wait_ge(*when("memsets"))
        ffn(0, 0, 0, g_norm(0, 0), 0, None, range(2, AHEAD), aside, load_late)

        c0 = first["hgrn"]
        norm(1, 1, g_norm(0, 1), 1, ("chunk", first["out0"] - 1), [c0 - 1 + AHEAD])
        for j in range(4):
            if j != 1:
                hi(c0 + j + AHEAD)
            if j == 0:
                hi(c0 + 1 + AHEAD)
                root(1)
            act.wait_ge(*when(("f", j)))
            A(hg_k[:, 2 * j:2 * j + 2, :], hg_a[:, 2 * j:2 * j + 2, :], ACT.Sigmoid, scale=-1.0).then_inc(*did(act_steps))
            act.wait_ge(*did.last)
            A(hg_a[:, 2 * j:2 * j + 2, :], hg_a[:, 2 * j:2 * j + 2, :], ACT.Sigmoid).then_inc(*did(act_steps, ("sg", j)))
        act.wait_ge(*did.last)
        act.wait_ge(*when("lb"))
        for h in range(HEADS_A):
            A(hg_a[:, h, :], hg_a[:, h, :], ACT.Ln, bias=lb[:, h:h + 1], scale=oml[:, h:h + 1]).then_inc(*did(act_steps, ("ln", h)))
        for j in range(4):
            hi(c0 + 4 + j + AHEAD)

        def level_exp(n):
            for half, hs in enumerate((slice(0, 4), slice(4, 8))):
                act.wait_ge(*when(("diff", n, half)))
                if n >= 2:
                    act.wait_ge(*when((("lev", n - 2), half)))
                elif n == 1 and half == 0:
                    act.wait_ge(*when(("sums", 1)))
                A(hg_f[n % 2][:, hs, :], hg_a[:, hs, :], ACT.Exp).then_inc(*did(act_steps, ("exp", n, half)))

        level_exp(0)
        for n in range(8):
            hi(c0 + 8 + n + AHEAD)
            if n < 7:
                level_exp(n + 1)
        act.wait_ge(*when(("g", 2)))
        A(hg_g[:, 0:6, :], hg_g[:, 0:6, :], ACT.Sigmoid).then_inc(*did(act_steps, ("gate_sg", 0)))
        for m in range(4):
            act.wait_ge(*when(("o", m)))
            A(sq[:, 2 * m:2 * m + 2, :], two(bank[4 + m][:, :]), ACT.Square).then_inc(*did(act_steps, ("osq", m)))
        for m in range(4):
            act.wait_ge(*when(("osum", m)))
            A(hg_a[:, 2 * m:2 * m + 2, :], two(bank[m][:, :]), ACT.Ln, bias=eps[:, :], scale=1.0 / P).then_inc(*did(act_steps, ("oln", m)))
        for m in range(4):
            act.wait_ge(*when(("oln", m)))
            A(hg_a[:, 2 * m:2 * m + 2, :], hg_a[:, 2 * m:2 * m + 2, :], ACT.Exp, scale=-0.5).then_inc(*did(act_steps, ("ors", m)))
        for m in range(4):
            if m == 3:
                act.wait_ge(*when(("g", 3)))
                A(hg_g[:, 6:8, :], hg_g[:, 6:8, :], ACT.Sigmoid).then_inc(*did(act_steps, ("gate_sg", 3)))
            act.wait_ge(*when(("og", m)))
            A(hg_oh[:, 2 * m:2 * m + 2, :], hg_b[:, 2 * m:2 * m + 2, :], ACT.Copy).then_inc(*did(act_steps, ("oh", m)))
        for j in range(3):
            hi(first["aout"] + j + AHEAD)

        def embedding(l):
            act.wait_ge(*when(("pt", l)))
            A(pth[:, :, :], pt[:, :, :], ACT.Copy).then_inc(*did(act_steps, ("pth", l)))

        ffn(1, 3, 2, g_norm(0, 2), 2, ("chunk", first["in1"] - 1), [first["in1"] - 1 + AHEAD], rope_tables, lambda: embedding(0))

        def ple(l, nu, v, s):
            c = first[f"ple{l}"]
            norm(nu, v, g_norm(l, 3), s, ("chunk", c - 1), [c - 1 + AHEAD, c + AHEAD])
            for j in range(4):
                if j != 1:
                    hi(c + 1 + j + AHEAD)
                if j == 0:
                    hi(c + 2 + AHEAD)
                    root(s)
                if l == 1 and j >= 1:
                    last_squares(j - 1)
                act.wait_ge(*when(("pg", l, j)))
                A(pg[:, 2 * j:2 * j + 2, :], pg[:, 2 * j:2 * j + 2, :], ACT.Sigmoid).then_inc(*did(act_steps, ("pgs", l, j)))

        def last_squares(m):
            pair_ = slice(2 * m, 2 * m + 2)
            act.wait_ge(*when(("x", 8, m)))
            A(sq[:, pair_, :], X[:, pair_, :], ACT.Square).then_inc(*did(act_steps, ("sq", 8, m)))
            for k in (2 * m, 2 * m + 1):
                A(sq_f[:, k, :], X[:, k, :], ACT.Square, scale=g_final(k)).then_inc(*did(act_steps, ("sq", 9, m)))

        ple(0, 4, 3, 3)

        norm(5, 4, g_kv, 4, ("chunk", first["kvd"] - 1))
        hi(first["kvd"] + AHEAD)
        hi(first["kvd"] + 1 + AHEAD)

        def latent_squares():
            act.wait_ge(*when("ck"))
            A(sq[:, 0:2, :], ck[:, :, :], ACT.Square).then_inc(*did(act_steps, "cksq"))

        def latent_split():
            act.wait_ge(*when("cksum"))
            A(std[:, :], bank[2][:, 0:T], ACT.Sqrt, bias=eps[:, :], scale=1.0 / 256).then_inc(*did(act_steps, "ckstd"))
            act.wait_ge(*when("ckn"))
            A(ckh[:, :, :], ck[:, :, :], ACT.Copy).then_inc(*did(act_steps, "ckh"))

        ffn(2, 6, 4, g_norm(1, 0), 4, ("chunk", first["in2"] - 1), (), latent_squares, latent_split, True)

        norm(7, 5, g_norm(1, 1), 5, ("chunk", first["out2"] - 1), [first["dq"] - 1 + AHEAD])
        c0 = first["dq"]
        for j in range(2):
            if j == 0:
                hi(c0 + AHEAD)
                hi(c0 + 1 + AHEAD)
                root(5)
            act.wait_ge(*when(("cq", j)))
            A(sq[:, 2 * j:2 * j + 2, :], cq[:, 2 * j:2 * j + 2, :], ACT.Square).then_inc(*did(act_steps, ("cqsq", j)))
        for u in range(4):
            hi(first["kvup"] + u + AHEAD)
            for b in range(TB):
                act.wait_ge(*when(("v", u, b)))
                A(vb[:, b, 512 * u:512 * u + 512], bank[4 * (u % 2) + 2 + b][:, :], ACT.Copy).then_inc(*did(act_steps, ("vb", u, b)))
            if u == 0:
                act.wait_ge(*when("cqsum"))
                A(std2[:, :], bank[4][:, 0:T], ACT.Sqrt, bias=eps[:, :], scale=1.0 / 512).then_inc(*did(act_steps, "cqstd"))
            if u == 1:
                for j in range(4):
                    act.wait_ge(*when(("cqn", j)))
                    A(cqh[:, j, :], cq[:, j, :], ACT.Copy).then_inc(*did(act_steps, ("cqh", j)))
        for u in range(8 - AHEAD):
            hi(first["uq"] + u + AHEAD)

        def exps(item, b0, s, nm, den, width=None):
            act.wait_ge(*when(("max", item)))
            i = item[-1]
            if i >= 3:
                act.wait_ge(*when(("pt", item[:-1] + (i - 3,))))
            for h in range(2):
                for t in range(TB):
                    n = (t + 1) * P
                    if width is None:
                        src, cols = bank[b0 + t][:, h * n:(h + 1) * n], slice(t * P, t * P + n)
                    else:
                        src, cols = bank[b0][:, (2 * t + h) * width:(2 * t + h + 1) * width], slice(16 * t, 16 * t + width)
                    A(s[:, h, cols], src, ACT.Exp, bias=nm[:, 2 * t + h:2 * t + h + 1],
                      accum_out=den[:, 2 * t + h:2 * t + h + 1]).then_inc(*did(act_steps, ("exps", item)))

        def probs_t(item, buf, width):
            act.wait_ge(*when(("pt", item)))
            for h in range(2):
                A(buf[:, h, 0:width], bank[4 + h][:, 0:width], ACT.Copy).then_inc(*did(act_steps, ("ptcopy", item)))

        for i in range(8):
            exps(("b", i), 2 * (i % 2), sB[:, i % 3], nmB[:, i % 3], denB[:, i % 3])
            if i >= 4:
                hi(first["bout"] + i - 4)
            if i >= 1:
                probs_t(("b", i - 1), ptB[:, (i - 1) % 2], 3 * P)
            if i >= 2:
                act.wait_ge(*when(("ob", i - 2)))
                A(oh[:, 2 * (i - 2):2 * (i - 2) + 2, :], two(bank[6 + i % 2][:, :]), ACT.Copy).then_inc(*did(act_steps, ("oh", "b", i - 2)))
        probs_t(("b", 7), ptB[:, 1], 3 * P)
        for i in (6, 7):
            act.wait_ge(*when(("ob", i)))
            A(oh[:, 2 * i:2 * i + 2, :], two(bank[6 + i % 2][:, :]), ACT.Copy).then_inc(*did(act_steps, ("oh", "b", i)))
        for j in range(1, 7):
            hi(first["bout"] + j + AHEAD)

        ffn(3, 8, 6, g_norm(1, 2), 6, ("chunk", first["in3"] - 1), [first["in3"] - 1 + AHEAD], None, lambda: embedding(1))
        ple(1, 9, 7, 7)

        def squares(v, s):
            for m in range(4):
                act.wait_ge(*when(("x", v, m)))
                if m == 0:
                    act.wait_ge(*when(("sums", s - 1)))
                A(sq[:, 2 * m:2 * m + 2, :], X[:, 2 * m:2 * m + 2, :], ACT.Square).then_inc(*did(act_steps, ("sq", s, m)))
            root(s)

        last_squares(3)
        root(8)
        act.wait_ge(*when("mean_f"))
        A(std[:, :], std[:, :], ACT.Sqrt, bias=eps[:, :], scale=1.0 / D).then_inc(*did(act_steps, ("std", 9)))

        for l in range(2):
            nu, v, s = 10 + 2 * l, 9 + l, 9 + 2 * l
            if l:
                squares(v, s)
                hi(first["win1"] + 1)
            for k in range(KD):
                act.wait_ge(*when(("xn", l, k)))
                A(xh[:, k, :], sq[:, k, :], ACT.Identity, bias=mods[:, l, k:k + 1]).then_inc(*did(act_steps, ("xh", nu, k)))
            c0 = first[f"win{l}"]
            if l:
                hi(c0 + 2)
            for n, (name, j) in enumerate(WIN):
                if n + AHEAD < 16:
                    hi(c0 + n + AHEAD)
                if n == 15:
                    act.wait_ge(*when(("gates_t", l)))
                    A(gates[:, :, :], two(bank[5][:, 0:64])[:, :, 0:24], ACT.Copy).then_inc(*did(act_steps, ("gates", l)))
                if name in ("zm", "zn"):
                    act.wait_ge(*when(("win", l, n)))
                    z = zm if name == "zm" else zn
                    A(z[:, 2 * j:2 * j + 2, :], two(bank[n % 8][:, :]), ACT.Silu).then_inc(*did(act_steps, ("z", l, n)))
                if name == "gl":
                    act.wait_ge(*when(("win", l, n)))
                    A(gates_f[:, :], bank[n % 8][0:24, 0:T], ACT.Sigmoid).then_inc(*did(act_steps, ("gates_f", l)))
            act.wait_ge(*when(("hid", l)))
            A(gh[:, 0:60], bank[0][0:DH, 0:60], ACT.Gelu_apprx_tanh).then_inc(*did(act_steps, ("gelu", l)))

            def tail(i):
                kind, m, start, stop = ITEMS[i]
                probs_t(("c", l, i), ptC[:, i % 2], 2 * P if kind == "cmp" else 3 * P)

            def y_hi(i):
                kind, m, start, stop = ITEMS[i]
                if stop:
                    k = m if kind == "moba" else 4 + m
                    act.wait_ge(*when(("y", l, k)))
                    A(xh[:, k, :], yC[:, k % 2, :], ACT.Copy).then_inc(*did(act_steps, ("yh", l, k)))

            for i, (kind, m, start, stop) in enumerate(ITEMS):
                exps(("c", l, i), 2 * (i % 2), sC[:, i % 3], nmC[:, i % 3], denC[:, i % 3], CMP_T if kind == "cmp" else None)
                if FIRST_HALF <= i < FIRST_HALF + 8:
                    hi(first[f"wout{l}"] + (i - FIRST_HALF) // 2, None, [(i - FIRST_HALF) % 2])
                if i >= 1:
                    tail(i - 1)
                if i >= 3:
                    y_hi(i - 3)
            tail(len(ITEMS) - 1)
            for i in range(len(ITEMS) - 3, len(ITEMS)):
                y_hi(i)
            s += 1
            for j in range(4):
                act.wait_ge(*when(("wout", l, j)))
                A(sq[:, 2 * j:2 * j + 2, :], two(bank[j][:, :]), ACT.Square).then_inc(*did(act_steps, ("sq", s, j)))
            root(s)
            hi(first[f"wout{l}"] + 4)
        for m in range(4):
            act.wait_ge(*when(("xout", m)))
            A(otok[:, :, T * m:T * m + T], two(bank[m][:, :]), ACT.Copy).then_inc(*did(act_steps, ("otok", m)))

    @block.tensor
    def _(pe):
        did = Steps(at)
        mm = nc.tensor.matmul
        release = {}

        def take(b):
            if b in release:
                pe.wait_ge(*when(release[b]))

        def keep_clock(n):
            take(7)
            for _ in range(n):
                mm(bank[7][:, 0:T], ones[:, :], const[:, 0:T], start=True, stop=True)

        def three(out, lhs, rhs, start, stop, skip=False):
            mm(out, lhs[1], rhs[0], start=start, stop=False, skip_group_check=skip)
            mm(out, lhs[0], rhs[1], start=False, stop=False, skip_group_check=skip)
            return mm(out, lhs[0], rhs[0], start=False, stop=stop, skip_group_check=skip)

        def split(c, k, cols=None):
            pair = [slot(w, c, k) for w in (w_hi, w_lo)]
            return pair

        def sums(s):
            b = sums_bank(s)
            take(b)
            tiles = 2 if s in FOLDED else KD
            for k in range(tiles):
                pe.wait_ge(*when(("folded", s) if s in FOLDED else ("sq", s, k // 2)))
                last = mm(bank[b][:, 0:T], ones[:, :], sq[:, k, :], start=(k == 0), stop=(k == tiles - 1))
            last.then_inc(*did(pe_groups, ("sums", s)))
            release[b] = ("std", s)

        def sums_pair(s, m, sq=sq):
            b = sums_bank(s)
            if m == 0:
                take(b)
            pe.wait_ge(*when(("sq", s, m)))
            for k in (2 * m, 2 * m + 1):
                last = mm(bank[b][:, 0:T], ones[:, :], sq[:, k, :], start=(k == 0), stop=(k == KD - 1))
            if m == 3:
                last.then_inc(*did(pe_groups, ("sums", s)))
                release[b] = ("std", s)

        def as_they_come(b, w, waits, xs=(xh, xl)):
            for k in range(KD):
                pe.wait_ge(*when(waits(k)))
                for n in range(2):
                    last = three(bank[b][:, n * T:(n + 1) * T], [a[:, k, n * P:(n + 1) * P] for a in w],
                                 [a[:, k, :] for a in xs], k == 0 and n == 0, k == KD - 1, True)
            return last

        def columns(c, b, xs, waits, name, tiles=2, kd=KD, width=256):
            take(b)
            pe.wait_ge(lo_ready, 2 * (c + 1))
            w = split(c, (kd, width))
            if waits is not None:
                last = as_they_come(b, w, waits, xs)
            else:
                for n in range(tiles):
                    for k in range(kd):
                        last = three(bank[b][:, n * T:(n + 1) * T], [a[:, k, n * P:(n + 1) * P] for a in w],
                                     [a[:, k, :] for a in xs], k == 0, k == kd - 1)
            last.then_inc(*did(pe_groups, name))
            at[("chunk", c)] = at[name]

        def tokens(c, b, xs, name, cols, kd=KD, width=256):
            take(b)
            pe.wait_ge(lo_ready, 2 * (c + 1))
            w = split(c, (kd, width))
            n = cols.stop - cols.start
            for t in range(TB):
                for k in range(kd):
                    last = three(bank[b][:, t * T:t * T + n],
                                 [a[:, k, t * P:(t + 1) * P] for a in xs], [a[:, k, cols] for a in w], k == 0, k == kd - 1)
            last.then_inc(*did(pe_groups, name))
            at[("chunk", c)] = at[name]

        def mod_sums(f):
            take(2)
            pe.wait_ge(sem["mod_steps"], MOD_STEPS * MOD * (f + 1))
            for n in range(2 * MOD):
                last = mm(bank[2][:, n:n + 1], mod_acc[:, n // 2, n % 2 * P:n % 2 * P + P], ones[:, 0:1], start=True, stop=True)
            last.then_inc(*did(pe_groups, ("modsum", f)))
            release[2] = ("mod", f)

        xs = (xh, xl)

        def xwait(nu):
            return lambda k: ("xl", nu, k)

        def ffn(f, nu, s, aside=None, before_out=None):
            c = first[f"in{f}"]
            n0 = PAIRS * f
            for b in range(4):
                take(b)

            def half(c, b, waits, it=None):
                pe.wait_ge(lo_ready, 2 * (c + 1) + (0 if it is None else 8 * it))
                w = split(c, (KD, 256))
                if waits:
                    return as_they_come(b, w, xwait(nu))
                for n in range(2):
                    for k in range(KD):
                        last = three(bank[b][:, n * T:(n + 1) * T], [a[:, k, n * P:(n + 1) * P] for a in w],
                                     [a[:, k, :] for a in xs], k == 0, k == KD - 1)
                return last

            half(c, 0, True).then_inc(*did(pe_groups, ("gate", f)))
            at[("chunk", c)] = at[("gate", f)]
            half(c + 1, 1, False).then_inc(*did(pe_groups, ("up", f)))
            at[("chunk", c + 1)] = at[("up", f)]
            if s is not None:
                sums(s)
            if aside is not None:
                aside()
            with pe.Fori(0, (PAIRS - 1) // 2) as it:
                for j in range(2):
                    p = 1 + j
                    b = 2 * (p % 2)
                    pe.wait_ge(gate_scaled, n0 + p + 2 * it)
                    half(c + 2 + 2 * j, b, False, it).then_inc(*did(pe_groups))
                    pe.wait_ge(up_scaled, n0 + p + 2 * it)
                    half(c + 3 + 2 * j, b + 1, False, it).then_inc(*did(pe_groups))
            start = did.count["pe_groups"] - 4
            for n in range(2 * (PAIRS - 1)):
                at[("chunk", c + 2 + n)] = ("pe_groups", start + 1 + n)
            did.skip(pe_groups, 2 * (PAIRS - 1) - 4)
            for b in range(2):
                release[b], release[2 + b] = ("ffn_" + "gu"[b], f, PAIRS - 1), ("ffn_" + "gu"[b], f, PAIRS - 2)
            if before_out is not None:
                before_out()
            c = first[f"out{f}"]
            for b in range(4, 8):
                take(b)

            def rows(c, q, it=None, only=None):
                pe.wait_ge(lo_ready, 2 * (c + 1) + (0 if it is None else 8 * it))
                pe.wait_ge(hidden_lo, n0 + q + 1 + (0 if it is None else 4 * it))
                w = split(c, (2, D))
                for n in range(KD):
                    for k in range(2):
                        kk = 2 * q + k if it is None else bass.ds(2 * q + k + 8 * it, 1)
                        xk = [a[:, kk, :] if it is None else a[:, kk, :].rearrange("p a n -> p (a n)") for a in (hh, hl)]
                        last = three(bank[4 + n // 2][:, (n % 2) * T:(n % 2 + 1) * T], [a[:, k, n * P:(n + 1) * P] for a in w],
                                     xk, it is None and q == 0 and n % 2 == 0 and k == 0, q == PAIRS - 1 and k == 1, True)
                    if q == PAIRS - 1 and n % 2:
                        last.then_inc(*did(pe_groups, ("ffn_out", f, n // 2)))
                return last

            for q in range(2):
                rows(c + q, q).then_inc(*did(pe_groups, ("chunk", c + q)))
            with pe.Fori(0, 2) as it:
                for q in range(4):
                    rows(c + 2 + q, 2 + q, it).then_inc(*did(pe_groups))
            start = at[("chunk", c + 1)][1]
            for n in range(8):
                at[("chunk", c + 2 + n)] = ("pe_groups", start + 1 + n)
            did.skip(pe_groups, 4)
            rows(c + PAIRS - 1, PAIRS - 1)
            at[("chunk", c + PAIRS - 1)] = at[("ffn_out", f, 3)]
            for m in range(4):
                release[4 + m] = ("x", {0: 1, 1: 3, 2: 5, 3: 7}[f], m)

        pe.wait_ge(sem["ident_landed"], 16)
        pe.wait_ge(sem["x_landed"], 16)
        for m in range(4):
            for n in range(2):
                for t in range(TB):
                    k = 2 * m + n
                    last = nc.tensor.transpose(bank[m][:, n * T + t * P:n * T + t * P + P], xtok[:, t, k * P:(k + 1) * P], ident)
            last.then_inc(*did(pe_groups, ("xin", m)))
            release[m] = ("x", 0, m)
        pe.wait_ge(sem["gains_landed"], 16)
        nc.tensor.transpose(bank[4][:, 0:103], vrow0[0:103, :], ident[0:103, 0:103]).then_inc(*did(pe_groups, ("cols", 0)))
        release[4] = ("col", 0)
        pe.wait_ge(*when("memsets"))

        def aside():
            pe.wait_ge(sem["others_landed"], 16 * 3)
            for n, (rows_, cnt) in ((1, (vrow1, 88)), (2, (vrow2, 64))):
                nc.tensor.transpose(bank[4 + n][:, 0:cnt], rows_[0:cnt, :], ident[0:cnt, 0:cnt]).then_inc(*did(pe_groups, ("cols", n)))
                release[4 + n] = ("col", n)

        def positions():
            take(7)
            pe.wait_ge(*when("pos_f"))
            mm(bank[7][:, 0:T], ones[0:1, :], turns[0:1, :], start=True, stop=True).then_inc(*did(pe_groups, "pos"))
            release[7] = "ang0"

        ffn(0, 0, 0, aside)

        c0 = first["hgrn"]
        for j in range(4):
            columns(c0 + j, 4 + j, xs, xwait(1) if j == 0 else None, ("pf", j))
            release[4 + j] = ("f", j)
            if j == 1:
                sums(1)
                mod_sums(0)
        for j in range(4):
            columns(c0 + 4 + j, 4 + j, xs, None, ("pq", j))
            release[4 + j] = ("q", j)
        pe.wait_ge(*when(("rs", 1)))
        take(3)
        for t in range(TB):
            last = nc.tensor.transpose(bank[3][:, t * P:(t + 1) * P], rs[:, t * P:(t + 1) * P], ident)
        last.then_inc(*did(pe_groups, "rst"))
        release[3] = "rst_copy"

        def scores(name, lhs, rhs, done):
            for m in range(4):
                take(m)
                for n in range(4):
                    h, t = 2 * m + n // 2, n % 2
                    last = mm(bank[m][:, n * P:(n + 1) * P], lhs[:, h, t * P:(t + 1) * P], rhs[:, h, t * P:(t + 1) * P], start=True, stop=True)
                last.then_inc(*did(pe_groups, (name, m)))
                release[m] = (done, m)

        pe.wait_ge(*when("k"))
        scores("diag", hg_k, hg_q, "diag_in")

        def level(n):
            L, f = LEVELS[n], hg_f[n % 2]
            for m in range(2):
                pe.wait_ge(*when(("factors", n, m)))
                b = 2 * (n % 2) + m
                take(b)
                for i in range(8):
                    h, t = 4 * m + i // 2, i % 2
                    keys = f[:, h, t * P:(t + 1) * P]
                    queries = keys.rearrange("p (b two n) -> p b two n", two=2, n=L)[:, :, 1, :]
                    last = mm(bank[b][:, i * P // 2:(i + 1) * P // 2], keys, queries, start=True, stop=True)
                last.then_inc(*did(pe_groups, (("lev", n), m)))
                release[b] = (("merge", n), m)

        for n in range(7):
            c, j = c0 + 8 + n, n % 4
            if n < 4:
                tokens(c, 4 + j, xs, ("pi", j), slice(0, 256))
                release[4 + j] = ("vi", j)
            else:
                columns(c, 4 + j, xs, None, ("pg", j))
                release[4 + j] = ("g", j)
            level(n)
        for m in range(2):
            pe.wait_ge(*when(("factors", 7, m)))
            take(2 + m)
            for n in range(4):
                h = 4 * m + n
                last = mm(bank[2 + m][:, n * P:(n + 1) * P], hg_f[1][:, h, 0:P], hg_f[1][:, h, P:T], start=True, stop=True)
            last.then_inc(*did(pe_groups, ("cross", m)))
            release[2 + m] = ("cross_in", m)
        pe.wait_ge(*when(("cross_in", 1)))
        for m in range(4):
            take(4 + m)
            for n in range(2):
                h = 2 * m + n
                o = bank[4 + m][:, n * T:(n + 1) * T]
                v = [hg_v[:, t, h * P:(h + 1) * P] for t in range(TB)]
                mm(o[:, 0:P], v[0], hg_s[:, h, 0, :], start=True, stop=True)
                mm(o[:, P:T], v[0], hg_x[:, h, :], start=True, stop=False)
                last = mm(o[:, P:T], v[1], hg_s[:, h, 1, :], start=False, stop=True)
            last.then_inc(*did(pe_groups, ("o", m)))
            release[4 + m] = ("og1", m)
        for m in range(4):
            take(m)
            pe.wait_ge(*when(("osq", m)))
            mm(bank[m][:, :], ones[:, :], sq[:, 2 * m:2 * m + 2, :].rearrange("p a n -> p (a n)"), start=True, stop=True).then_inc(*did(pe_groups, ("osum", m)))
            release[m] = ("oln", m)
        columns(c0 + 15, 0, xs, None, ("pg", 3))
        release[0] = ("g", 3)
        for j in range(4):
            columns(first["aout"] + j, 4 + j, (hg_oh, hg_ol), (lambda k: ("ol", k // 2)) if j == 0 else None, ("aout", j))
            release[4 + j] = ("x", 2, j)

        def embedding(l):
            pe.wait_ge(sem["ple_landed"], 32)
            take(2)
            for k in range(2):
                for t in range(TB):
                    last = nc.tensor.transpose(bank[2][:, k * T + t * P:k * T + t * P + P], ptok[:, l, t, k * P:(k + 1) * P], ident)
            last.then_inc(*did(pe_groups, ("ptin", l)))
            release[2] = ("pt", l)

        ffn(1, 3, 2, positions, lambda: embedding(0))

        def ple(l, nu, v, s):
            c = first[f"ple{l}"]
            pe.wait_ge(lo_ready, 2 * (c + 1))
            pe.wait_ge(*when(("ptl", l)))
            w = split(c, (2, D))
            for m in range(4):
                take(m)
                for n in (2 * m, 2 * m + 1):
                    for k in range(2):
                        last = three(bank[m][:, (n % 2) * T:(n % 2 + 1) * T], [a[:, k, n * P:(n + 1) * P] for a in w],
                                     [pth[:, k, :], ptl[:, k, :]], k == 0, k == 1)
                last.then_inc(*did(pe_groups, ("pp", l, m)))
                release[m] = ("ppc", l, m)
            at[("chunk", c)] = at[("pp", l, 3)]
            for j in range(4):
                columns(c + 1 + j, 4 + j, xs, xwait(nu) if j == 0 else None, ("pgate", l, j))
                release[4 + j] = ("pg", l, j)
                if j == 1:
                    sums(s)
                    mod_sums(2 * l + 1)

        ple(0, 4, 3, 3)

        keep_clock(5)
        c = first["kvd"]
        columns(c, 4, xs, xwait(5), "kd0")
        release[4] = "ck"
        take(5)
        pe.wait_ge(lo_ready, 2 * (c + 2))
        w = split(c + 1, (KD, P))
        for k in range(KD):
            last = three(bank[5][:, 0:T], [a[:, k, :] for a in w], [a[:, k, :] for a in xs], k == 0, k == KD - 1)
        last.then_inc(*did(pe_groups, ("chunk", c + 1)))
        release[5] = "kr"
        sums(4)

        def latent_sums():
            take(2)
            pe.wait_ge(*when("cksq"))
            for k in range(2):
                last = mm(bank[2][:, 0:T], ones[:, :], sq[:, k, :], start=(k == 0), stop=(k == 1))
            last.then_inc(*did(pe_groups, "cksum"))
            release[2] = "ckstd"
            take(3)
            pe.wait_ge(*when("kr"))
            mm(bank[3][:, 0:T], const[:, C_PERM:C_PERM + P], kr[:, :], start=True, stop=True).then_inc(*did(pe_groups, "krswap"))
            release[3] = "kr_sin"

        ffn(2, 6, None, None, latent_sums)

        for j in range(2):
            columns(first["dq"] + j, 4 + j, xs, xwait(7) if j == 0 else None, ("dq", j))
            release[4 + j] = ("cq", j)
            if j == 1:
                sums(5)
                mod_sums(2)
        pe.wait_ge(*when("ckl"))
        for u in range(4):
            c = first["kvup"] + u
            pe.wait_ge(lo_ready, 2 * (c + 1))
            w = split(c, (2, D))
            b0 = 4 * (u % 2)
            for n in range(2):
                take(b0 + n)
                for h in (2 * n, 2 * n + 1):
                    for k in range(2):
                        last = three(bank[b0 + n][:, (h % 2) * T:(h % 2 + 1) * T], [a[:, k, h * 256:h * 256 + P] for a in w],
                                     [ckh[:, k, :], ckl[:, k, :]], k == 0, k == 1)
                last.then_inc(*did(pe_groups, ("k", u, n)))
                release[b0 + n] = ("kn", u, n)
            for t in range(TB):
                take(b0 + 2 + t)
                for k in range(2):
                    vw = [a[:, k, :].rearrange("p (h e) -> p h e", h=4)[:, :, NOPE:NOPE + VDIM] for a in w]
                    last = three(bank[b0 + 2 + t][:, :], [a[:, k, t * P:(t + 1) * P] for a in (ckh, ckl)], vw, k == 0, k == 1)
                last.then_inc(*did(pe_groups, ("v", u, t)))
                release[b0 + 2 + t] = ("vb", u, t)
            at[("chunk", c)] = at[("v", u, 1)]
            if u == 0:
                take(4)
                for k in range(4):
                    pe.wait_ge(*when(("cqsq", k // 2)))
                    last = mm(bank[4][:, 0:T], ones[:, :], sq[:, k, :], start=(k == 0), stop=(k == 3))
                last.then_inc(*did(pe_groups, "cqsum"))
                release[4] = "cqstd"

        def swap(u):
            b = 4 + u % 2
            take(b)
            pe.wait_ge(*when(("qraw", u)))
            mm(bank[b][:, 0:T], const[:, C_PERM:C_PERM + P], qraw[:, u % 2, :], start=True, stop=True).then_inc(*did(pe_groups, ("qswap", u)))
            release[b] = ("q_sin", u)

        for u in range(8):
            c = first["uq"] + u
            pe.wait_ge(lo_ready, 2 * (c + 1))
            w = split(c, (4, 384))
            b0 = 2 * (u % 2)
            take(b0)
            for h in range(2):
                for k in range(4):
                    if u == 0 and h == 0:
                        pe.wait_ge(*when(("cql", k)))
                    last = three(bank[b0][:, h * T:(h + 1) * T], [a[:, k, h * NOPE:(h + 1) * NOPE] for a in w],
                                 [cqh[:, k, :], cql[:, k, :]], k == 0, k == 3)
            last.then_inc(*did(pe_groups, ("qnope", u)))
            release[b0] = ("qn", u)
            take(b0 + 1)
            for k in range(4):
                last = three(bank[b0 + 1][:, 0:T], [a[:, k, 2 * NOPE:] for a in w], [cqh[:, k, :], cql[:, k, :]], k == 0, k == 3)
            last.then_inc(*did(pe_groups, ("chunk", c)))
            release[b0 + 1] = ("qraw", u)
            if u >= 1:
                swap(u - 1)
        swap(7)

        def transposes(item, p):
            for h in range(2):
                take(4 + h)
            pe.wait_ge(*when(("probs", item)))
            for h in range(2):
                for n, (src, dst) in enumerate(((0, 0), (1, 1), (2, 2))):
                    last = nc.tensor.transpose(bank[4 + h][:, dst * P:(dst + 1) * P], p[:, h, src * P:(src + 1) * P], ident)
                release[4 + h] = ("ptcopy", item)
            last.then_inc(*did(pe_groups, ("pt", item)))

        def scores_b(i):
            pe.wait_ge(*when(("qr", i)))
            b0 = 2 * (i % 2)
            for t in range(TB):
                b = b0 + t
                take(b)
                n = (t + 1) * P
                o = bank[b][:, 0:2 * n]
                mm(o, qr[:, i, t * P:(t + 1) * P], krz[:, :, 0:n], start=True, stop=False, skip_group_check=True)
                for h in range(2):
                    mm(o[:, h * n:(h + 1) * n], qn[:, 2 * i + h, t * P:(t + 1) * P], kn[:, 2 * i + h, 0:n],
                       start=False, stop=(t == 1), skip_group_check=True)
                own = two(o)[:, :, t * P:n]
                last = mm(own, ident_bf[:, :], rep(caus_bf[:, :], 2), start=False, stop=True, skip_group_check=True)
                last.then_inc(*did(pe_groups, ("s", ("b", i), t)))
                release[b] = ("exps", ("b", i))

        def values_b(i):
            pe.wait_ge(*when(("ptcopy", ("b", i))))
            b = 6 + i % 2
            take(b)
            for h in range(2):
                o = bank[b][:, h * T:(h + 1) * T]
                v = [vb[:, t, (2 * i + h) * VDIM:(2 * i + h + 1) * VDIM] for t in range(TB)]
                mm(o[:, 0:P], v[0], ptB[:, i % 2, h, 0:P], start=True, stop=True)
                mm(o[:, P:T], v[0], ptB[:, i % 2, h, P:T], start=True, stop=False)
                last = mm(o[:, P:T], v[1], ptB[:, i % 2, h, T:T + P], start=False, stop=True)
            last.then_inc(*did(pe_groups, ("ob", i)))
            release[b] = ("ol", "b", i)

        c0 = first["bout"]

        def bout(q):
            if q == 0:
                for b in range(4):
                    take(b)
            pe.wait_ge(lo_ready, 2 * (c0 + q + 1))
            pe.wait_ge(*when(("ol", "b", q)))
            w = split(c0 + q, (2, D))
            for n in range(KD):
                for k in range(2):
                    last = three(bank[n // 2][:, (n % 2) * T:(n % 2 + 1) * T], [a[:, k, n * P:(n + 1) * P] for a in w],
                                 [oh[:, 2 * q + k, :], ol[:, 2 * q + k, :]], q == 0 and n % 2 == 0 and k == 0, q == 7 and k == 1, True)
                if q == 7 and n % 2:
                    last.then_inc(*did(pe_groups, ("bout", n // 2)))
            if q < 7:
                last.then_inc(*did(pe_groups, ("chunk", c0 + q)))

        scores_b(0)
        scores_b(1)
        for i in range(8):
            if i < 6:
                scores_b(i + 2)
            if i >= 1:
                values_b(i - 1)
            if i == 7:
                bout(0)
            transposes(("b", i), sB[:, i % 3])
        bout(1)
        values_b(7)
        for q in range(2, 8):
            bout(q)
        at[("chunk", c0 + 7)] = at[("bout", 3)]
        for m in range(4):
            release[m] = ("x", 6, m)

        ffn(3, 8, 6, None, lambda: embedding(1))
        ple(1, 9, 7, 7)
        for m in range(4):
            sums_pair(8, m)
            sums_pair(9, m, sq_f)
        release[sums_bank(9)] = "mean_f"

        for l in range(2):
            nu, v, s = 10 + 2 * l, 9 + l, 9 + 2 * l
            if l:
                sums(s)
            c0 = first[f"win{l}"]
            for n, (name, j) in enumerate(WIN):
                c, b = c0 + n, n % 8
                key = ("win", l, n)
                if name in ("qm", "km", "qn", "zm", "zn"):
                    columns(c, b, xs, xwait(nu) if n == 0 else None, key)
                    release[b] = ("z", l, n) if name[0] == "z" else ("proj", l, n)
                elif name in ("vm", "vsvw"):
                    tokens(c, b, xs, key, slice(0, 256))
                    release[b] = ("proj", l, n)
                elif name == "gl":
                    take(b)
                    pe.wait_ge(lo_ready, 2 * (c + 1))
                    w = split(c, (KD, 24))
                    for k in range(KD):
                        last = three(bank[b][0:24, 0:T], [a[:, k, :] for a in w], [a[:, k, :] for a in xs], k == 0, k == KD - 1)
                    last.then_inc(*did(pe_groups, key))
                    at[("chunk", c)] = at[key]
                    release[b] = ("gates_f", l)
                elif name in ("kcvc", "kskw"):
                    columns(c, b, xs, None, key)
                    release[b] = ("proj", l, n)
                if n == 14:
                    take(5)
                    for t in range(TB):
                        last = nc.tensor.transpose(bank[5][:, 32 * t:32 * t + 24], gates_f[0:24, t * P:(t + 1) * P], ident[0:24, 0:24])
                    last.then_inc(*did(pe_groups, ("gates_t", l)))
                    release[5] = ("gates", l)
                if name in ("kskw", "gl"):
                    half_ = 0 if name == "kskw" else 1
                    take(half_)
                    pe.wait_ge(*when(("kA", l, half_)))
                    mm(bank[half_][:, :], const[:, C_SWAP:C_SWAP + P], kA[:, 2 * half_:2 * half_ + 2, :].rearrange("p a n -> p (a n)"),
                       start=True, stop=True).then_inc(*did(pe_groups, ("kB", l, half_)))
                    release[half_] = ("kB_used", l, half_)
            take(0)
            pe.wait_ge(sem["cmp_landed"], 80 * (l + 1))
            for kv in range(2):
                pe.wait_ge(*when(("windows", l, kv)))
                for r in range(16):
                    last = mm(bank[0][0:DH, 30 * kv:30 * kv + 30], wc1[:, kv, r, :], win[:, kv, r, :], start=(r == 0), stop=(r == 15))
            last.then_inc(*did(pe_groups, ("hid", l)))
            release[0] = ("gelu", l)
            take(1)
            pe.wait_ge(*when(("gelu", l)))
            mm(bank[1][:, 0:30], wc2[:, 0:2, :].rearrange("p a n -> p (a n)"), gh[:, 0:30], start=True, stop=True).then_inc(*did(pe_groups, ("kcmp", l)))
            release[1] = ("kcz", l)
            take(2)
            for g in range(GROUPS):
                last = mm(bank[2][0:CMP_T, g * DH:(g + 1) * DH], gh[:, 30 + 15 * g:45 + 15 * g], wc2[:, 2, :], start=True, stop=True)
            last.then_inc(*did(pe_groups, ("vcmp", l)))
            release[2] = ("vcz", l)

            def scores_c(i):
                kind, m, _, _ = ITEMS[i]
                g = m // 2
                q = qm if kind == "moba" else qs
                b0 = 2 * (i % 2)
                if i == 0:
                    pe.wait_ge(*when(("attn", l)))
                    pe.wait_ge(*when(("z", l, 15)))
                if kind == "cmp":
                    take(b0)
                    for t in range(TB):
                        last = mm(bank[b0][:, t * 2 * CMP_T:(t + 1) * 2 * CMP_T], q[:, m, t * P:(t + 1) * P], kcz[:, g, :, 0:CMP_T], start=True, stop=False)
                        last = mm(bank[b0][:, t * 2 * CMP_T:(t + 1) * 2 * CMP_T], ident_bf[:, :], cbias[:, 2 * m:2 * m + 2, t, :], start=False, stop=True)
                    last.then_inc(*did(pe_groups, ("s", ("c", l, i), 1)))
                    release[b0] = ("exps", ("c", l, i))
                    return
                kz = {"moba": kmz[:, m], "slc": ksz[:, g], "win": kwz[:, g]}[kind]
                for t in range(TB):
                    b, n = b0 + t, (t + 1) * P
                    take(b)
                    mm(bank[b][:, 0:2 * n], q[:, m, t * P:(t + 1) * P], kz[:, :, 0:n], start=True, stop=False)
                    mm(bank[b][:, 0:2 * n], ident_bf[:, :], bias[:, 2 * m:2 * m + 2, T - n:T], start=False, stop=True).then_inc(*did(pe_groups, ("s", ("c", l, i), t)))
                    release[b] = ("exps", ("c", l, i))

            def transposes_c(i):
                if ITEMS[i][0] != "cmp":
                    return transposes(("c", l, i), sC[:, i % 3])
                for h in range(2):
                    take(4 + h)
                pe.wait_ge(*when(("probs", ("c", l, i))))
                for h in range(2):
                    for t in range(TB):
                        last = nc.tensor.transpose(bank[4 + h][0:16, t * P:(t + 1) * P], sC[:, i % 3, h, 16 * t:16 * t + 16], ident)
                    release[4 + h] = ("ptcopy", ("c", l, i))
                last.then_inc(*did(pe_groups, ("pt", ("c", l, i))))

            def values_c(i):
                kind, m, start, stop = ITEMS[i]
                g = m // 2
                k = m if kind == "moba" else 4 + m
                b = 6 + k % 2
                pe.wait_ge(*when(("ptcopy", ("c", l, i))))
                if start:
                    take(b)
                o = bank[b][:, 0:T]
                for h in range(2):
                    if kind == "cmp":
                        last = mm(o, vcz[0:CMP_T, g, h, :], ptC[0:CMP_T, i % 2, h, 0:T], start=False, stop=(h == 1), skip_group_check=True)
                        continue
                    v = {"moba": [vmz[:, t, 2 * m + h, :] for t in range(TB)],
                         "slc": [vsz[:, t, g, h, :] for t in range(TB)], "win": [vwz[:, t, g, h, :] for t in range(TB)]}[kind]
                    block0 = lambda: mm(o, v[0], ptC[:, i % 2, h, 0:T], start=(start and h == 0), stop=(stop and h == 1), skip_group_check=True)
                    block1 = lambda: mm(o[:, P:T], v[1], ptC[:, i % 2, h, T:T + P], start=False, stop=False, skip_group_check=True)
                    for product in ((block0, block1) if h == 0 else (block1, block0)):
                        last = product()
                last.then_inc(*did(pe_groups, ("oc", l, i)))
                if stop:
                    release[b] = ("y", l, k)

            def wout(k):
                pe.wait_ge(*when(("yl", l, k)))
                for j in range(4):
                    c = first[f"wout{l}"] + j
                    if k == 0:
                        take(j)
                        pe.wait_ge(lo_ready, 2 * (c + 1))
                    w = split(c, (KD, 256))
                    for i in range(2):
                        last = three(bank[j][:, i * T:(i + 1) * T], [a[:, k, i * P:(i + 1) * P] for a in w],
                                     [a[:, k, :] for a in xs], k == 0 and i == 0, k == KD - 1, True)
                    if k == KD - 1:
                        last.then_inc(*did(pe_groups, ("wout", l, j)))
                        at[("chunk", c)] = at[("wout", l, j)]
                        release[j] = ("y2", l, j)

            scores_c(0)
            scores_c(1)
            n_items = len(ITEMS)
            for i in range(n_items):
                if i + 2 < n_items:
                    scores_c(i + 2)
                if i == n_items - 1:
                    wout(0)
                if i >= 1:
                    values_c(i - 1)
                if i == n_items - 1:
                    wout(1)
                transposes_c(i)
            wout(2)
            wout(3)
            values_c(n_items - 1)
            for k in range(4, KD):
                wout(k)
            for m in range(4):
                sums_pair(s + 1, m)
            keep_clock(8)
        for m in range(4):
            take(m)
            pe.wait_ge(*when(("x", 11, m)))
            for t in range(TB):
                for k in (2 * m, 2 * m + 1):
                    last = nc.tensor.transpose(bank[m][:, t * T + k % 2 * P:t * T + k % 2 * P + P], X[:, k, t * P:(t + 1) * P], ident)
            last.then_inc(*did(pe_groups, ("xout", m)))

    @block.vector
    def _(dve):
        did = Steps(at)
        V = nc.vector

        def lo(c, it=None, halves=(0, 1)):
            if c >= n_chunks:
                return
            for h in halves:
                dve.wait_ge(hi_ready, 2 * c + h + 1 + (0 if it is None else 8 * it))
                cols = half_columns(c, h)
                V.tensor_tensor(w_lo[:, c % NSLOT, cols], w_raw[:, c % NRAW, cols], f32(w_hi[:, c % NSLOT, cols]), ALU.subtract).then_inc(*did(lo_ready))

        def norm(nu, gain, late=()):
            for k in range(KD):
                dve.wait_ge(*when(("xh", nu, k)))
                V.scalar_tensor_tensor(xl[:, k, :], X[:, k, :], gain(k), f32(xh[:, k, :]), ALU.mult, ALU.subtract).then_inc(*did(dve_steps, ("xl", nu, k)))
            for c in late:
                lo(c)

        def inv(s):
            dve.wait_ge(*when(("std", s)))
            dve.wait_ge(*did.last)
            V.reciprocal(rs[:, :], std[:, :]).then_inc(*did(dve_steps, ("rs", s)))
            dve.wait_ge(*did.last)

        def modulation(f):
            dve.wait_ge(*when(("modsum", f)))
            n = slice(2 * MOD * f, 2 * MOD * (f + 1))
            V.tensor_tensor(mods[:, :, :].rearrange("p l n -> p (l n)")[:, n], bank[2][:, 0:2 * MOD], col1[:, n], ALU.add).then_inc(*did(dve_steps, ("mod", f)))

        def ffn(f, nu, v, gain, s, late=(), aside=None, before_out=None):
            norm(nu, gain, late)
            c = first[f"in{f}"]
            n0 = PAIRS * f
            group0 = when(("gate", f))[1]
            up0 = when(("up", f))[1]
            pairs0 = when(("chunk", c + 2))[1] - 1

            def pair(c, p, it=None):
                o = 0 if it is None else 2 * it
                o4 = 0 if it is None else 4 * it
                b = 2 * (p % 2)
                lo(c + AHEAD, it)
                if it is None:
                    lo(c + 1 + AHEAD)
                    if s is not None:
                        inv(s)
                dve.wait_ge(pe_groups, (group0 if p == 0 else pairs0 + 2 * p - 1) + o4)
                if it is not None or p >= 2:
                    dve.wait_ge(silu_ready, n0 + max(p - 1, 1) + o)
                V.tensor_tensor(gate_t[:, p % 2, :, :], two(bank[b][:, :]), rep(rs[:, :], 2), ALU.mult).then_inc(*did(gate_scaled))
                if it is not None:
                    lo(c + 1 + AHEAD, it)
                dve.wait_ge(pe_groups, (up0 if p == 0 else pairs0 + 2 * p) + o4)
                if it is not None or p >= 2:
                    dve.wait_ge(hidden_ready, n0 + max(p - 1, 1) + o)
                V.tensor_tensor(up_t[:, p % 2, :, :], two(bank[b + 1][:, :]), rep(rs[:, :], 2), ALU.mult).then_inc(*did(up_scaled))
                dve.wait_ge(silu_ready, n0 + p + 1 + o)
                dve.wait_ge(up_scaled, n0 + p + 2 + o)
                if it is not None or p >= 2:
                    dve.wait_ge(hidden_hi, n0 + max(p - 1, 1) + o)
                    dve.wait_ge(hidden_lo, n0 + max(p - 1, 1) + o)
                V.tensor_tensor(hid_t[:, p % 2, :, :], silu_t[:, p % 2, :, :], up_t[:, p % 2, :, :], ALU.mult).then_inc(*did(hidden_ready))
                dve.wait_ge(hidden_hi, n0 + p + 1 + o)
                k = bass.ds(2 * p + (0 if it is None else 4 * it), 2)
                V.tensor_tensor(hl[:, k, :], hid_t[:, p % 2, :, :], f32(hh[:, k, :]), ALU.subtract).then_inc(*did(hidden_lo))

            pair(c, 0)
            if aside is not None:
                aside()
            with dve.Fori(0, (PAIRS - 1) // 2) as it:
                for j in range(2):
                    pair(c + 2 + 2 * j, 1 + j, it)
            turns_left = (PAIRS - 1) // 2 - 1
            did.skip(lo_ready, 8 * turns_left)
            for q in (gate_scaled, up_scaled, hidden_ready, hidden_lo):
                did.skip(q, 2 * turns_left)
            for p in (PAIRS - 2, PAIRS - 1):
                at[("ffn_g", f, p)], at[("ffn_u", f, p)] = ("gate_scaled", n0 + p + 2), ("up_scaled", n0 + p + 2)
            c = first[f"out{f}"]
            for q in range(2):
                lo(c + q + AHEAD)
            if before_out is not None:
                before_out()
            with dve.Fori(0, 2) as it:
                for q in range(4):
                    lo(c + 2 + q + AHEAD, it)
            did.skip(lo_ready, 8)
            for m in range(4):
                dve.wait_ge(*when(("ffn_out", f, m)))
                V.scalar_tensor_tensor(X[:, 2 * m:2 * m + 2, :], two(bank[4 + m][:, :]), 0.5, X[:, 2 * m:2 * m + 2, :], ALU.mult, ALU.add).then_inc(*did(dve_steps, ("x", v + 1, m)))

        for m in range(4):
            if m == 2:
                lo(0)
            dve.wait_ge(*when(("xin", m)))
            V.tensor_copy(X[:, 2 * m:2 * m + 2, :], two(bank[m][:, :])).then_inc(*did(dve_steps, ("x", 0, m)))
        V.memset(small[:, 50:51], 0.0).then_inc(*did(gate_scaled))
        V.memset(small[:, 51:52], 0.0).then_inc(*did(up_scaled))
        dve.wait_ge(*when(("cols", 0)))
        V.tensor_copy(col0[:, 0:103], bank[4][:, 0:103]).then_inc(*did(dve_steps, ("col", 0)))

        def aside():
            dve.wait_ge(sem["others_landed"], 16 * 3)
            V.tensor_copy(turns[0:1, :], pos_i[0:1, :]).then_inc(*did(dve_steps, "pos_f"))
            V.tensor_copy(ident_bf[:, :], ident).then_inc(*did(dve_steps))
            for n, (col, cnt) in ((1, (col1, 88)), (2, (col2, 64))):
                dve.wait_ge(*when(("cols", n)))
                V.tensor_copy(col[:, 0:cnt], bank[4 + n][:, 0:cnt]).then_inc(*did(dve_steps, ("col", n)))
            V.tensor_max(small[:, 32:40], col0[:, 64:72], col0[:, 72:80]).then_inc(*did(dve_steps))
            dve.wait_ge(*did.last)
            V.tensor_tensor(two(small[:, 0:16]), two(col0[:, 64:80]), rep(small[:, 32:40], 2), ALU.subtract).then_inc(*did(dve_steps, "lb_shift"))
            dve.wait_ge(*when("lb_exp"))
            V.tensor_tensor(small[:, 32:40], small[:, 16:24], small[:, 24:32], ALU.add).then_inc(*did(dve_steps))
            dve.wait_ge(*did.last)
            V.reciprocal(small[:, 40:48], small[:, 32:40]).then_inc(*did(dve_steps))
            dve.wait_ge(*did.last)
            V.tensor_tensor(lb[:, :], small[:, 16:24], small[:, 40:48], ALU.mult).then_inc(*did(dve_steps))
            dve.wait_ge(*did.last)
            V.tensor_scalar(oml[:, :], lb[:, :], -1.0, 1.0, ALU.mult, ALU.add).then_inc(*did(dve_steps, "lb"))

        def angles():
            dve.wait_ge(*when("pos"))
            V.tensor_scalar(ang[:, :], bank[7][:, 0:T], const[:, C_FREQ:C_FREQ + 1], None, ALU.mult).then_inc(*did(dve_steps, "ang0"))
            dve.wait_ge(*did.last)
            V.tensor_scalar(turns[:, :], ang[:, :], float(1 / (2 * np.pi)), None, ALU.mult).then_inc(*did(dve_steps))
            big = float(1.5 * 2 ** 23)
            for step in (big, -big):
                dve.wait_ge(*did.last)
                V.tensor_scalar(turns[:, :], turns[:, :], step, None, ALU.add).then_inc(*did(dve_steps))
            part1 = 6.28125
            part2 = float(np.float32(np.round((2 * np.pi - part1) * 2 ** 20) / 2 ** 20))
            part3 = float(np.float32(2 * np.pi - part1 - part2))
            src = ang
            for part in (part1, part2, part3):
                dve.wait_ge(*did.last)
                V.scalar_tensor_tensor(red[:, :], turns[:, :], -part, src[:, :], ALU.mult, ALU.add).then_inc(*did(dve_steps))
                src = red
            dve.wait_ge(*did.last)
            V.tensor_scalar(red[:, :], red[:, :], 3.1415925, -3.1415925, ALU.min, ALU.max).then_inc(*did(dve_steps, "angles"))
            dve.wait_ge(*did.last)
            V.tensor_scalar(mag[:, :], red[:, :], -1.0, None, ALU.mult).then_inc(*did(dve_steps))
            dve.wait_ge(*did.last)
            V.tensor_tensor(mag[:, :], mag[:, :], red[:, :], ALU.max).then_inc(*did(dve_steps))
            dve.wait_ge(*did.last)
            V.tensor_scalar(mag[:, :], mag[:, :], -1.0, float(np.pi / 2), ALU.mult, ALU.add).then_inc(*did(dve_steps, "quarter"))
            dve.wait_ge(*when("sin"))
            V.tensor_scalar(sin[:, :], sin[:, :], const[:, C_SIGN:C_SIGN + 1], None, ALU.mult).then_inc(*did(dve_steps, "rope"))

        ffn(0, 0, 0, g_norm(0, 0), 0, range(1, AHEAD), aside)

        c0 = first["hgrn"]
        norm(1, g_norm(0, 1), [c0 - 1 + AHEAD])
        for j in range(4):
            if j != 1:
                lo(c0 + j + AHEAD)
            if j == 0:
                lo(c0 + 1 + AHEAD)
                inv(1)
            dve.wait_ge(*when(("pf", j)))
            if j == 2:
                modulation(0)
            V.tensor_tensor(hg_a[:, 2 * j:2 * j + 2, :], two(bank[4 + j][:, :]), rep(rs[:, :], 2), ALU.mult).then_inc(*did(dve_steps, ("f", j)))
        for j in range(4):
            lo(c0 + 4 + j + AHEAD)
            dve.wait_ge(*when(("pq", j)))
            V.scalar_tensor_tensor(hg_q[:, 2 * j:2 * j + 2, :], two(bank[4 + j][:, :]), float(P ** -0.5), rep(rs[:, :], 2), ALU.mult, ALU.mult).then_inc(*did(dve_steps, ("q", j)))
            dve.wait_ge(*when(("sg", j)))
            for h in (2 * j, 2 * j + 1):
                V.tensor_scalar(hg_k[:, h, :], hg_k[:, h, :], oml[:, h:h + 1], None, ALU.mult).then_inc(*did(dve_steps, "k"))
        dve.wait_ge(sem["const_landed"], 16)
        V.tensor_copy(caus_bf[:, :], const[:, C_CAUS:C_CAUS + P]).then_inc(*did(dve_steps))
        for h in range(HEADS_A):
            dve.wait_ge(*when(("ln", h)))
            V.tensor_tensor_scan(hg_b[:, h, :], const[:, C_RESET:C_RESET + T], hg_a[:, h, :], 0.0, ALU.mult, ALU.add).then_inc(*did(dve_steps, "scans"))
        dve.wait_ge(*when("rst"))
        V.tensor_copy(rst[:, :], two(bank[3][:, 0:T])[:, :, 0:1].rearrange("p a n -> p (a n)")).then_inc(*did(dve_steps, "rst_copy"))
        dve.wait_ge(*did.last)

        def factors(n):
            L = LEVELS[n] if n < 7 else P
            for half, hs in enumerate((slice(0, 4), slice(4, 8))):
                dve.wait_ge(*when(("exp", n, half)))
                halves = [t[:, hs, :].rearrange("p h n -> p (h n)").rearrange("p (b two n) -> p b two n", two=2, n=L) for t in (hg_f[n % 2], hg_k, hg_q)]
                V.tensor_tensor(halves[0][:, :, 0, :], halves[0][:, :, 0, :], halves[1][:, :, 0, :], ALU.mult).then_inc(*did(dve_steps))
                V.tensor_tensor(halves[0][:, :, 1, :], halves[0][:, :, 1, :], halves[2][:, :, 1, :], ALU.mult).then_inc(*did(dve_steps, ("factors", n, half)))

        def diag_view(m):
            return hg_s[:, 2 * m:2 * m + 2, :, :]

        for m in range(4):
            dve.wait_ge(*when(("diag", m)))
            V.tensor_tensor(diag_view(m), bank[m][:, :].rearrange("p (h t n) -> p h t n", h=2, t=2),
                            rep(rep(ident, 2), 2), ALU.mult).then_inc(*did(dve_steps, ("diag_in", m)))
        factors(0)

        def merge(n):
            L = LEVELS[n]
            mask = const[:, C_LVL + n * P // 2:C_LVL + (n + 1) * P // 2].bitcast(U32).rearrange("p (b n) -> p b n", n=L)
            for m in range(2):
                dve.wait_ge(*when((("lev", n), m)))
                dve.wait_ge(*did.last)
                right = hg_s[:, 4 * m:4 * m + 4, :, :].rearrange("p h t n -> p (h t) n").rearrange("p x (b two n) -> p x b two n", two=2, n=L)[:, :, :, 1, :]
                V.copy_predicated(right, rep(mask, 8), bank[2 * (n % 2) + m][:, :].rearrange("p (x b n) -> p x b n", x=8, n=L)).then_inc(*did(dve_steps, (("merge", n), m)))

        def gates_in(j, b):
            dve.wait_ge(*when(("pg", j)))
            V.tensor_tensor(hg_g[:, 2 * j:2 * j + 2, :], two(b[:, :]), rep(rs[:, :], 2), ALU.mult).then_inc(*did(dve_steps, ("g", j)))

        for n in range(8):
            j = n % 4
            lo(c0 + 8 + n + AHEAD)
            if n < 4:
                dve.wait_ge(*when(("pi", j)))
                for t in range(TB):
                    V.tensor_scalar(hg_v[:, t, 256 * j:256 * j + 256], bank[4 + j][:, t * T:(t + 1) * T], rst[:, t:t + 1], None, ALU.mult).then_inc(*did(dve_steps, ("vi", j)))
            elif n < 7:
                gates_in(j, bank[4 + j])
            if n < 6:
                merge(n)
                factors(n + 1)
            elif n == 6:
                factors(7)
                merge(6)
        for m in range(2):
            dve.wait_ge(*when(("cross", m)))
            V.tensor_copy(hg_x[:, 4 * m:4 * m + 4, :], bank[2 + m][:, :].rearrange("p (h n) -> p h n", h=4)).then_inc(*did(dve_steps, ("cross_in", m)))
        dve.wait_ge(*when(("gate_sg", 0)))
        for m in range(3):
            pair_ = slice(2 * m, 2 * m + 2)
            dve.wait_ge(*when(("osq", m)))
            V.scalar_tensor_tensor(hg_b[:, pair_, :], two(bank[4 + m][:, :]), out_gain, hg_g[:, pair_, :], ALU.mult, ALU.mult).then_inc(*did(dve_steps, ("og1", m)))

        def out_lo(m):
            pair_ = slice(2 * m, 2 * m + 2)
            dve.wait_ge(*when(("oh", m)))
            V.tensor_tensor(hg_ol[:, pair_, :], hg_b[:, pair_, :], f32(hg_oh[:, pair_, :]), ALU.subtract).then_inc(*did(dve_steps, ("ol", m)))

        for m in range(3):
            pair_ = slice(2 * m, 2 * m + 2)
            dve.wait_ge(*when(("ors", m)))
            dve.wait_ge(*when(("og1", m)))
            V.tensor_tensor(hg_b[:, pair_, :], hg_b[:, pair_, :], hg_a[:, pair_, :], ALU.mult).then_inc(*did(dve_steps, ("og", m)))
        dve.wait_ge(*when(("ors", 3)))
        V.scalar_tensor_tensor(hg_b[:, 6:8, :], two(bank[7][:, :]), out_gain, hg_a[:, 6:8, :], ALU.mult, ALU.mult).then_inc(*did(dve_steps, ("og1", 3)))
        out_lo(0)
        out_lo(1)
        gates_in(3, bank[0])
        out_lo(2)
        dve.wait_ge(*when(("gate_sg", 3)))
        V.tensor_tensor(hg_b[:, 6:8, :], hg_b[:, 6:8, :], hg_g[:, 6:8, :], ALU.mult).then_inc(*did(dve_steps, ("og", 3)))
        out_lo(3)

        def add_x(v, name, b0):
            for j in range(4):
                if j < 3:
                    yield j
                dve.wait_ge(*when(name + (j,)))
                V.tensor_tensor(X[:, 2 * j:2 * j + 2, :], X[:, 2 * j:2 * j + 2, :], two(bank[b0 + j][:, :]), ALU.add).then_inc(*did(dve_steps, ("x", v, j)))

        for j in add_x(2, ("aout",), 4):
            lo(first["aout"] + j + AHEAD)

        def embedding(l):
            dve.wait_ge(*when(("ptin", l)))
            V.tensor_copy(pt[:, :, :], two(bank[2][:, :])).then_inc(*did(dve_steps, ("pt", l)))
            dve.wait_ge(*when(("pth", l)))
            V.tensor_tensor(ptl[:, :, :], pt[:, :, :], f32(pth[:, :, :]), ALU.subtract).then_inc(*did(dve_steps, ("ptl", l)))

        ffn(1, 3, 2, g_norm(0, 2), 2, [first["in1"] - 1 + AHEAD], angles, lambda: embedding(0))

        def ple(l, nu, v, s):
            c = first[f"ple{l}"]
            norm(nu, g_norm(l, 3), [c - 1 + AHEAD, c + AHEAD])
            for m in range(4):
                dve.wait_ge(*when(("pp", l, m)))
                V.tensor_copy(pp[:, 2 * m:2 * m + 2, :], two(bank[m][:, :])).then_inc(*did(dve_steps, ("ppc", l, m)))

            def finish(j):
                pair_ = slice(2 * j, 2 * j + 2)
                dve.wait_ge(*when(("pgs", l, j)))
                V.tensor_tensor(pg[:, pair_, :], pg[:, pair_, :], pp[:, pair_, :], ALU.mult).then_inc(*did(dve_steps))
                dve.wait_ge(*did.last)
                V.tensor_tensor(X[:, pair_, :], X[:, pair_, :], pg[:, pair_, :], ALU.add).then_inc(*did(dve_steps, ("x", v + 1, j)))

            for j in range(4):
                if j != 1:
                    lo(c + 1 + j + AHEAD)
                if j == 0:
                    lo(c + 2 + AHEAD)
                    inv(s)
                dve.wait_ge(*when(("pgate", l, j)))
                if j == 2:
                    modulation(2 * l + 1)
                V.tensor_tensor(pg[:, 2 * j:2 * j + 2, :], two(bank[4 + j][:, :]), rep(rs[:, :], 2), ALU.mult).then_inc(*did(dve_steps, ("pg", l, j)))
                finish(j)

        ple(0, 4, 3, 3)

        norm(5, g_kv)
        lo(first["kvd"] + AHEAD)
        lo(first["kvd"] + 1 + AHEAD)

        def latent():
            dve.wait_ge(*when("kd0"))
            V.tensor_tensor(ck[:, :, :], two(bank[4][:, :]), rep(rs[:, :], 2), ALU.mult).then_inc(*did(dve_steps, "ck"))
            dve.wait_ge(*when(("chunk", first["kvd"] + 1)))
            V.tensor_tensor(kr[:, :], bank[5][:, 0:T], rs[:, :], ALU.mult).then_inc(*did(dve_steps, "kr"))
            dve.wait_ge(*did.last)
            V.tensor_tensor(kr_t[:, 0, :], kr[:, :], cos[:, :], ALU.mult).then_inc(*did(dve_steps))

        def latent_split():
            dve.wait_ge(*when("ckstd"))
            V.reciprocal(rs2_kv[:, :], std[:, :]).then_inc(*did(dve_steps))
            dve.wait_ge(*did.last)
            for k in range(2):
                V.scalar_tensor_tensor(ck[:, k, :], ck[:, k, :], g_latent(k), rs2_kv[:, :], ALU.mult, ALU.mult).then_inc(*did(dve_steps, "ckn"))
            dve.wait_ge(*when("krswap"))
            V.tensor_tensor(kr_t[:, 1, :], bank[3][:, 0:T], sin[:, :], ALU.mult).then_inc(*did(dve_steps, "kr_sin"))
            dve.wait_ge(*did.last)
            for h in range(2):
                rows_ = slice(h * ROPE, (h + 1) * ROPE)
                V.tensor_tensor(krz[rows_, h, :], kr_t[rows_, 0, :], kr_t[rows_, 1, :], ALU.add).then_inc(*did(dve_steps))
            dve.wait_ge(*when("ckh"))
            V.tensor_tensor(ckl[:, :, :], ck[:, :, :], f32(ckh[:, :, :]), ALU.subtract).then_inc(*did(dve_steps, "ckl"))

        ffn(2, 6, 4, g_norm(1, 0), 4, (), latent, latent_split)

        norm(7, g_norm(1, 1), [first["dq"] - 1 + AHEAD])
        for j in range(2):
            if j == 0:
                lo(first["dq"] + AHEAD)
                lo(first["dq"] + 1 + AHEAD)
                inv(5)
            dve.wait_ge(*when(("dq", j)))
            if j == 1:
                modulation(2)
            V.tensor_tensor(cq[:, 2 * j:2 * j + 2, :], two(bank[4 + j][:, :]), rep(rs[:, :], 2), ALU.mult).then_inc(*did(dve_steps, ("cq", j)))
        for u in range(4):
            lo(first["kvup"] + u + AHEAD)
            for n in range(2):
                dve.wait_ge(*when(("k", u, n)))
                V.tensor_copy(kn[:, 4 * u + 2 * n:4 * u + 2 * n + 2, :], two(bank[4 * (u % 2) + n][:, :])).then_inc(*did(dve_steps, ("kn", u, n)))
            if u == 0:
                dve.wait_ge(*when("cqstd"))
                V.reciprocal(rs2[:, :], std2[:, :]).then_inc(*did(dve_steps))
                dve.wait_ge(*did.last)
                for k in range(4):
                    V.scalar_tensor_tensor(cq[:, k, :], cq[:, k, :], g_q(k), rs2[:, :], ALU.mult, ALU.mult).then_inc(*did(dve_steps, ("cqn", k)))
        for k in range(4):
            dve.wait_ge(*when(("cqh", k)))
            V.tensor_tensor(cql[:, k, :], cq[:, k, :], f32(cqh[:, k, :]), ALU.subtract).then_inc(*did(dve_steps, ("cql", k)))

        def rotate(u):
            dve.wait_ge(*when(("qswap", u)))
            dve.wait_ge(*did.last)
            V.tensor_tensor(qr_t[:, 1, :], bank[4 + u % 2][:, 0:T], sin[:, :], ALU.mult).then_inc(*did(dve_steps, ("q_sin", u)))
            V.tensor_tensor(qr_t[:, 0, :], qraw[:, u % 2, :], cos[:, :], ALU.mult).then_inc(*did(dve_steps))
            dve.wait_ge(*did.last)
            V.tensor_tensor(qr[:, u, :], qr_t[:, 0, :], qr_t[:, 1, :], ALU.add).then_inc(*did(dve_steps, ("qr", u)))

        for u in range(8):
            if u + AHEAD < 8:
                lo(first["uq"] + u + AHEAD)
            dve.wait_ge(*when(("qnope", u)))
            V.tensor_scalar(qn[:, 2 * u:2 * u + 2, :], two(bank[2 * (u % 2)][:, :]), SCALE_B, None, ALU.mult).then_inc(*did(dve_steps, ("qn", u)))
            dve.wait_ge(*when(("chunk", first["uq"] + u)))
            if u >= 2:
                dve.wait_ge(*when(("qr", u - 2)))
            V.tensor_scalar(qraw[:, u % 2, :], bank[2 * (u % 2) + 1][:, 0:T], SCALE_B, None, ALU.mult).then_inc(*did(dve_steps, ("qraw", u)))
            if u >= 1:
                rotate(u - 1)
        rotate(7)

        def maxima(item, b0, nm):
            for t in range(TB):
                dve.wait_ge(*when(("s", item, t)))
                V.tensor_reduce(nm[:, 2 * t:2 * t + 2], two(bank[b0 + t][:, 0:2 * (t + 1) * P]), AX.X, ALU.max, negate=True).then_inc(*did(dve_steps, ("max", item)))

        def maxima_b(i):
            maxima(("b", i), 2 * (i % 2), nmB[:, i % 3])

        def weigh(item, s, den, rd, gate=None, valid=False, width=None):
            dve.wait_ge(*when(("exps", item)))
            dve.wait_ge(*did.last)
            V.reciprocal(rd[:, :], den[:, :]).then_inc(*did(dve_steps))
            if valid:
                dve.wait_ge(*did.last)
                V.tensor_tensor(two(rd[:, :]), two(rd[:, :]), const[:, C_ROWV:C_ROWV + 2].unsqueeze(2).to_broadcast([P, 2, 2]), ALU.mult).then_inc(*did(dve_steps))
            if gate is not None:
                dve.wait_ge(*did.last)
                V.tensor_tensor(two(rd[:, :]), two(rd[:, :]), gate, ALU.mult).then_inc(*did(dve_steps))
            dve.wait_ge(*did.last)
            for h in range(2):
                for t in range(TB):
                    cols = (slice(0, P) if t == 0 else slice(P, 3 * P)) if width is None else slice(16 * t, 16 * t + width)
                    V.tensor_scalar(s[:, h, cols], s[:, h, cols], rd[:, 2 * t + h:2 * t + h + 1], None, ALU.mult).then_inc(*did(dve_steps, ("probs", item)))

        def out_b(i):
            dve.wait_ge(*when(("oh", "b", i)))
            V.tensor_tensor(ol[:, 2 * i:2 * i + 2, :], two(bank[6 + i % 2][:, :]), f32(oh[:, 2 * i:2 * i + 2, :]), ALU.subtract).then_inc(*did(dve_steps, ("ol", "b", i)))

        maxima_b(0)
        maxima_b(1)
        for i in range(8):
            weigh(("b", i), sB[:, i % 3], denB[:, i % 3], rdB[:, i % 3])
            if i >= 2:
                out_b(i - 2)
            if i < 6:
                maxima_b(i + 2)
            if i >= 4:
                lo(first["bout"] + i - 4)
        for i in (6, 7):
            out_b(i)
        for j in range(1, 7):
            lo(first["bout"] + j + AHEAD)
        for m in range(4):
            dve.wait_ge(*when(("bout", m)))
            V.tensor_tensor(X[:, 2 * m:2 * m + 2, :], X[:, 2 * m:2 * m + 2, :], two(bank[m][:, :]), ALU.add).then_inc(*did(dve_steps, ("x", 6, m)))

        ffn(3, 8, 6, g_norm(1, 2), 6, [first["in3"] - 1 + AHEAD], None, lambda: embedding(1))
        ple(1, 9, 7, 7)
        inv(8)
        V.tensor_tensor(std[:, :], rs[:, :], rs[:, :], ALU.mult).then_inc(*did(dve_steps))
        dve.wait_ge(*did.last)
        dve.wait_ge(*when(("sums", 9)))
        V.tensor_tensor(std[:, :], std[:, :], bank[sums_bank(9)][:, 0:T], ALU.mult).then_inc(*did(dve_steps, "mean_f"))
        for m in (0, 1):
            dve.wait_ge(*when(("x_gain", m)))
            V.tensor_tensor(X[:, 2 * m:2 * m + 2, :], X[:, 2 * m:2 * m + 2, :], rep(rs[:, :], 2), ALU.mult).then_inc(*did(dve_steps, ("x", 9, m)))

        for l in range(2):
            nu, v, s = 10 + 2 * l, 9 + l, 9 + 2 * l
            V.scalar_tensor_tensor(gpre[:, :], mods[:, l, 8:16], 1.0, col1[:, 48 + 8 * l:56 + 8 * l], ALU.add, ALU.mult).then_inc(*did(dve_steps))
            V.tensor_tensor(gpost[:, :], mods[:, l, 16:24], col1[:, 64 + 8 * l:72 + 8 * l], ALU.mult).then_inc(*did(dve_steps))
            if l == 0:
                dve.wait_ge(*when(("x", 9, 3)))
            inv(s)
            dve.wait_ge(*when(("sums", s)))
            def scaled(k):
                V.scalar_tensor_tensor(sq[:, k, :], X[:, k, :], gpre[:, k:k + 1], rs[:, :], ALU.mult, ALU.mult).then_inc(*did(dve_steps, ("xn", l, k)))

            scaled(0)
            scaled(1)
            for k in range(KD):
                if k + 2 < KD:
                    scaled(k + 2)
                dve.wait_ge(*when(("xh", nu, k)))
                V.scalar_tensor_tensor(xl[:, k, :], sq[:, k, :], mods[:, l, k:k + 1], f32(xh[:, k, :]), ALU.add, ALU.subtract).then_inc(*did(dve_steps, ("xl", nu, k)))
            if l:
                lo(first["win1"] + 1)
                lo(first["win1"] + 2)
            dve.wait_ge(*did.last)
            dve.wait_ge(*when(("zeros", l)))
            def slope(h):
                return float(2.0 ** (-8.0 * (h + 1) / HEADS_C))
            for h in range(HEADS_C):
                V.scalar_tensor_tensor(bias[:, h, :], const[:, C_DIST:C_DIST + T], -slope(h), const[:, C_DMASK:C_DMASK + T], ALU.mult, ALU.add).then_inc(*did(dve_steps))
                V.scalar_tensor_tensor(cbias[:, h, :, :].rearrange("p a n -> p (a n)"), const[:, C_CMPD:C_CMPD + 2 * CMP_T], -slope(h),
                                       const[:, C_CMPM:C_CMPM + 2 * CMP_T], ALU.mult, ALU.add).then_inc(*did(dve_steps))
            c0 = first[f"win{l}"]

            def zero_padded(dst, src, key):
                for h in range(2):
                    rows_ = slice(h * DH, (h + 1) * DH)
                    V.tensor_copy(dst[rows_, :, h, :], src[rows_, :, :]).then_inc(*did(dve_steps, key))

            for n, (name, j) in enumerate(WIN):
                if n + AHEAD < 16:
                    lo(c0 + n + AHEAD)
                b = n % 8
                key, done = ("win", l, n), ("proj", l, n)
                src = two(bank[b][:, :])
                if name in ("qm", "qn"):
                    dve.wait_ge(*when(key))
                    q = qm if name == "qm" else qs
                    V.tensor_scalar(q[:, 2 * j:2 * j + 2, :], src, float(DH ** -0.5), None, ALU.mult).then_inc(*did(dve_steps, done))
                elif name == "km":
                    dve.wait_ge(*when(key))
                    zero_padded(kmz[:, 2 * j:2 * j + 2, :, :], src, done)
                elif name == "vm":
                    dve.wait_ge(*when(key))
                    for t in range(TB):
                        for h in range(2):
                            V.tensor_copy(vmz[:, t, 4 * j + h:4 * j + 4:2, h * DH:(h + 1) * DH],
                                          src[:, t, :].rearrange("p (m h d) -> p m h d", h=2, d=DH)[:, :, h, :]).then_inc(*did(dve_steps, done))
                elif name == "kcvc":
                    dve.wait_ge(*when(key))
                    V.tensor_copy(kA[:, 0:2, :], src).then_inc(*did(dve_steps, ("kA", l, 0)))
                    at[done] = at[("kA", l, 0)]
                elif name == "kskw":
                    dve.wait_ge(*when(key))
                    V.tensor_copy(kA[:, 2:4, :], src).then_inc(*did(dve_steps, ("kA", l, 1)))
                    at[done] = at[("kA", l, 1)]
                elif name == "vsvw":
                    dve.wait_ge(*when(key))
                    for which, vz in enumerate((vsz, vwz)):
                        for h in range(2):
                            V.tensor_copy(vz[:, :, :, h, h * DH:(h + 1) * DH],
                                          src[:, :, which * P:(which + 1) * P].rearrange("p t (g d) -> p t g d", g=GROUPS)).then_inc(*did(dve_steps, done))
                if name == "vsvw":
                    dve.wait_ge(*when(("kB", l, 0)))
                    kB = two(bank[0][:, :])
                    for g, low, high in ((0, kA[:, 0:2, :], kB), (1, kB, kA[:, 0:2, :])):
                        V.tensor_copy(kc2[0:DH, :, g, :], low[0:DH, :, :]).then_inc(*did(dve_steps))
                        V.tensor_copy(kc2[DH:P, :, g, 0:T - 1], high[DH:P, :, 1:T]).then_inc(*did(dve_steps, ("kB_used", l, 0)))
                    dve.wait_ge(*did.last)
                    for kv in range(2):
                        pe_col = col2[:, 32 * kv + 16 * l:32 * kv + 16 * l + 16]
                        for g in range(GROUPS):
                            for a in range(2):
                                toks = kc2[:, kv, g, 16 * a:16 * a + 240].rearrange("p (t r two) -> p t r two", r=8, two=2)[:, :, :, 0]
                                dst = win[:, kv, 8 * a:8 * a + 8, CMP_T * g:CMP_T * (g + 1)].rearrange("p r t -> p t r")
                                V.tensor_tensor(dst, toks, rep(pe_col[:, 8 * a:8 * a + 8], CMP_T), ALU.add).then_inc(*did(dve_steps, ("windows", l, kv)))
            dve.wait_ge(*when(("kB", l, 1)))
            for which, kz in ((0, ksz), (1, kwz)):
                here, there = kA[:, 2 + which, :], bank[1][:, which * T:(which + 1) * T]
                for g in range(GROUPS):
                    for h in range(2):
                        rows_ = slice(h * DH, (h + 1) * DH)
                        V.tensor_copy(kz[rows_, g, h, :], (here if g == h else there)[rows_, :]).then_inc(*did(dve_steps, ("kB_used", l, 1)))
            dve.wait_ge(*when(("kcmp", l)))
            for h in range(2):
                rows_ = slice(h * DH, (h + 1) * DH)
                V.tensor_copy(kcz[rows_, :, h, 0:CMP_T], bank[1][rows_, 0:30].rearrange("p (g t) -> p g t", g=GROUPS)).then_inc(*did(dve_steps, ("kcz", l)))
            dve.wait_ge(*when(("vcmp", l)))
            for h in range(2):
                V.tensor_copy(vcz[0:CMP_T, :, h, h * DH:(h + 1) * DH], bank[2][0:CMP_T, 0:P].rearrange("p (g d) -> p g d", g=GROUPS)).then_inc(*did(dve_steps, ("vcz", l)))
            nc.vector.memset(small[:, 48:49], 0.0).then_inc(*did(dve_steps, ("attn", l)))

            def maxima_c(i):
                kind, m, _, _ = ITEMS[i]
                s_, nm = sC[:, i % 3], nmC[:, i % 3]
                b0 = 2 * (i % 2)
                item = ("c", l, i)
                if kind != "cmp":
                    return maxima(item, b0, nm)
                if i >= 3:
                    dve.wait_ge(*when(("pt", ("c", l, i - 3))))
                V.memset(s_[:, :, 0:32], 0.0).then_inc(*did(dve_steps))
                dve.wait_ge(*when(("s", item, 1)))
                for t in range(TB):
                    V.tensor_reduce(nm[:, 2 * t:2 * t + 2], two(bank[b0][:, 30 * t:30 * t + 30]), AX.X, ALU.max, negate=True).then_inc(*did(dve_steps, ("max", item)))

            def weigh_c(i):
                kind, m, _, _ = ITEMS[i]
                gate = None
                if kind != "moba":
                    branch = {"cmp": 0, "slc": 1, "win": 2}[kind]
                    gate = gates[:, :, :].rearrange("p t (h b) -> p t h b", b=3)[:, :, 2 * m:2 * m + 2, branch]
                weigh(("c", l, i), sC[:, i % 3], denC[:, i % 3], rdC[:, i % 3], gate, kind == "cmp", CMP_T if kind == "cmp" else None)

            def gated(i):
                kind, m, _, stop = ITEMS[i]
                if stop:
                    k = m if kind == "moba" else 4 + m
                    z = (zm if kind == "moba" else zn)[:, m, :]
                    dve.wait_ge(*when(("oc", l, i)))
                    dve.wait_ge(*did.last)
                    V.tensor_tensor(yC[:, k % 2, :], bank[6 + k % 2][:, 0:T], z, ALU.mult).then_inc(*did(dve_steps, ("y", l, k)))

            def gated_lo(i):
                kind, m, _, stop = ITEMS[i]
                if stop:
                    k = m if kind == "moba" else 4 + m
                    dve.wait_ge(*when(("yh", l, k)))
                    V.tensor_tensor(xl[:, k, :], yC[:, k % 2, :], f32(xh[:, k, :]), ALU.subtract).then_inc(*did(dve_steps, ("yl", l, k)))

            dve.wait_ge(*when(("gates", l)))
            maxima_c(0)
            maxima_c(1)
            for i in range(len(ITEMS)):
                weigh_c(i)
                if i >= 2:
                    gated(i - 2)
                if i + 2 < len(ITEMS):
                    maxima_c(i + 2)
                if i >= 3:
                    gated_lo(i - 3)
                if FIRST_HALF <= i < FIRST_HALF + 8:
                    lo(first[f"wout{l}"] + (i - FIRST_HALF) // 2, None, [(i - FIRST_HALF) % 2])
            gated(len(ITEMS) - 2)
            gated(len(ITEMS) - 1)
            for i in range(len(ITEMS) - 3, len(ITEMS)):
                gated_lo(i)
            for j in range(4):
                dve.wait_ge(*when(("sq", s + 1, j)))
                for k in (2 * j, 2 * j + 1):
                    V.tensor_scalar(y2[:, k, :], bank[j][:, k % 2 * T:(k % 2 + 1) * T], gpost[:, k:k + 1], None, ALU.mult).then_inc(*did(dve_steps, ("y2", l, j)))
            inv(s + 1)
            for j in range(4):
                pair_ = slice(2 * j, 2 * j + 2)
                if j < 2:
                    V.tensor_tensor(y2[:, pair_, :], y2[:, pair_, :], rep(rs[:, :], 2), ALU.mult).then_inc(*did(dve_steps))
                    dve.wait_ge(*did.last)
                else:
                    dve.wait_ge(*when(("y2_scaled", l, j)))
                V.tensor_tensor(X[:, pair_, :], X[:, pair_, :], y2[:, pair_, :], ALU.add).then_inc(*did(dve_steps, ("x", 10 + l, j)))
            lo(first[f"wout{l}"] + 4)

    block_ctx.__exit__(None, None, None)
    return at


_INS = ['x', 'p', 'positions', 'ffn_w_in', 'ffn_w_out', 'ple_w_gate', 'ple_w_in', 'a_w_in', 'a_w_out', 'kv_w_down', 'kv_w_up',
        'b_w_dq', 'b_w_uq', 'b_w_out', 'w_ada_2', 'w_in_2', 'w_out_2', 'w_ck1_2', 'w_ck2_2', 'w_cv1_2', 'w_cv2_2']
_ROWS = {'rows0': ['norm_gains', 'a_lb_logits', 'a_out_gain', 'kv_norm_in', 'kv_latent_norm', 'b_q_norm', 'final_norm'],
         'rows1': ['b_ada_2', 'g_pre_2', 'g_post_2', 'c_2'], 'rows2': ['pe_k_2', 'pe_v_2']}


def lay_out(inputs):
    arrays = {f"in_{name}": np.ascontiguousarray(inputs[name]) for name in _INS}
    for rows, members in _ROWS.items():
        arrays[f"in_{rows}"] = np.concatenate([np.reshape(inputs[name], (-1, P)) for name in members])
    arrays["in_consts"] = shape_constants()
    return arrays


def kernel(**inputs):
    import concourse.bacc as _bacc
    from concourse import mybir as _mybir
    from concourse.bass_utils import run_bass_kernel_spmd as _run

    arrays = lay_out(inputs)

    def program(known):
        nc = _bacc.Bacc("TRN2", target_bir_lowering=False, num_devices=1)
        io = {n[3:]: nc.dram_tensor(n, a.shape, _mybir.dt.from_np(a.dtype), kind="ExternalInput").ap() for n, a in arrays.items()}
        io["out"] = nc.dram_tensor("out_0", (1, T, D), _mybir.dt.float32, kind="ExternalOutput").ap()
        return nc, build(nc, io, known)

    _, counts = program({})
    nc, _ = program(counts)
    r = _run(nc, [arrays], core_ids=[0])
    return r.results[0]["out_0"]
```
